# Optimizing a Trainium2 kernel written in Bass

```python
import math
import jax, jax.numpy as jnp
from jax import lax
import numpy as np
import jax
import jax.numpy as jnp

D_MODEL = 1024
BATCH = 1
SEQ = 256
DEPTH = 1

HEAD_DIM = 64
FOX_HEADS = D_MODEL // 2 // HEAD_DIM
RWKV_HEADS = D_MODEL // 2 // HEAD_DIM
FOX_WIDTH = FOX_HEADS * HEAD_DIM
RWKV_WIDTH = RWKV_HEADS * HEAD_DIM
D_MIX = FOX_WIDTH + RWKV_WIDTH
Q_BLOCK = 128
RMS_EPS = 1e-6
LNX_EPS = 64e-5
DECAY_LORA = max(32, int(round(1.8 * D_MODEL ** 0.5 / 32)) * 32)
ICLR_LORA = max(32, int(round(1.8 * D_MODEL ** 0.5 / 32)) * 32)
GATE_LORA = max(32, int(round(0.6 * D_MODEL ** 0.8 / 32)) * 32)
FOX_SPLITS = [FOX_WIDTH, FOX_WIDTH, FOX_WIDTH, FOX_WIDTH, FOX_HEADS, FOX_HEADS, FOX_HEADS]
RWKV_SPLITS = [RWKV_WIDTH, RWKV_WIDTH, RWKV_WIDTH, DECAY_LORA, ICLR_LORA, GATE_LORA]
FOX_COLS = sum(FOX_SPLITS)
RWKV_COLS = sum(RWKV_SPLITS)
D_IN_PROJ = FOX_COLS + RWKV_COLS
FORGET_BIAS_MEAN = 3.0
N_EXPERTS = 64
N_GROUPS = 8
TOPK_GROUPS = 4
TOP_K = 6
D_EXPERT = 256
D_SHARED = 256
ROUTED_SCALE = 2.5
EXPERT_BLOCK = 256


def rms_norm(x, gain, eps=RMS_EPS):
    xf = x.astype(jnp.float32)
    y = xf * lax.rsqrt(jnp.mean(xf * xf, axis=-1, keepdims=True) + eps)
    return (y * gain.astype(jnp.float32)).astype(x.dtype)

def shift_prev(z):
    pad = [(0, 0), (1, 0)] + [(0, 0)] * (z.ndim - 2)
    return jnp.pad(z, pad)[:, :-1]

def split_cols(z, sizes):
    cuts = [int(s) for s in np.cumsum(sizes)[:-1]]
    return jnp.split(z, cuts, axis=-1)

def swiglu(x, wg, wu, wd):
    return (jax.nn.silu(x @ wg) * (x @ wu)) @ wd

def fox_attention(q, k, v, cum):
    B, T, H, D = q.shape
    nb = T // Q_BLOCK
    scale = D ** -0.5
    qb = q.reshape(B, nb, Q_BLOCK, H, D).transpose(1, 0, 3, 2, 4)
    cb = cum.reshape(B, nb, Q_BLOCK, H).transpose(1, 0, 3, 2)
    kh = k.transpose(0, 2, 1, 3)
    vh = v.transpose(0, 2, 1, 3)
    ck = cum.transpose(0, 2, 1)
    key_pos = jnp.arange(T)

    def block(args):
        q_blk, c_blk, i = args
        s = jnp.einsum('bhqd,bhkd->bhqk', q_blk, kh).astype(jnp.float32) * scale
        s = s + (c_blk[..., :, None] - ck[:, :, None, :])
        q_pos = i * Q_BLOCK + jnp.arange(Q_BLOCK)
        s = jnp.where(key_pos[None, :] <= q_pos[:, None], s, -jnp.inf)
        p = jax.nn.softmax(s, axis=-1)
        return jnp.einsum('bhqk,bhkd->bhqd', p.astype(vh.dtype), vh)

    o = lax.map(block, (qb, cb, jnp.arange(nb)))
    return o.transpose(1, 0, 3, 2, 4).reshape(B, T, H, D)

def fox_mixer(zf, qn_g, kn_g, on_g, forget_b):
    B, T, _ = zf.shape
    q, k, v, g, f_logit, a_k, a_v = split_cols(zf, FOX_SPLITS)
    heads = lambda t: t.reshape(B, T, FOX_HEADS, HEAD_DIM)
    q, k, v = heads(q), heads(k), heads(v)
    a_k = jax.nn.sigmoid(a_k)[..., None]
    a_v = jax.nn.sigmoid(a_v)[..., None]
    k = a_k * shift_prev(k) + (1 - a_k) * k
    v = a_v * shift_prev(v) + (1 - a_v) * v
    q = rms_norm(q, qn_g)
    k = rms_norm(k, kn_g)
    log_f = jax.nn.log_sigmoid((f_logit + forget_b).astype(jnp.float32))
    cum = jnp.cumsum(log_f, axis=1)
    o = fox_attention(q, k, v, cum)
    o = rms_norm(o, on_g) * jax.nn.sigmoid(heads(g))
    return o.reshape(B, T, FOX_WIDTH)

def wkv7_scan(r, w, k, v, a, b):
    B, T, H, N = r.shape

    def step(S, inp):
        r_t, w_t, k_t, v_t, a_t, b_t = inp
        Sa = jnp.einsum('bhij,bhj->bhi', S, a_t)
        S = S * w_t[:, :, None, :] + Sa[..., None] * b_t[:, :, None, :] + v_t[..., None] * k_t[:, :, None, :]
        return S, jnp.einsum('bhij,bhj->bhi', S, r_t)

    xs = tuple(t.transpose(1, 0, 2, 3) for t in (r, w, k, v, a, b))
    S0 = jnp.zeros((B, H, N, N), jnp.float32)
    _, ys = lax.scan(step, S0, xs)
    return ys.transpose(1, 0, 2, 3)

def rwkv7_mixer(zr, mu, w0, decay_up, a0, iclr_up, gate_up, k_k, k_a, r_k, lnx_g, lnx_b):
    B, T, _ = zr.shape
    f32 = jnp.float32
    zr = zr + mu * (shift_prev(zr) - zr)
    r, k, v, wd, ad, gd = split_cols(zr, RWKV_SPLITS)
    w_log = -jax.nn.softplus(-(w0 + jnp.tanh(wd) @ decay_up).astype(f32)) - 0.5
    decay = jnp.exp(-jnp.exp(w_log))
    a = jax.nn.sigmoid((a0 + ad @ iclr_up).astype(f32))
    g = jax.nn.sigmoid(gd) @ gate_up
    heads = lambda t: t.astype(f32).reshape(B, T, RWKV_HEADS, HEAD_DIM)
    kk = heads(k * k_k)
    kk = kk / jnp.maximum(jnp.sqrt(jnp.sum(kk * kk, axis=-1, keepdims=True)), 1e-12)
    k = k.astype(f32) * (1 + (a - 1) * k_a.astype(f32))
    rh, kh, vh, ah, wh = heads(r), heads(k), heads(v), heads(a), heads(decay)
    o = wkv7_scan(rh, wh, kh, vh, -kk, kk * ah)
    mean = jnp.mean(o, axis=-1, keepdims=True)
    var = jnp.mean(jnp.square(o - mean), axis=-1, keepdims=True)
    o = (o - mean) * lax.rsqrt(var + LNX_EPS)
    o = o * lnx_g.astype(f32).reshape(RWKV_HEADS, HEAD_DIM) + lnx_b.astype(f32).reshape(RWKV_HEADS, HEAD_DIM)
    o = o + jnp.sum(rh * kh * r_k.astype(f32), axis=-1, keepdims=True) * vh
    return (o.reshape(B, T, RWKV_WIDTH) * g.astype(f32)).astype(zr.dtype)

def routed_experts(h, idx, wts, w_gate, w_up, w_down):
    n_tok, d = h.shape
    n_assign = n_tok * TOP_K
    flat_e = idx.reshape(-1).astype(jnp.int32)
    order = jnp.argsort(flat_e)
    sorted_e = flat_e[order]
    counts = jnp.bincount(flat_e, length=N_EXPERTS).astype(jnp.int32)
    padded = (counts + EXPERT_BLOCK - 1) // EXPERT_BLOCK * EXPERT_BLOCK
    pad_end = jnp.cumsum(padded)
    pad_start = pad_end - padded
    grp_start = jnp.cumsum(counts) - counts
    dest = pad_start[sorted_e] + jnp.arange(n_assign, dtype=jnp.int32) - grp_start[sorted_e]
    n_blocks = -(-n_assign // EXPERT_BLOCK) + N_EXPERTS
    n_rows = n_blocks * EXPERT_BLOCK
    row_tok = jnp.zeros((n_rows,), jnp.int32).at[dest].set((order // TOP_K).astype(jnp.int32))
    row_w = jnp.zeros((n_rows,), wts.dtype).at[dest].set(wts.reshape(-1)[order])
    blk_start = jnp.arange(n_blocks, dtype=pad_end.dtype) * EXPERT_BLOCK
    blk_e = jnp.minimum(jnp.searchsorted(pad_end, blk_start, side='right'), N_EXPERTS - 1)

    def block(args):
        tok, w, e = args
        y = swiglu(h[tok], w_gate[e], w_up[e], w_down[e])
        return y * w[:, None]

    ys = lax.map(block, (row_tok.reshape(n_blocks, EXPERT_BLOCK), row_w.reshape(n_blocks, EXPERT_BLOCK), blk_e))
    return jax.ops.segment_sum(ys.reshape(n_rows, d), row_tok, num_segments=n_tok)

def moe_ffn(h, router_w, router_bias, w_gate, w_up, w_down, sw_gate, sw_up, sw_down):
    B, T, D = h.shape
    hf = h.reshape(B * T, D)
    n = hf.shape[0]
    scores = jax.nn.sigmoid((hf @ router_w).astype(jnp.float32))
    sel = scores + router_bias.astype(jnp.float32)
    grp = sel.reshape(n, N_GROUPS, N_EXPERTS // N_GROUPS)
    grp_score = jnp.sum(lax.top_k(grp, 2)[0], axis=-1)
    _, top_g = lax.top_k(grp_score, TOPK_GROUPS)
    gmask = jnp.any(top_g[..., None] == jnp.arange(N_GROUPS), axis=-2)
    emask = jnp.repeat(gmask, N_EXPERTS // N_GROUPS, axis=-1)
    _, idx = lax.top_k(jnp.where(emask, sel, -jnp.inf), TOP_K)
    wts = jnp.take_along_axis(scores, idx, axis=-1)
    wts = wts / jnp.sum(wts, axis=-1, keepdims=True) * ROUTED_SCALE
    routed = routed_experts(hf, idx, wts.astype(h.dtype), w_gate, w_up, w_down)
    shared = swiglu(hf, sw_gate, sw_up, sw_down)
    return (routed + shared).reshape(B, T, D)

def first_inputs(seed: int = 0) -> dict:
    key = jax.random.key(seed)
    ks = iter(jax.random.split(key, 40))
    nrm = lambda shape, s: jax.random.normal(next(ks), shape, jnp.float32) * s
    gain = lambda shape: 1.0 + nrm(shape, 0.02)
    L, D = DEPTH, D_MODEL
    return {
        "x": nrm((BATCH, SEQ, D), 1.0),
        "c": nrm((BATCH, D), 1.0),
        "norm1_g": gain((L, D)),
        "norm2_g": gain((L, D)),
        "ada_w": nrm((L, D, 6 * D), 0.5 * D ** -0.5),
        "ada_b": nrm((L, 6 * D), 0.02),
        "w_in": nrm((L, D, D_IN_PROJ), D ** -0.5),
        "w_out": nrm((L, D_MIX, D), D_MIX ** -0.5),
        "fox_qn_g": gain((L, FOX_HEADS, HEAD_DIM)),
        "fox_kn_g": gain((L, FOX_HEADS, HEAD_DIM)),
        "fox_on_g": gain((L, FOX_HEADS, HEAD_DIM)),
        "fox_forget_b": FORGET_BIAS_MEAN + nrm((L, FOX_HEADS), 0.5),
        "rw_mu": jax.random.uniform(next(ks), (L, RWKV_COLS), jnp.float32),
        "rw_w0": jax.random.uniform(next(ks), (L, RWKV_WIDTH), jnp.float32, -6.0, -1.0),
        "rw_decay_up": nrm((L, DECAY_LORA, RWKV_WIDTH), 0.1 * DECAY_LORA ** -0.5),
        "rw_a0": nrm((L, RWKV_WIDTH), 0.1),
        "rw_iclr_up": nrm((L, ICLR_LORA, RWKV_WIDTH), 0.1 * ICLR_LORA ** -0.5),
        "rw_gate_up": nrm((L, GATE_LORA, RWKV_WIDTH), GATE_LORA ** -0.5),
        "rw_k_k": 0.85 + nrm((L, RWKV_WIDTH), 0.05),
        "rw_k_a": 1.0 + nrm((L, RWKV_WIDTH), 0.05),
        "rw_r_k": nrm((L, RWKV_HEADS, HEAD_DIM), 0.1),
        "rw_lnx_g": gain((L, RWKV_WIDTH)),
        "rw_lnx_b": nrm((L, RWKV_WIDTH), 0.02),
        "router_w": nrm((L, D, N_EXPERTS), D ** -0.5),
        "router_bias": nrm((L, N_EXPERTS), 0.01),
        "exp_w_gate": nrm((L, N_EXPERTS, D, D_EXPERT), D ** -0.5),
        "exp_w_up": nrm((L, N_EXPERTS, D, D_EXPERT), D ** -0.5),
        "exp_w_down": nrm((L, N_EXPERTS, D_EXPERT, D), D_EXPERT ** -0.5),
        "sh_w_gate": nrm((L, D, D_SHARED), D ** -0.5),
        "sh_w_up": nrm((L, D, D_SHARED), D ** -0.5),
        "sh_w_down": nrm((L, D_SHARED, D), D_SHARED ** -0.5),
        "final_g": gain((D,)),
    }

def first_block(x, c, norm1_g, norm2_g, ada_w, ada_b, w_in, w_out,
              fox_qn_g, fox_kn_g, fox_on_g, fox_forget_b,
              rw_mu, rw_w0, rw_decay_up, rw_a0, rw_iclr_up, rw_gate_up, rw_k_k, rw_k_a, rw_r_k, rw_lnx_g, rw_lnx_b,
              router_w, router_bias, exp_w_gate, exp_w_up, exp_w_down, sh_w_gate, sh_w_up, sh_w_down, final_g):
    for l in range(DEPTH):
        mod = jax.nn.silu(c) @ ada_w[l] + ada_b[l]
        sh1, sc1, g1, sh2, sc2, g2 = jnp.split(mod[:, None, :], 6, axis=-1)
        h = rms_norm(x, norm1_g[l]) * (1 + sc1) + sh1
        z = h @ w_in[l]
        y_fox = fox_mixer(z[..., :FOX_COLS], fox_qn_g[l], fox_kn_g[l], fox_on_g[l], fox_forget_b[l])
        y_rwkv = rwkv7_mixer(z[..., FOX_COLS:], rw_mu[l], rw_w0[l], rw_decay_up[l], rw_a0[l], rw_iclr_up[l],
                             rw_gate_up[l], rw_k_k[l], rw_k_a[l], rw_r_k[l], rw_lnx_g[l], rw_lnx_b[l])
        x = x + g1 * (jnp.concatenate([y_fox, y_rwkv], axis=-1) @ w_out[l])
        h = rms_norm(x, norm2_g[l]) * (1 + sc2) + sh2
        x = x + g2 * moe_ffn(h, router_w[l], router_bias[l], exp_w_gate[l], exp_w_up[l], exp_w_down[l],
                             sh_w_gate[l], sh_w_up[l], sh_w_down[l])
    return rms_norm(x, final_g)


GROUP_HEADS = 4
GROUP_WIDTH = GROUP_HEADS * HEAD_DIM
N_GROUPS_2 = 4
D_MIX_2 = N_GROUPS_2 * GROUP_WIDTH
IN_SIZES = (GROUP_WIDTH, GROUP_WIDTH, GROUP_WIDTH, GROUP_WIDTH, GROUP_HEADS, GROUP_HEADS, GROUP_WIDTH, GROUP_WIDTH, GROUP_WIDTH, GROUP_WIDTH, GROUP_WIDTH, GROUP_WIDTH, GROUP_WIDTH, GROUP_WIDTH, GROUP_WIDTH, GROUP_WIDTH)
N_IN = sum(IN_SIZES)
MLSTM_F_OFFSET = 4 * GROUP_WIDTH + GROUP_HEADS
MLSTM_CHUNK = 64
HGRN_CHUNK = 64
SCONV_WIDTH = 3
MOBA_BLOCK = 256
MOBA_TOPK = 3
MOBA_QCHUNK = 32
REL_BUCKETS = 32
REL_MAX_DIST = 128
N_MEM = 256
CROSS_HEADS = 4
CROSS_HEAD_DIM = 128
CROSS_WIDTH = CROSS_HEADS * CROSS_HEAD_DIM
D_FF = 2816
FFN_CONV_WIDTH = 3
NEG_BIG = -1e30


def rmsnorm(x, gain):
    x32 = x.astype(jnp.float32)
    y = x32 * lax.rsqrt(jnp.mean(x32 * x32, axis=-1, keepdims=True) + RMS_EPS)
    return (y * gain.astype(jnp.float32)).astype(x.dtype)

def head_rmsnorm(h, gain):
    b, nh, s, d = h.shape
    h32 = h.astype(jnp.float32).transpose(0, 2, 1, 3)
    h32 = h32 * lax.rsqrt(jnp.mean(h32 * h32, axis=-1, keepdims=True) + RMS_EPS)
    return h32.reshape(b, s, nh * d) * gain.astype(jnp.float32)

def causal_dwconv(x, w):
    width, ch = w.shape
    return lax.conv_general_dilated(x, w.astype(x.dtype)[:, None, :], window_strides=(1,), padding=[(width - 1, 0)], dimension_numbers=('NWC', 'WIO', 'NWC'), feature_group_count=ch)

def to_heads(a, n_heads):
    b, s, _ = a.shape
    return a.reshape(b, s, n_heads, -1).transpose(0, 2, 1, 3)

def _chunks(a, size):
    b, h, s = a.shape[:3]
    return jnp.moveaxis(a.reshape(b, h, s // size, size, *a.shape[3:]), 2, 0)

def _unchunk(a):
    nc, b, h, l, d = a.shape
    return jnp.moveaxis(a, 0, 2).reshape(b, h, nc * l, d)

def rel_bucket(dist):
    n = jnp.maximum(dist, 0)
    exact = REL_BUCKETS // 2
    nf = jnp.maximum(n, 1).astype(jnp.float32)
    large = exact + (jnp.log(nf / exact) / math.log(REL_MAX_DIST / exact) * (REL_BUCKETS - exact)).astype(jnp.int32)
    large = jnp.minimum(large, REL_BUCKETS - 1)
    return jnp.where(n < exact, n, large)

def mlstm_chunkwise(q, k, v, i_pre, f_pre):
    b, nh, s, d = q.shape
    f32 = jnp.float32
    q = q.astype(f32)
    k = k.astype(f32) * (d ** -0.5)
    v = v.astype(f32)
    log_i = i_pre.astype(f32)
    log_f = jax.nn.log_sigmoid(f_pre.astype(f32))
    causal = jnp.tril(jnp.ones((MLSTM_CHUNK, MLSTM_CHUNK), dtype=bool))

    def step(carry, xs):
        c_mat, n_vec, m_prev = carry
        qc, kc, vc, lic, lfc = xs
        g = jnp.cumsum(lfc, axis=-1)
        dlog = jnp.where(causal, g[..., :, None] - g[..., None, :] + lic[..., None, :], NEG_BIG)
        a = g + m_prev[..., None]
        m_t = jnp.maximum(a, jnp.max(dlog, axis=-1))
        w = jnp.exp(dlog - m_t[..., None]) * jnp.einsum('bhtd,bhsd->bhts', qc, kc)
        inter = jnp.exp(a - m_t)
        num = jnp.einsum('bhts,bhsd->bhtd', w, vc) + inter[..., None] * jnp.einsum('bhvk,bhtk->bhtv', c_mat, qc)
        den = jnp.sum(w, axis=-1) + inter * jnp.einsum('bhk,bhtk->bht', n_vec, qc)
        h = num / jnp.maximum(jnp.abs(den), jnp.exp(-m_t))[..., None]
        g_last = g[..., -1]
        u = g_last[..., None] - g + lic
        m_new = jnp.maximum(g_last + m_prev, jnp.max(u, axis=-1))
        ws = jnp.exp(u - m_new[..., None])
        decay = jnp.exp(g_last + m_prev - m_new)
        c_new = decay[..., None, None] * c_mat + jnp.einsum('bhs,bhsv,bhsk->bhvk', ws, vc, kc)
        n_new = decay[..., None] * n_vec + jnp.einsum('bhs,bhsk->bhk', ws, kc)
        return (c_new, n_new, m_new), h

    init = (jnp.zeros((b, nh, d, d), f32), jnp.zeros((b, nh, d), f32), jnp.zeros((b, nh), f32))
    _, hs = lax.scan(step, init, tuple(_chunks(a, MLSTM_CHUNK) for a in (q, k, v, log_i, log_f)))
    return _unchunk(hs)

def hgrn2_chunkwise(q, k, log_f, v):
    b, nh, s, dk = q.shape
    dv = v.shape[-1]
    causal = jnp.tril(jnp.ones((HGRN_CHUNK, HGRN_CHUNK), dtype=bool))[:, :, None]

    def step(state, xs):
        qc, kc, lfc, vc = xs
        g = jnp.cumsum(lfc, axis=2)
        rel = jnp.exp(jnp.where(causal, g[:, :, :, None, :] - g[:, :, None, :, :], NEG_BIG))
        attn = jnp.einsum('bhtk,bhtsk,bhsk->bhts', qc, rel, kc)
        out = jnp.einsum('bhts,bhsv->bhtv', attn, vc) + jnp.einsum('bhtk,bhkv->bhtv', qc * jnp.exp(g), state)
        g_last = g[:, :, -1:, :]
        new_state = jnp.exp(g_last[:, :, 0, :])[..., None] * state + jnp.einsum('bhsk,bhsv->bhkv', kc * jnp.exp(g_last - g), vc)
        return new_state, out

    init = jnp.zeros((b, nh, dk, dv), jnp.float32)
    _, outs = lax.scan(step, init, tuple(_chunks(a, HGRN_CHUNK) for a in (q, k, log_f, v)))
    return _unchunk(outs)

def moba_attention(q, k, v, rel_bias):
    b, nh, s, d = q.shape
    f32 = jnp.float32
    nb = -(-s // MOBA_BLOCK)
    s_pad = nb * MOBA_BLOCK
    padw = ((0, 0), (0, 0), (0, s_pad - s), (0, 0))
    q, k, v = jnp.pad(q, padw), jnp.pad(k, padw), jnp.pad(v, padw)
    kb = k.reshape(b, nh, nb, MOBA_BLOCK, d)
    vb = v.reshape(b, nh, nb, MOBA_BLOCK, d)
    n_sel = min(MOBA_TOPK, nb - 1)
    scale = d ** -0.5
    bias_t = rel_bias.astype(f32).T
    blk_of = jnp.arange(s_pad, dtype=jnp.int32) // MOBA_BLOCK
    if n_sel > 0:
        kmean = jnp.mean(kb.astype(f32), axis=3)
        gate = jnp.einsum('bhsd,bhnd->bhsn', q.astype(f32), kmean)
        past = jnp.arange(nb, dtype=jnp.int32)[None, :] < blk_of[:, None]
        gate = jnp.where(past, gate, NEG_BIG)
        _, sel = lax.top_k(gate, n_sel)
        sel = sel.astype(jnp.int32)
        sel_valid = sel < blk_of[:, None]
    b_ix = jnp.arange(b)[:, None, None, None]
    h_ix = jnp.arange(nh)[None, :, None, None]
    key_off = jnp.arange(MOBA_BLOCK, dtype=jnp.int32)

    def attend_chunk(c):
        start = c * MOBA_QCHUNK
        qc = lax.dynamic_slice_in_dim(q, start, MOBA_QCHUNK, axis=2)
        t = start + jnp.arange(MOBA_QCHUNK, dtype=jnp.int32)
        j = start // MOBA_BLOCK
        k_own = lax.dynamic_index_in_dim(kb, j, axis=2, keepdims=False)
        v_own = lax.dynamic_index_in_dim(vb, j, axis=2, keepdims=False)
        dist_own = t[:, None] - (j * MOBA_BLOCK + key_off)[None, :]
        s_own = jnp.einsum('bhqd,bhkd->bhqk', qc, k_own).astype(f32) * scale + bias_t[:, rel_bucket(dist_own)][None]
        s_own = jnp.where(dist_own >= 0, s_own, NEG_BIG)
        if n_sel == 0:
            p = jax.nn.softmax(s_own, axis=-1)
            out = jnp.einsum('bhqk,bhkd->bhqd', p, v_own.astype(f32))
        else:
            sel_c = lax.dynamic_slice_in_dim(sel, start, MOBA_QCHUNK, axis=2)
            valid_c = lax.dynamic_slice_in_dim(sel_valid, start, MOBA_QCHUNK, axis=2)
            k_sel = kb[b_ix, h_ix, sel_c]
            v_sel = vb[b_ix, h_ix, sel_c]
            dist = t[None, None, :, None, None] - (sel_c[..., None] * MOBA_BLOCK + key_off)
            bias = bias_t[h_ix[..., None], rel_bucket(dist)]
            s_past = jnp.einsum('bhqd,bhqnkd->bhqnk', qc, k_sel).astype(f32) * scale + bias
            s_past = jnp.where(valid_c[..., None], s_past, NEG_BIG)
            n_past = n_sel * MOBA_BLOCK
            p = jax.nn.softmax(jnp.concatenate([s_past.reshape(b, nh, MOBA_QCHUNK, n_past), s_own], axis=-1), axis=-1)
            p_past = p[..., :n_past].reshape(b, nh, MOBA_QCHUNK, n_sel, MOBA_BLOCK)
            out = jnp.einsum('bhqnk,bhqnkd->bhqd', p_past, v_sel.astype(f32)) + jnp.einsum('bhqk,bhkd->bhqd', p[..., n_past:], v_own.astype(f32))
        return out.astype(q.dtype)

    outs = lax.map(attend_chunk, jnp.arange(s_pad // MOBA_QCHUNK, dtype=jnp.int32))
    return _unchunk(outs)[:, :, :s]

def token_mixer(xn, w_in, b_in, mlstm_norm, sconv_w, rel_bias, hgrn_lb, hgrn_norm, w_out):
    b, s, _ = xn.shape
    f32 = jnp.float32
    dt = xn.dtype
    proj = xn @ w_in + b_in
    splits = np.cumsum(IN_SIZES)[:-1].tolist()
    (m_q, m_k, m_v, m_o, m_i, m_f, c_b, c_c, c_h, a_q, a_k, a_v, h_q, h_f, h_i, h_g) = jnp.split(proj, splits, axis=-1)
    h_m = mlstm_chunkwise(to_heads(m_q, GROUP_HEADS), to_heads(m_k, GROUP_HEADS), to_heads(m_v, GROUP_HEADS), m_i.transpose(0, 2, 1), m_f.transpose(0, 2, 1))
    y_m = head_rmsnorm(h_m, mlstm_norm) * jax.nn.sigmoid(m_o.astype(f32))
    y_c = c_b * causal_dwconv(c_c * c_h, sconv_w)
    y_a = moba_attention(to_heads(a_q, GROUP_HEADS), to_heads(a_k, GROUP_HEADS), to_heads(a_v, GROUP_HEADS), rel_bias)
    y_a = y_a.transpose(0, 2, 1, 3).reshape(b, s, GROUP_WIDTH)
    lb = hgrn_lb.astype(f32).reshape(1, GROUP_HEADS, 1, HEAD_DIM)
    z = to_heads(h_f, GROUP_HEADS).astype(f32)
    f_gate = lb + (1.0 - lb) * jax.nn.sigmoid(z)
    log_f = jnp.log(f_gate)
    k_h = 1.0 - f_gate
    q_h = jax.nn.silu(to_heads(h_q, GROUP_HEADS).astype(f32))
    o_h = hgrn2_chunkwise(q_h, k_h, log_f, to_heads(h_i, GROUP_HEADS).astype(f32))
    y_h = head_rmsnorm(o_h, hgrn_norm) * jax.nn.silu(h_g.astype(f32))
    y = jnp.concatenate([y_m.astype(dt), y_c.astype(dt), y_a.astype(dt), y_h.astype(dt)], axis=-1)
    return y @ w_out

def memory_cross_attention(xn, memn, wq, wk, wv, wo):
    b, s, _ = xn.shape
    m = memn.shape[1]
    q = (xn @ wq).reshape(b, s, CROSS_HEADS, CROSS_HEAD_DIM)
    k = (memn @ wk).reshape(b, m, CROSS_HEADS, CROSS_HEAD_DIM)
    v = (memn @ wv).reshape(b, m, CROSS_HEADS, CROSS_HEAD_DIM)
    logits = jnp.einsum('bshd,bmhd->bhsm', q, k).astype(jnp.float32) * (CROSS_HEAD_DIM ** -0.5)
    p = jax.nn.softmax(logits, axis=-1)
    o = jnp.einsum('bhsm,bmhd->bshd', p, v.astype(jnp.float32)).astype(xn.dtype).reshape(b, s, CROSS_WIDTH)
    return o @ wo

def conv_glu_ffn(xn, w_up, conv_w, conv_b, w_down):
    gu = xn @ w_up
    gate, up = jnp.split(gu, 2, axis=-1)
    gate = causal_dwconv(gate, conv_w) + conv_b.astype(gate.dtype)
    return (jax.nn.silu(gate) * up) @ w_down

def second_inputs(seed: int = 0) -> dict:
    key = jax.random.key(seed)
    ks = jax.random.split(key, 26)
    f32 = jnp.float32

    def nrm(k, shape, scale):
        return scale * jax.random.normal(k, shape, f32)

    def gain(k, shape):
        return 1.0 + 0.05 * jax.random.normal(k, shape, f32)

    b_in = nrm(ks[3], (DEPTH, N_IN), 0.01)
    b_in = b_in.at[:, MLSTM_F_OFFSET:MLSTM_F_OFFSET + GROUP_HEADS].add(jnp.linspace(3.0, 6.0, GROUP_HEADS))
    return {
        'x': nrm(ks[0], (BATCH, SEQ, D_MODEL), 1.0),
        'mem': nrm(ks[1], (BATCH, N_MEM, D_MODEL), 1.0),
        'w_in': nrm(ks[2], (DEPTH, D_MODEL, N_IN), D_MODEL ** -0.5),
        'b_in': b_in,
        'mlstm_norm': gain(ks[4], (DEPTH, GROUP_WIDTH)),
        'sconv_w': nrm(ks[5], (DEPTH, SCONV_WIDTH, GROUP_WIDTH), SCONV_WIDTH ** -0.5),
        'rel_bias': nrm(ks[6], (REL_BUCKETS, GROUP_HEADS), 0.5),
        'hgrn_lb_logits': nrm(ks[7], (DEPTH, GROUP_WIDTH), 0.5),
        'hgrn_norm': gain(ks[8], (DEPTH, GROUP_WIDTH)),
        'w_mix_out': nrm(ks[9], (DEPTH, D_MIX_2, D_MODEL), D_MIX_2 ** -0.5),
        'norm_mix_pre': gain(ks[10], (DEPTH, D_MODEL)),
        'norm_mix_post': gain(ks[11], (DEPTH, D_MODEL)),
        'mem_norm': gain(ks[12], (DEPTH, D_MODEL)),
        'w_cq': nrm(ks[13], (DEPTH, D_MODEL, CROSS_WIDTH), D_MODEL ** -0.5),
        'w_ck': nrm(ks[14], (DEPTH, D_MODEL, CROSS_WIDTH), D_MODEL ** -0.5),
        'w_cv': nrm(ks[15], (DEPTH, D_MODEL, CROSS_WIDTH), D_MODEL ** -0.5),
        'w_co': nrm(ks[16], (DEPTH, CROSS_WIDTH, D_MODEL), CROSS_WIDTH ** -0.5),
        'norm_cross_pre': gain(ks[17], (DEPTH, D_MODEL)),
        'norm_cross_post': gain(ks[18], (DEPTH, D_MODEL)),
        'w_ffn_in': nrm(ks[19], (DEPTH, D_MODEL, 2 * D_FF), D_MODEL ** -0.5),
        'ffn_conv_w': nrm(ks[20], (DEPTH, FFN_CONV_WIDTH, D_FF), FFN_CONV_WIDTH ** -0.5),
        'ffn_conv_b': nrm(ks[21], (DEPTH, D_FF), 0.01),
        'w_ffn_out': nrm(ks[22], (DEPTH, D_FF, D_MODEL), D_FF ** -0.5),
        'norm_ffn_pre': gain(ks[23], (DEPTH, D_MODEL)),
        'norm_ffn_post': gain(ks[24], (DEPTH, D_MODEL)),
    }

def second_block(x, mem, w_in, b_in, mlstm_norm, sconv_w, rel_bias, hgrn_lb_logits, hgrn_norm, w_mix_out, norm_mix_pre, norm_mix_post, mem_norm, w_cq, w_ck, w_cv, w_co, norm_cross_pre, norm_cross_post, w_ffn_in, ffn_conv_w, ffn_conv_b, w_ffn_out, norm_ffn_pre, norm_ffn_post):
    lb_soft = jax.nn.softmax(hgrn_lb_logits.astype(jnp.float32), axis=0)
    lb_all = jnp.cumsum(lb_soft, axis=0) - lb_soft[0]
    for l in range(DEPTH):
        h = token_mixer(rmsnorm(x, norm_mix_pre[l]), w_in[l], b_in[l], mlstm_norm[l], sconv_w[l], rel_bias, lb_all[l], hgrn_norm[l], w_mix_out[l])
        x = x + rmsnorm(h, norm_mix_post[l])
        h = memory_cross_attention(rmsnorm(x, norm_cross_pre[l]), rmsnorm(mem, mem_norm[l]), w_cq[l], w_ck[l], w_cv[l], w_co[l])
        x = x + rmsnorm(h, norm_cross_post[l])
        h = conv_glu_ffn(rmsnorm(x, norm_ffn_pre[l]), w_ffn_in[l], ffn_conv_w[l], ffn_conv_b[l], w_ffn_out[l])
        x = x + rmsnorm(h, norm_ffn_post[l])
    return x


def setup_inputs(seed=0):
    out = dict(first_inputs(seed))
    for name, value in second_inputs(seed + 1).items():
        if name != "x":
            out[name + "_2"] = value
    return out


def reference(
    x, c, norm1_g, norm2_g, ada_w, ada_b, w_in, w_out, fox_qn_g, fox_kn_g, fox_on_g,
    fox_forget_b, rw_mu, rw_w0, rw_decay_up, rw_a0, rw_iclr_up, rw_gate_up, rw_k_k, rw_k_a,
    rw_r_k, rw_lnx_g, rw_lnx_b, router_w, router_bias, exp_w_gate, exp_w_up, exp_w_down,
    sh_w_gate, sh_w_up, sh_w_down, final_g, mem_2, w_in_2, b_in_2, mlstm_norm_2, sconv_w_2,
    rel_bias_2, hgrn_lb_logits_2, hgrn_norm_2, w_mix_out_2, norm_mix_pre_2, norm_mix_post_2,
    mem_norm_2, w_cq_2, w_ck_2, w_cv_2, w_co_2, norm_cross_pre_2, norm_cross_post_2, w_ffn_in_2,
    ffn_conv_w_2, ffn_conv_b_2, w_ffn_out_2, norm_ffn_pre_2, norm_ffn_post_2,
):
    x = first_block(
        x, c, norm1_g, norm2_g, ada_w, ada_b, w_in, w_out, fox_qn_g, fox_kn_g, fox_on_g,
        fox_forget_b, rw_mu, rw_w0, rw_decay_up, rw_a0, rw_iclr_up, rw_gate_up, rw_k_k, rw_k_a,
        rw_r_k, rw_lnx_g, rw_lnx_b, router_w, router_bias, exp_w_gate, exp_w_up, exp_w_down,
        sh_w_gate, sh_w_up, sh_w_down, final_g,
    )
    return second_block(
        x, mem_2, w_in_2, b_in_2, mlstm_norm_2, sconv_w_2, rel_bias_2, hgrn_lb_logits_2,
        hgrn_norm_2, w_mix_out_2, norm_mix_pre_2, norm_mix_post_2, mem_norm_2, w_cq_2, w_ck_2,
        w_cv_2, w_co_2, norm_cross_pre_2, norm_cross_post_2, w_ffn_in_2, ffn_conv_w_2,
        ffn_conv_b_2, w_ffn_out_2, norm_ffn_pre_2, norm_ffn_post_2,
    )


_drawn_inputs = setup_inputs


def setup_inputs(seed=0):
    import zlib

    import numpy as np

    out = dict(_drawn_inputs(seed))
    spreads = {}
    factors = {'fox_qn_g': 3.002,
     'fox_kn_g': 3.23,
     'rw_decay_up': 12.095,
     'mlstm_norm_2': 3.22,
     'hgrn_norm_2': 3.206,
     'ffn_conv_b_2': 8.0,
     'fox_on_g': 3.223,
     'rw_lnx_g': 3.026,
     'rw_lnx_b': 5.112}
    for name, (base, spread) in spreads.items():
        noise = np.random.default_rng([zlib.crc32(name.encode()), seed]).standard_normal(out[name].shape)
        drawn = base * np.exp(spread * noise) if base else spread * noise
        out[name] = jnp.asarray(drawn.astype(out[name].dtype))
    for name, factor in factors.items():
        out[name] = (out[name] * factor).astype(out[name].dtype)
    return out
```

```python
import math
from contextlib import ExitStack

import concourse.bass as bass
import numpy as np
from concourse import mybir

F32 = mybir.dt.float32
I32 = mybir.dt.int32
ALU = mybir.AluOpType
ACT = mybir.ActivationFunctionType
AX = mybir.AxisListType

P = 128
T = 2
D = 1024
KT = D // P
BANK = 512
HD = 64
HEADS = 8
W1 = HEADS * HD
FOX_COLS = 4 * W1 + 3 * HEADS
DECAY_R, ICLR_R, GATE_R = 64, 64, 160
RW_COLS = 3 * W1 + DECAY_R + ICLR_R + GATE_R
EXPERTS, GROUPS, TOP_GROUPS, TOP_K = 64, 8, 4, 6
GROUP_SIZE = EXPERTS // GROUPS
D_E = 256
ROUTED_SCALE = 2.5
CS = 64
TH = [CS * i for i in range(T * P // CS)]
MAX_CHUNKS = (T * P * TOP_K + EXPERTS * (CS - 1)) // CS
MAX_QUADS = -(-MAX_CHUNKS // 4)
NC = 4 * MAX_QUADS + 4
UNMATCHED = 4096.0
GH = 4
GW = GH * HD
IN2 = 14 * GW + 2 * GH
(M_Q, M_K, M_V, M_O) = (i * GW for i in range(4))
M_I, M_F = 4 * GW, 4 * GW + GH
(C_B, C_C, C_H, A_Q, A_K, A_V, H_Q, H_F, H_I, H_G) = (4 * GW + 2 * GH + i * GW for i in range(10))
CH, CHD = 4, 128
CW = CH * CHD
BUCKETS, MAX_DIST = 32, 128
D_FF = 2816
FT_TILES = D_FF // P
FF_JOBS = D_FF // 256
TINY = 2.0 ** -64
RMS_EPS = 1e-6
LNX_EPS = 64e-5
MASKED = -1e30
LEVELS = 7



def shape_constants():
    row = np.arange(P)[:, None]
    col = np.arange(P)[None, :]
    f = lambda a: np.ascontiguousarray(a.astype(np.float32))
    c = {}
    c["ident"] = f(row == col)
    c["triu"] = f(row <= col)
    c["mid"] = f((row <= col)) - f((row <= P // 2 - 1) & (col >= 0))
    causal = np.where(row >= col, 0.0, MASKED)
    c["causal"] = f(np.concatenate([causal, np.zeros((P, P)), causal], 1))
    strict, incl = f(row < col), f(row <= col)
    c["wkv_mask"] = f(np.concatenate([strict, incl, strict, incl], 1))
    lv = []
    for level in range(LEVELS):
        n = 1 << level
        lv.append(((row // (2 * n)) == (col // (2 * n))) & ((row // n) % 2 == 1) & ((col // n) % 2 == 0))
    c["level"] = f(np.concatenate(lv, 1))
    half = f((row >= P // 2) & (np.arange(2)[None, :] == 0)) + f((row < P // 2) & (np.arange(2)[None, :] == 1))
    c["halves"] = half
    c["pairs"] = f((row // HD) == (col // HD))
    idx = np.concatenate([np.arange(NC), TH, np.arange(1, CS + 1)])[None, :] + np.zeros((P, 1))
    c["moe_idx"] = f(np.concatenate([idx, row], 1))
    c["anti"] = f(row + col == P - 1)
    causal_t = np.where(row <= col, 0.0, MASKED)
    c["causal_t"] = f(np.concatenate([causal_t, np.zeros((P, P)), causal_t], 1))
    c["tril_strict"] = f(row > col)
    lt, span = [], []
    for level in range(LEVELS):
        n = 1 << level
        lt.append(lv[level].T)
        same = (row // (2 * n)) == (col // (2 * n))
        up_r, up_c = (row // n) % 2 == 1, (col // n) % 2 == 1
        span.append(same & ((up_c & up_r & (row <= col)) | (~up_c & ~up_r & (row > col))))
    c["level_t"] = f(np.concatenate(lt, 1))
    c["span"] = f(np.concatenate(span, 1))
    c["upper"] = f(np.concatenate([(row // (1 << level)) % 2 == 1 for level in range(LEVELS)], 1))
    c["neg_head"] = f(-(np.arange(GH)[:, None] == np.arange(GH * P)[None, :] // P).astype(np.float32))
    j = np.arange(3 * P)
    dist = T * P - 1 - j
    exact = BUCKETS // 2
    nf = np.maximum(dist, 1).astype(np.float32)
    large = exact + (np.log(nf / exact) / math.log(MAX_DIST / exact) * (BUCKETS - exact)).astype(np.int32)
    bucket = np.where(dist < exact, dist, np.minimum(large, BUCKETS - 1))
    c["bucket"] = f(np.where(dist[None, :] >= 0, np.arange(BUCKETS + 1)[:, None] == bucket[None, :],
                             np.arange(BUCKETS + 1)[:, None] == BUCKETS))
    return c


INPUTS = ["x", "c", "norm1_g", "norm2_g", "ada_w", "ada_b", "w_in", "w_out", "fox_qn_g", "fox_kn_g", "fox_on_g",
          "fox_forget_b", "rw_mu", "rw_w0", "rw_decay_up", "rw_a0", "rw_iclr_up", "rw_gate_up", "rw_k_k", "rw_k_a",
          "rw_r_k", "rw_lnx_g", "rw_lnx_b", "router_w", "router_bias", "exp_w_gate", "exp_w_up", "exp_w_down",
          "sh_w_gate", "sh_w_up", "sh_w_down", "final_g", "mem_2", "w_in_2", "b_in_2", "mlstm_norm_2", "sconv_w_2",
          "rel_bias_2", "hgrn_lb_logits_2", "hgrn_norm_2", "w_mix_out_2", "norm_mix_pre_2", "norm_mix_post_2",
          "mem_norm_2", "w_cq_2", "w_ck_2", "w_cv_2", "w_co_2", "norm_cross_pre_2", "norm_cross_post_2",
          "w_ffn_in_2", "ffn_conv_w_2", "ffn_conv_b_2", "w_ffn_out_2", "norm_ffn_pre_2", "norm_ffn_post_2"]
UNLAYERED = ("final_g", "rel_bias_2")
FLAT = ("fox_qn_g", "fox_kn_g", "fox_on_g", "rw_r_k")
CONST_0 = ("ident", "triu")
CONST_1 = ("mid", "causal", "wkv_mask", "level", "halves", "pairs")


CONST_2 = ("anti", "causal_t", "tril_strict", "level_t", "span", "upper", "neg_head", "bucket")

def build(nc, A, consts, out):
    def load_cols(name, lo, n):
        return A[name].rearrange("(k p) n -> p k n", p=P)[:, :, lo:lo + n]

    def bcast(ap1d):
        return bass.AP(ap1d.tensor, ap1d.offset, [[0, P], [1, ap1d.shape[-1]]])

    ctx = ExitStack()

    def sb(name, shape, stack=ctx):
        return stack.enter_context(nc.sbuf_tensor(name, shape, F32))

    def stack_i32(stack, name, shape):
        return stack.enter_context(nc.sbuf_tensor(name, shape, I32))

    def sem(name):
        return ctx.enter_context(nc.semaphore(name))

    with ctx:
        RING = 2
        ring = sb("ring", [P, RING, KT * BANK + BANK])
        x = sb("x", [P, T, D])
        xn = sb("xn", [P, T, D])
        xT = sb("xT", [P, KT, T * P])
        mod = sb("mod", [P, 3, D])
        gain = sb("gain", [P, 2, D])
        small = sb("small", [P, 64])
        ones = sb("ones", [1, P])
        cst = {}
        for name in CONST_0:
            cst[name] = sb("c_" + name, list(consts[name].shape))
        tmp = sb("tmp", [P, D])
        silu_c = sb("silu_c", [P, KT, P])
        ones_pp = sb("ones_pp", [P, P])

        SH, SC, GT = range(3)

        rw_stack = ExitStack()
        for name in CONST_1:
            cst[name] = sb("c_" + name, list(consts[name].shape), rw_stack)
        z_rw = sb("z_rw", [P, T, RW_COLS], rw_stack)
        lora_up = sb("lora_up", [P, BANK], rw_stack)
        gate_up = sb("gate_up", [P, 2, BANK], rw_stack)
        rwp = sb("rwp", [P, 7, W1], rw_stack)
        W0, A0, KK_, KA_, RK_, LG, LB = range(7)

        fox_stack = ExitStack()
        z_fox = sb("z_fox", [P, T, FOX_COLS], fox_stack)
        kv_prev = sb("kv_prev", [P, T, 2 * W1], fox_stack)
        fxp = sb("fxp", [P, 3, W1], fox_stack)
        forget_b = sb("forget_b", [P, HEADS], fox_stack)
        AUG = HD + 2
        q_aug = sb("q_aug", [P, T, HEADS, AUG], fox_stack)
        k_aug = sb("k_aug", [P, T, HEADS, AUG], fox_stack)
        sc_sb = sb("sc_sb", [P, 2, 3 * P], fox_stack)
        pr_sb = sb("pr_sb", [P, 2, 3 * P], fox_stack)
        prT = sb("prT", [P, 2, 3 * P], fox_stack)
        fs = sb("fs", [P, 12, T * 16], fox_stack)
        lerp_stack = ExitStack()
        z_prev = sb("z_prev", [P, T, RW_COLS], lerp_stack)
        mu = sb("mu", [P, RW_COLS], lerp_stack)
        lerp_stack.close()
        q_augT = sb("q_augT", [AUG, HEADS, T * P], fox_stack)
        k_augT = sb("k_augT", [AUG, HEADS, T * P], fox_stack)
        fox_stack.close()

        wkv_stack = ExitStack()
        logw = sb("logw", [P, T, W1], wkv_stack)
        iclr = sb("iclr", [P, T, W1], wkv_stack)
        gate = sb("gate", [P, T, W1], wkv_stack)
        RT_, AT_, BT_, KTT_ = range(4)
        til = sb("til", [P, 4, T, W1], wkv_stack)
        tilT = sb("tilT", [P, 4, 4, P], wkv_stack)
        gram = sb("gram", [P, HEADS, 4, P], wkv_stack)
        lora_stack = ExitStack()
        loraT = sb("loraT", [P, 3, T * P], lora_stack)
        lora_stack.close()
        amat = sb("amat", [P, HEADS, P], wkv_stack)
        inv = sb("inv", [P, HEADS, P], wkv_stack)
        invT = sb("invT", [P, HEADS, P], wkv_stack)
        rhs_u = sb("rhs_u", [P, 2, W1], wkv_stack)
        stateT = sb("stateT", [P, 4, P], wkv_stack)
        ws = sb("ws", [P, 8, T * HEADS], wkv_stack)
        y_rw = sb("y_rw", [P, T, W1], wkv_stack)
        wkv_stack.close()
        rw_stack.close()

        p2_stack = ExitStack()
        GAINS = ("final_g", "norm_mix_pre_2", "norm_mix_post_2", "mem_norm_2", "norm_cross_pre_2",
                 "norm_cross_post_2", "norm_ffn_pre_2", "norm_ffn_post_2")
        gains2 = sb("gains2", [P, len(GAINS) - 2, D], p2_stack)

        def gain_of(i):
            return gain[:, i, :] if i < 2 else gains2[:, i - 2, :]

        ROWS = ("mlstm_norm_2", "hgrn_norm_2", "hgrn_lb_logits_2")
        rows2 = sb("rows2", [P, 3 + 3, GW], p2_stack)
        conv_w = sb("conv_w", [P, 3, FT_TILES], p2_stack)
        conv_b = sb("conv_b", [P, FT_TILES], p2_stack)
        rel = sb("rel", [BUCKETS + 1, GH], p2_stack)
        for name in CONST_2:
            cst[name] = sb("c_" + name, list(consts[name].shape), p2_stack)
        rel_row = sb("rel_row", [GH, 3 * P], p2_stack)
        hankel = sb("hankel", [P, GH, 2 * P], p2_stack)

        moe_stack = ExitStack()
        GU_W = KT * 2 * D_E
        DN_W = (D_E // P) * D
        gu_odd = sb("gu_odd", [P, 2, GU_W], moe_stack)
        dn = sb("dn", [P, 4, DN_W], moe_stack)
        moe_idx = sb("moe_idx", list(consts["moe_idx"].shape), moe_stack)
        chunk_no, thresholds = moe_idx[:, 0:NC], moe_idx[0:EXPERTS, NC:NC + len(TH)]
        slot_no = moe_idx[:, NC + len(TH):NC + len(TH) + CS]
        expert_no = moe_idx[0:EXPERTS, NC + len(TH) + CS:NC + len(TH) + CS + 1]
        taken = [0]

        def in_gu_odd(rows, *dims):
            n = math.prod(dims)
            a = gu_odd[0:rows, 1, taken[0]:taken[0] + n]
            taken[0] += n
            assert taken[0] <= GU_W
            return a if len(dims) == 1 else a.rearrange(("p (a b) -> p a b", "p (a b c) -> p a b c")[len(dims) - 2],
                                                        **dict(zip("ab", dims[:-1])))

        router_w = in_gu_odd(P, KT, EXPERTS)
        router_b = in_gu_odd(P, EXPERTS)
        score = in_gu_odd(P, T, EXPERTS)
        sel = in_gu_odd(P, T, EXPERTS)
        rt = in_gu_odd(P, 6, T, EXPERTS)
        wts = in_gu_odd(P, T, EXPERTS)
        maskT = in_gu_odd(EXPERTS, T * P)
        rankT = in_gu_odd(EXPERTS, T * P)
        wtsT = in_gu_odd(EXPERTS, T * P)
        of_chunk = in_gu_odd(EXPERTS, 2, NC)
        rc = sb("rc", [P, 16], moe_stack)
        place = sb("place", [P, T, NC], moe_stack)
        weight = sb("weight", [P, T, NC], moe_stack)
        expert_of = stack_i32(moe_stack, "expert_of", [1, NC])
        quads_i = stack_i32(moe_stack, "quads_i", [1, 1])
        hgT = xT[:, :, 0:P]
        y_sb = mod[:, SC, :]
        pick = mod[:, SH, 0:BANK].rearrange("p (b t c) -> p b t c", b=2, t=T)
        putT = mod[:, SH, BANK:D].rearrange("p (b t c) -> p b t c", b=2, t=T)
        silu_g = silu_c[:, 4:8, :].rearrange("p (t b) c -> p t (b c)", t=T)
        act_e = tmp[:, 0:BANK].rearrange("p (t c) -> p t c", t=T)
        act_eT = tmp[:, BANK:D].rearrange("p (t k c) -> p t k c", t=T, k=D_E // P)
        put = silu_c[:, 0:4, :].rearrange("p (b t) c -> p b t c", b=2)
        moe_stack.close()

        mix_stack = ExitStack()
        z2 = sb("z2", [P, T, IN2], mix_stack)
        ms = sb("ms", [P, 28, T * GH], mix_stack)
        e_row = sb("e_row", [GH, 2, T * P], mix_stack)
        qT2 = sb("qT2", [P, 2, T * P], mix_stack)
        kT2 = sb("kT2", [P, 2, T * P], mix_stack)
        v_aug = sb("v_aug", [P, T, GH, HD + 1], mix_stack)
        sc2 = sb("sc2", [P, 2, 3 * P], mix_stack)
        pr2 = sb("pr2", [P, 2, 3 * P], mix_stack)
        wT2 = sb("wT2", [P, 2, 3 * P], mix_stack)
        conv = sb("conv", [P, 3, T, GW], mix_stack)
        hg = sb("hg", [P, 5, T, GW], mix_stack)
        LF, HQ, HK, QK, HS = range(5)
        ex2 = sb("ex2", [P, 2, T * GW], mix_stack)
        fT = sb("fT", [P, 2, T * P], mix_stack)
        at = mod[:, SH, :].rearrange("p (a i c) -> p a i c", a=2, i=4)
        atx = mod[:, SC, 0:BANK].rearrange("p (a i c) -> p a i c", a=2, i=2)
        mix_stack.close()

        end_stack = ExitStack()
        hbuf = sb("hbuf", [P, T, D], end_stack)
        mem = sb("mem", [P, T, D], end_stack)
        memT = sb("memT", [P, KT, T * P], end_stack)
        ckT = sb("ckT", [P, CH, T * P], end_stack)
        cqT = sb("cqT", [P, CH, T * P], end_stack)
        cv = sb("cv", [P, T, CW], end_stack)
        scx = sb("scx", [P, 2, T, 2 * P], end_stack)
        prx = sb("prx", [P, 2, T, 2 * P], end_stack)
        prxT = sb("prxT", [P, 2, 4 * P], end_stack)
        cs = sb("cs", [P, 6, T * CH], end_stack)
        end_stack.close()
        ffn_stack = ExitStack()
        hbuf_f = sb("hbuf_f", [P, T, D], ffn_stack)
        gateT = sb("gateT", [P, 2, 2, 2 + T * P], ffn_stack)
        convT = sb("convT", [P, 2, 2, T * P], ffn_stack)
        siluT = sb("siluT", [P, 2, 2, T * P], ffn_stack)
        actT = sb("actT", [P, FT_TILES, T * P], ffn_stack)
        ffn_stack.close()
        p2_stack.close()

        bank = [ctx.enter_context(nc.psum_tensor(f"bank{i}", [P, BANK], F32)) for i in range(8)]

        w_full = [sem(f"w_full{i}") for i in range(RING)]
        w_used = sem("w_used")
        lin_mm = sem("lin_mm")
        lin_evac = sem("lin_evac")
        tp_mm = sem("tp_mm")
        tp_evac = sem("tp_evac")
        sc_mm = sem("sc_mm")
        sc_evac = sem("sc_evac")
        x_loaded = sem("x_loaded")
        c_loaded = sem("c_loaded")
        const_loaded = sem("const_loaded")
        gain_loaded = [sem(f"gain_loaded{i}") for i in range(2)]
        par_loaded = sem("par_loaded")
        silu_done = sem("silu_done")
        cb_ready = sem("cb_ready")
        ones_ready = sem("ones_ready")
        inv_var = sem("inv_var")
        rstd_done = sem("rstd_done")
        xn_ready = sem("xn_ready")
        mod_used = sem("mod_used")
        pad_zero = sem("pad_zero")
        kv_shifted = sem("kv_shifted")
        zr_shifted = sem("zr_shifted")
        lerp_done = sem("lerp_done")
        pool_chain = sem("pool_chain")
        vec_chain = sem("vec_chain")
        act_chain = sem("act_chain")
        fox_gates = sem("fox_gates")
        fox_in = sem("fox_in")
        fox_ln = sem("fox_ln")
        logf_ready = sem("logf_ready")
        aug_ready = sem("aug_ready")
        negmax_ready = sem("negmax_ready")
        prob_ready = sem("prob_ready")
        pv_mm = sem("pv_mm")
        pv_evac = sem("pv_evac")
        fox_sig = sem("fox_sig")
        rw_tanh = sem("rw_tanh")
        lora_in = sem("lora_in")
        rw_sig = sem("rw_sig")
        logw_ready = sem("logw_ready")
        rw_exp = sem("rw_exp")
        til_ready = sem("til_ready")
        wkv_w = sem("wkv_w")
        wkv_mm = sem("wkv_mm")
        wkv_upd = sem("wkv_upd")
        u_mm = sem("u_mm")
        u_evac = sem("u_evac")
        state_ready = sem("state_ready")
        y_ready = sem("y_ready")
        x1_ready = sem("x1_ready")
        router_loaded = sem("router_loaded")
        router_sig = sem("router_sig")
        sh_full = sem("sh_full")
        gu_full = [sem(f"gu_full{i}") for i in range(2)]
        dn_full = [sem(f"dn_full{i}") for i in range(2)]
        mixer_read = sem("mixer_read")
        routed = sem("routed")
        quads_ready = sem("quads_ready")
        pick_ready = sem("pick_ready")
        gather_mm = sem("gather_mm")
        gather_copied = sem("gather_copied")
        gu_mm = sem("gu_mm")
        gate_act = sem("gate_act")
        act_made = sem("act_made")
        actT_mm = sem("actT_mm")
        actT_copied = sem("actT_copied")
        down_mm = sem("down_mm")
        y_copied = sem("y_copied")
        put_mm = sem("put_mm")
        put_copied = sem("put_copied")
        spread_mm = sem("spread_mm")
        experts_added = sem("experts_added")
        experts_copied = sem("experts_copied")
        x2_ready = sem("x2_ready")
        w_done = sem("w_done")
        p2_loaded = sem("p2_loaded")
        rel_made = sem("rel_made")
        rel_mm = sem("rel_mm")
        rel_copied = sem("rel_copied")
        hankel_made = sem("hankel_made")
        ml_in = sem("ml_in")
        ml_ln = sem("ml_ln")
        ml_logf = sem("ml_logf")
        e_ready = sem("e_ready")
        m_row = sem("m_row")
        qk_ready = sem("qk_ready")
        m_ready = sem("m_ready")
        m_exp = sem("m_exp")
        d_ready = sem("d_ready")
        w_exp = sem("w_exp")
        w_ready = sem("w_ready")
        o_mm = sem("o_mm")
        o_used = sem("o_used")
        den_ready = sem("den_ready")
        z2_act = sem("z2_act")
        conv_prod = sem("conv_prod")
        conv_shift = sem("conv_shift")
        f_ready = sem("f_ready")
        hg_act = sem("hg_act")
        hg_exp = sem("hg_exp")
        ft_src = sem("ft_src")
        mem_loaded = sem("mem_loaded")
        up_mm = sem("up_mm")
        conv_done = sem("conv_done")
        silu_ready = sem("silu_ready")
        act_ready = sem("act_ready")
        ffn_mm = sem("ffn_mm")
        h_used = sem("h_used")
        out_ready = sem("out_ready")
        store_done = sem("store_done")

        jobs = []

        def job(kind, w, lo, n, kt=KT, bias=None):
            dst = lambda slot: ring[:, slot, 0:kt * n].rearrange("p (k n) -> p k n", k=kt)
            parts = [(dst, A[w].rearrange("(k p) n -> p k n", p=P)[:, :, lo:lo + n])]
            if bias is not None:
                parts.append((lambda slot: ring[0:1, slot, KT * BANK:KT * BANK + n],
                              A[bias][lo:lo + n].rearrange("(a n) -> a n", a=1)))
            jobs.append((kind, lo, n, kt, parts, bias is not None))

        ADA_FIRST = [(SH, 0), (SH, 1), (SC, 0), (SC, 1)]
        ADA_GATE = [(GT, 0), (GT, 1)]
        for which, h in ADA_FIRST:
            job("ada", "ada_w", which * D + h * BANK, BANK, bias="ada_b")
        FOX_JOBS = [(512, 512), (1024, 512), (2048, 24), (0, 512), (1536, 512)]
        RW_JOBS = [(FOX_COLS, 512), (FOX_COLS + 512, 512), (FOX_COLS + 1024, 512), (FOX_COLS + 1536, 288)]
        for lo, n in FOX_JOBS + RW_JOBS:
            job("in", "w_in", lo, n)
        for which, h in ADA_GATE:
            job("ada", "ada_w", which * D + h * BANK, BANK, bias="ada_b")
        for which, h in ADA_FIRST:
            job("ada", "ada_w", (3 + which) * D + h * BANK, BANK, bias="ada_b")
        for h in range(2):
            job("out", "w_out", h * BANK, BANK)
        for h in range(2):
            job("ada", "ada_w", 5 * D + h * BANK, BANK, bias="ada_b")
        for lo in range(0, IN2, BANK):
            job("in2", "w_in_2", lo, min(BANK, IN2 - lo), bias="b_in_2")
        for h in range(2):
            job("mix", "w_mix_out_2", h * BANK, BANK)
        for w in ("w_ck_2", "w_cv_2", "w_cq_2"):
            job("cross", w, 0, CW)
        job("co", "w_co_2", 0, D, kt=CW // P)
        for i in range(FF_JOBS):
            job("ffn", "w_ffn_in_2", i * 256, 256)
            dst = lambda slot, lo=0: ring[:, slot, 0:KT * BANK].rearrange("p (k n) -> p k n", k=KT)[:, :, lo:lo + 256]
            w = A["w_ffn_in_2"].rearrange("(k p) n -> p k n", p=P)
            jobs[-1][4][:] = [(dst, w[:, :, i * 256:(i + 1) * 256]),
                              (lambda slot, f=dst: f(slot, 256), w[:, :, D_FF + i * 256:D_FF + (i + 1) * 256])]
        for i in range(0, FT_TILES, 4):
            n = min(4, FT_TILES - i)
            job("ffn_out", "w_ffn_out_2", 0, D, kt=n)
            jobs[-1][4][:] = [(lambda slot, n=n: ring[:, slot, 0:n * D].rearrange("p (k n) -> p k n", k=n),
                               A["w_ffn_out_2"].rearrange("(k p) n -> p k n", p=P)[:, i:i + n, :])]
        N_OUT = dict(ada=1, co=4, ffn=1, ffn_out=0)
        outputs = {}
        for j, (kind, *_rest) in enumerate(jobs):
            for t in range(N_OUT.get(kind, T)):
                outputs[(j, t)] = len(outputs)
        J_ADA1, J_FOX, J_RW = 0, 4, 4 + len(FOX_JOBS)
        J_GATE = J_RW + len(RW_JOBS)
        J_ADA2 = J_GATE + 2
        J_OUT = J_ADA2 + 4
        J_GATE2 = J_OUT + 2
        J_IN2 = J_GATE2 + 2
        N_P2 = len(GAINS) + len(ROWS) + 3 + 2 + 1 + len(CONST_2)
        N_IN2 = -(-IN2 // BANK)
        J_MIX = J_IN2 + N_IN2
        J_CK, J_CV, J_CQ, J_CO = (J_MIX + 2 + i for i in range(4))
        J_FFN = J_CO + 1
        J_FFO = J_FFN + FF_JOBS
        assert J_FFO + -(-FT_TILES // 4) == len(jobs)

        def after(j, t=0):
            return outputs[(j, t)] + 1

        TP_H = 0
        TP_AUG = 4
        TP_PROB = TP_AUG + 8
        TP_LORA = TP_PROB + HEADS
        TP_TIL = TP_LORA + 2
        TP_Y = TP_TIL + 8
        SC_CUMF = 0
        SC_FOX = 1
        SC_LORA = SC_FOX + HEADS
        SC_CUM = SC_LORA + 6
        SC_GRAM = SC_CUM + 3
        SC_ROUTER = SC_GRAM + 21
        SC_ROUTE = SC_ROUTER + 1
        SC_G2 = SC_ROUTE + 4
        SC_ML = SC_G2 + 1
        SC_MOBA = SC_ML + 2 * GH
        SC_HG = SC_MOBA + GH
        SC_X = SC_HG + 3 * (LEVELS + 1)
        TP_H2 = TP_Y + 4
        TP_IN2 = TP_H2 + 4
        TP_ML = TP_IN2 + 4
        TP_MOBA = TP_ML + 4
        TP_P2 = TP_MOBA + 2
        TP_HG = TP_P2 + GH
        TP_Y2 = TP_HG + LEVELS + 1
        TP_MEM = TP_Y2 + 4
        TP_XN = TP_MEM + 4
        TP_PX = TP_XN + 4
        TP_O = TP_PX + CH
        TP_FF = TP_O + 2


        def slot(h):
            return 4 * (h % 2) + h // 2

        def wkv_count(t, level, g, which):
            base = t * (2 + 4 * (LEVELS - 1))
            return base + g + 1 if level == 0 else base + 2 + 4 * (level - 1) + 2 * g + 1 + which

        block = ctx.enter_context(nc.Block())

        @block.sync
        def _(sp):
            def stream(first, last):
                for j in range(first, last):
                    if j >= RING:
                        sp.wait_ge(w_used, j - RING + 1)
                    for dst, src in jobs[j][4]:
                        sp.dma_start(dst(j % RING), src).then_inc(w_full[j % RING], 16)

            stream(0, J_IN2)
            def gate_up(dst, gate_w, up_w, full):
                dst = dst.rearrange("p (k n) -> p k n", k=KT)
                sp.dma_start(dst[:, :, 0:D_E], gate_w.rearrange("(k p) n -> p k n", p=P)).then_inc(full, 16)
                sp.dma_start(dst[:, :, D_E:2 * D_E], up_w.rearrange("(k p) n -> p k n", p=P)).then_inc(full, 16)

            def down(dst, down_w, full):
                sp.dma_start(dst.rearrange("p (k n) -> p k n", k=D_E // P),
                             down_w.rearrange("(k p) n -> p k n", p=P)).then_inc(full, 16)

            sp.wait_ge(mixer_read, 1)
            gate_up(gu_odd[:, 0, :], A["sh_w_gate"], A["sh_w_up"], sh_full)
            down(dn[:, 2, :], A["sh_w_down"], sh_full)
            sp.wait_ge(quads_ready, 1)
            sp.wait_ge(w_used, J_IN2)
            quads = sp.value_load(quads_i[0:1, 0:1], min_val=1, max_val=MAX_QUADS)
            with sp.Fori(0, quads) as i:
                for parity in range(2):
                    p = i * 2 + parity
                    e = [sp.value_load(expert_of[0:1, bass.ds(i * 4 + 2 * parity + c, 1)], min_val=0,
                                       max_val=EXPERTS - 1) for c in range(2)]
                    sp.wait_ge(gu_mm, p + 1)
                    for c in range(2):
                        gate_up(ring[:, c, 0:GU_W] if parity == 0 else gu_odd[:, c, :],
                                A["exp_w_gate"][e[c]], A["exp_w_up"][e[c]], gu_full[parity])
                    sp.wait_ge(spread_mm, p + 2)
                    for c in range(2):
                        down(dn[:, 2 * parity + c, :], A["exp_w_down"][e[c]], dn_full[parity])
            sp.wait_ge(experts_copied, 1)
            stream(J_IN2, len(jobs))
            sp.wait_ge(out_ready, 1)
            sp.dma_start(out.rearrange("(t p) d -> p t d", p=P), x[:, :, :]).then_inc(store_done, 16)
            sp.wait_ge(store_done, 16)

        @block.scalar
        def _(act):
            chain = [0]

            def link(ins):
                chain[0] += 1
                ins.then_inc(act_chain, 1)
                act.wait_ge(act_chain, chain[0])

            rstd_n = [0]

            def rstd(dst, src):
                rstd_n[0] += 1
                act.wait_ge(inv_var, rstd_n[0])
                act.activation(dst, src, ACT.Sqrt).then_inc(rstd_done, 1)

            def lin_copy(j, t, dst):
                act.wait_ge(lin_mm, after(j, t))
                act.activation(dst, bank[outputs[(j, t)] % 2][:, 0:jobs[j][2]], ACT.Copy).then_inc(lin_evac, 1)

            def lin_copy_heads(j, i, dst):
                act.wait_ge(lin_mm, after(j, i))
                act.activation(dst[:, 2 * i:2 * i + 2, :],
                               bank[outputs[(j, i)] % 2][:, :].rearrange("p (h c) -> p h c", h=2), ACT.Copy)\
                    .then_inc(lin_evac, 1)

            act.dma_start(small[:, 0:KT], A["c"]).then_inc(c_loaded, 16)
            act.dma_start(x[:, :, :], A["x"].rearrange("(t p) d -> p t d", p=P)).then_inc(x_loaded, 16)
            act.dma_start(gain[:, 0, :], bcast(A["norm1_g"])).then_inc(gain_loaded[0], 16)
            act.dma_start(gain[:, 1, :], bcast(A["norm2_g"])).then_inc(gain_loaded[1], 16)
            for name in CONST_0 + CONST_1:
                act.dma_start(cst[name][:, :], consts[name]).then_inc(const_loaded, 16)
            for i, name in enumerate(("fox_qn_g", "fox_kn_g", "fox_on_g")):
                act.dma_start(fxp[:, i, :], bcast(A[name])).then_inc(par_loaded, 16)
            act.dma_start(forget_b[:, :], bcast(A["fox_forget_b"])).then_inc(par_loaded, 16)
            act.dma_start(mu[:, :], bcast(A["rw_mu"])).then_inc(par_loaded, 16)
            for i, name in enumerate(("rw_w0", "rw_a0", "rw_k_k", "rw_k_a", "rw_r_k", "rw_lnx_g", "rw_lnx_b")):
                act.dma_start(rwp[:, i, :], bcast(A[name])).then_inc(par_loaded, 16)
            act.dma_start(lora_up[0:DECAY_R, :], A["rw_decay_up"]).then_inc(par_loaded, 16)
            act.dma_start(lora_up[DECAY_R:P, :], A["rw_iclr_up"]).then_inc(par_loaded, 16)
            act.dma_start(gate_up[:, 0, :], A["rw_gate_up"][0:P, :]).then_inc(par_loaded, 16)
            act.dma_start(gate_up[0:GATE_R - P, 1, :], A["rw_gate_up"][P:GATE_R, :]).then_inc(par_loaded, 16)

            act.wait_ge(c_loaded, 16)
            act.activation(small[:, KT:2 * KT], small[:, 0:KT], ACT.Silu).then_inc(silu_done, 1)
            rstd(small[:, 18:20], small[:, 16:18])
            for j, (which, h) in enumerate(ADA_FIRST):
                lin_copy(J_ADA1 + j, 0, mod[:, which, h * BANK:(h + 1) * BANK])
            for j, (lo, n) in enumerate(FOX_JOBS):
                for t in range(T):
                    lin_copy(J_FOX + j, t, z_fox[:, t, lo:lo + n])
                if lo == 2048:
                    act.wait_ge(lin_evac, after(J_FOX + j, 1))
                    act.activation(fs[:, 0, :].rearrange("p (t h) -> p t h", t=T), z_fox[:, :, 2056:2072],
                                   ACT.Sigmoid).then_inc(fox_gates, 1)
                    act.wait_ge(fox_in, 1)
                    link(act.activation(fs[:, 2, 0:16], fs[:, 1, 0:16], ACT.Abs))
                    link(act.activation(fs[:, 3, 0:16], fs[:, 2, 0:16], ACT.Exp, scale=-1.0))
                    act.activation(fs[:, 4, 0:16], fs[:, 3, 0:16], ACT.Ln, bias=1.0).then_inc(fox_ln, 1)
            for j, (lo, n) in enumerate(RW_JOBS):
                for t in range(T):
                    lin_copy(J_RW + j, t, z_rw[:, t, lo - FOX_COLS:lo - FOX_COLS + n])
            rstd(fs[:, 6, 0:16], fs[:, 5, 0:16])
            rstd(fs[:, 8, 0:16], fs[:, 7, 0:16])
            act.wait_ge(lin_evac, after(J_FOX + 4, 1))
            act.activation(z_fox[:, :, 1536:2048], z_fox[:, :, 1536:2048], ACT.Sigmoid).then_inc(fox_sig, 1)
            for j, (which, h) in enumerate(ADA_GATE):
                lin_copy(J_GATE + j, 0, mod[:, which, h * BANK:(h + 1) * BANK])
            act.wait_ge(mod_used, 1)
            for j, (which, h) in enumerate(ADA_FIRST):
                lin_copy(J_ADA2 + j, 0, mod[:, which, h * BANK:(h + 1) * BANK])
            for h in range(HEADS):
                act.wait_ge(negmax_ready, h + 1)
                if h >= 2:
                    act.wait_ge(tp_evac, TP_PROB + h - 1)
                act.activation(pr_sb[:, h % 2, 0:P], sc_sb[:, h % 2, 0:P], ACT.Exp,
                               bias=fs[:, 9, 2 * h:2 * h + 1], accum_out=fs[:, 10, 2 * h:2 * h + 1])
                act.activation(pr_sb[:, h % 2, P:3 * P], sc_sb[:, h % 2, P:3 * P], ACT.Exp,
                               bias=fs[:, 9, 2 * h + 1:2 * h + 2], accum_out=fs[:, 10, 2 * h + 1:2 * h + 2])\
                    .then_inc(prob_ready, 1)
            rstd(fs[:, 6, 0:16], fs[:, 5, 0:16])
            act.wait_ge(lerp_done, 2)
            act.activation(z_rw[:, :, 1536:1600], z_rw[:, :, 1536:1600], ACT.Tanh)
            act.activation(z_rw[:, :, 1664:1824], z_rw[:, :, 1664:1824], ACT.Sigmoid).then_inc(rw_tanh, 1)
            for t in range(T):
                act.wait_ge(lora_in, 2 * t + 1)
                act.activation(logw[:, t, :], logw[:, t, :], ACT.Sigmoid).then_inc(rw_sig, 1)
                act.wait_ge(lora_in, 2 * t + 2)
                act.activation(iclr[:, t, :], iclr[:, t, :], ACT.Sigmoid).then_inc(rw_sig, 1)
            rstd(ws[:, 1, :], ws[:, 0, :])
            for t in range(T):
                act.wait_ge(sc_mm, SC_CUM + t + 1)
                act.activation(rhs_u[:, 0, :], bank[6 + (SC_CUM + t) % 2][:, :], ACT.Exp)
                act.activation(rhs_u[:, 1, :], bank[6 + (SC_CUM + t) % 2][:, :], ACT.Exp, scale=-1.0)\
                    .then_inc(rw_exp, 1)
                act.wait_ge(logw_ready, 2 + t + 1)
                act.activation(y_rw[:, t, :], y_rw[:, t, :], ACT.Exp).then_inc(rw_exp, 1)
                act.wait_ge(til_ready, t + 1)
            act.wait_ge(sc_mm, SC_CUM + 3)
            act.activation(ws[:, 2, 0:4], bank[6 + (SC_CUM + 2) % 2][:, 0:4], ACT.Exp).then_inc(rw_exp, 1)
            for t in range(T):
                act.wait_ge(u_mm, 3 * t + 1)
                act.activation(rhs_u[:, 0, :], bank[2][:, :], ACT.Copy).then_inc(u_evac, 1)
                act.wait_ge(u_mm, 3 * t + 2)
                act.activation(rhs_u[:, 1, :], bank[3][:, :], ACT.Copy).then_inc(u_evac, 1)
                act.wait_ge(u_mm, 3 * t + 3)
                act.activation(y_rw[:, t, :], bank[2][:, :], ACT.Copy).then_inc(u_evac, 1)
            rstd(ws[:, 1, :], ws[:, 0, :])
            act.wait_ge(y_ready, 1)
            act.dma_start(router_w[:, :, :], A["router_w"].rearrange("(k p) n -> p k n", p=P)).then_inc(router_loaded, 16)
            act.dma_start(router_b[:, :], bcast(A["router_bias"])).then_inc(router_loaded, 16)
            act.dma_start(moe_idx[:, :], consts["moe_idx"]).then_inc(router_loaded, 16)
            for i, name in enumerate(GAINS):
                if i >= 2:
                    act.dma_start(gain_of(i), bcast(A[name])).then_inc(p2_loaded, 16)
            for i, name in enumerate(ROWS):
                act.dma_start(rows2[:, i, :], bcast(A[name])).then_inc(p2_loaded, 16)
            for i in range(3):
                act.dma_start(rows2[:, 3 + i, :], bcast(A["sconv_w_2"][i])).then_inc(p2_loaded, 16)
            act.dma_start(conv_w[:, :, :], A["ffn_conv_w_2"]).then_inc(p2_loaded, 16)
            act.dma_start(conv_b[:, :], A["ffn_conv_b_2"]).then_inc(p2_loaded, 16)
            act.wait_ge(rel_made, 1)
            act.dma_start(rel[0:BUCKETS, :], A["rel_bias_2"]).then_inc(p2_loaded, 16)
            for name in CONST_2:
                act.dma_start(cst[name][:, :], consts[name]).then_inc(p2_loaded, 16)
            rstd(small[:, 18:20], small[:, 16:18])
            act.wait_ge(x1_ready, 2)
            for h in range(2):
                lin_copy(J_GATE2 + h, 0, mod[:, GT, h * BANK:(h + 1) * BANK])
            act.wait_ge(xn_ready, 2)
            for i in range(2):
                act.dma_start(gain_of(i), bcast(A[GAINS[i]])).then_inc(p2_loaded, 16)
            act.wait_ge(sc_mm, SC_ROUTER + 1)
            act.activation(score[:, :, :], bank[6 + SC_ROUTER % 2][:, 0:T * EXPERTS].rearrange("p (t e) -> p t e", t=T),
                           ACT.Sigmoid).then_inc(router_sig, 1)

            for t in range(T):
                act.wait_ge(gu_mm, t + 1)
                act.activation(silu_g[:, t, :], bank[4 + t][:, 0:D_E], ACT.Silu).then_inc(gate_act, 1)
            for t in range(T):
                act.wait_ge(actT_mm, t + 1)
                act.activation(act_eT[:, t, :, :], bank[6 + t][:, 0:D_E].rearrange("p (k c) -> p k c", c=P),
                               ACT.Copy).then_inc(actT_copied, 1)

            def gathered(p):
                act.wait_ge(gu_mm, p + 2)
                for h in range(2):
                    act.wait_ge(gather_mm, p * 2 + h + 1)
                    act.activation(hgT[:, 4 * h:4 * h + 4, :], bank[6 + h][:, :].rearrange("p (k c) -> p k c", c=P),
                                   ACT.Copy).then_inc(gather_copied, 1)

            def put_copy(p, parity):
                act.wait_ge(put_mm, p + 1)
                act.activation(putT[:, parity, :, :], bank[5][:, 2 * P:4 * P].rearrange("p (t c) -> p t c", t=T),
                               ACT.Copy).then_inc(put_copied, 1)

            gathered(0)
            put_copy(0, 0)
            act.wait_ge(quads_ready, 1)
            quads = act.value_load(quads_i[0:1, 0:1], min_val=1, max_val=MAX_QUADS)
            with act.Fori(0, quads) as i:
                for parity in range(2):
                    p = i * 2 + parity
                    act.wait_ge(gu_mm, p + 3)
                    act.activation(silu_g[:, 0, :], bank[4][:, 0:D_E], ACT.Silu).then_inc(gate_act, 1)
                    gathered(p + 1)
                    act.wait_ge(actT_mm, p + 3)
                    act.activation(act_eT[:, 0, :, :], bank[5][:, 0:D_E].rearrange("p (k c) -> p k c", c=P),
                                   ACT.Copy).then_inc(actT_copied, 1)
                    act.wait_ge(spread_mm, p + 3)
                    for h in range(2):
                        act.wait_ge(down_mm, p * 2 + 1 + h)
                        act.activation(y_sb[:, h * BANK:(h + 1) * BANK], bank[6 + h][:, :], ACT.Copy)\
                            .then_inc(y_copied, 1)
                    put_copy(p + 1, 1 - parity)
            act.sem_inc(experts_copied, 1)
            act.wait_ge(hankel_made, 1)
            for h in range(GH):
                row = rel_row[h:h + 1, :]
                act.dma_start(hankel[:, h, :], bass.AP(row.tensor, row.offset, [list(row.ap[0]), [1, P], [1, 2 * P]]))\
                    .then_inc(rel_copied, 16)
            rstd(small[:, 18:20], small[:, 16:18])
            rstd(small[:, 18:20], small[:, 16:18])
            for j in range(N_IN2):
                lo, n = jobs[J_IN2 + j][1:3]
                for t in range(T):
                    lin_copy(J_IN2 + j, t, z2[:, t, lo:lo + n])
                if j == 2:
                    act.wait_ge(lin_evac, after(J_IN2 + j, 1))
                    f = ms[:, 0, :].rearrange("p (t h) -> p t h", t=T)
                    link(act.activation(f, z2[:, :, M_F:M_F + GH], ACT.Abs))
                    link(act.activation(ms[:, 1, :], ms[:, 0, :], ACT.Exp, scale=-1.0))
                    act.activation(ms[:, 2, :], ms[:, 1, :], ACT.Ln, bias=1.0).then_inc(ml_ln, 1)
            act.wait_ge(lin_evac, after(J_IN2 + N_IN2 - 1, 1))
            act.activation(z2[:, :, M_O:M_O + GW], z2[:, :, M_O:M_O + GW], ACT.Sigmoid).then_inc(z2_act, 1)
            act.activation(hg[:, LF, :, :], z2[:, :, H_F:H_F + GW], ACT.Sigmoid)
            act.activation(hg[:, HQ, :, :], z2[:, :, H_Q:H_Q + GW], ACT.Silu)
            act.activation(z2[:, :, H_G:H_G + GW], z2[:, :, H_G:H_G + GW], ACT.Silu).then_inc(hg_act, 1)
            act.wait_ge(f_ready, 1)
            act.activation(rows2[:, 2, :], rows2[:, 2, :], ACT.Exp).then_inc(hg_act, 1)
            act.wait_ge(f_ready, 2)
            act.activation(hg[:, LF, :, :], hg[:, LF, :, :], ACT.Ln).then_inc(hg_act, 1)
            act.wait_ge(m_ready, 1)
            act.activation(ms[:, 8, :], ms[:, 7, :], ACT.Exp, scale=-1.0).then_inc(m_exp, 1)
            for h in range(GH):
                act.wait_ge(d_ready, h + 1)
                if h >= 2:
                    act.wait_ge(w_ready, h - 1)
                act.activation(pr2[:, h % 2, 0:2 * P], sc2[:, h % 2, 0:2 * P], ACT.Exp, bias=ms[:, 5, h:h + 1])
                act.activation(pr2[:, h % 2, 2 * P:3 * P], sc2[:, h % 2, 2 * P:3 * P], ACT.Exp,
                               bias=ms[:, 5, GH + h:GH + h + 1]).then_inc(w_exp, 1)
            act.wait_ge(den_ready, 1)
            act.activation(ms[:, 10, :], ms[:, 9, :], ACT.Abs).then_inc(m_exp, 1)
            rstd(ms[:, 12, :], ms[:, 11, :])
            for h in range(GH):
                act.wait_ge(d_ready, GH + h + 1)
                if h >= 2:
                    act.wait_ge(tp_evac, TP_P2 + h - 1)
                act.activation(pr2[:, h % 2, 0:P], sc2[:, h % 2, 0:P], ACT.Exp,
                               bias=ms[:, 13, 2 * h:2 * h + 1], accum_out=ms[:, 14, 2 * h:2 * h + 1])
                act.activation(pr2[:, h % 2, P:3 * P], sc2[:, h % 2, P:3 * P], ACT.Exp,
                               bias=ms[:, 13, 2 * h + 1:2 * h + 2], accum_out=ms[:, 14, 2 * h + 1:2 * h + 2])\
                    .then_inc(w_exp, 1)
            for level in range(LEVELS + 1):
                n = SC_HG + 3 * level
                act.wait_ge(sc_mm, n + 1)
                if level >= 2:
                    act.wait_ge(ft_src, level - 1)
                act.activation(ex2[:, level % 2, :], bank[6 + n % 2][:, :], ACT.Exp).then_inc(hg_exp, 1)
            rstd(ms[:, 17, :], ms[:, 16, :])
            act.wait_ge(y_ready, 2)
            act.dma_start(mem[:, :, :], A["mem_2"].rearrange("(t p) d -> p t d", p=P)).then_inc(mem_loaded, 16)
            rstd(small[:, 18:20], small[:, 16:18])
            for j in range(2):
                for t in range(T):
                    lin_copy(J_MIX + j, t, hbuf[:, t, j * BANK:(j + 1) * BANK])
            for i in range(2):
                lin_copy_heads(J_CK, i, ckT)
            for t in range(T):
                lin_copy(J_CV, t, cv[:, t, :])
            rstd(small[:, 18:20], small[:, 16:18])
            rstd(small[:, 18:20], small[:, 16:18])
            for i in range(2):
                lin_copy_heads(J_CQ, i, cqT)
            for h in range(CH):
                act.wait_ge(d_ready, 2 * GH + h + 1)
                if h >= 2:
                    act.wait_ge(tp_evac, TP_PX + h - 1)
                for t in range(T):
                    ins = act.activation(prx[:, h % 2, t, :], scx[:, h % 2, t, :], ACT.Exp, scale=CHD ** -0.5,
                                         bias=cs[:, 0, T * h + t:T * h + t + 1],
                                         accum_out=cs[:, 1, T * h + t:T * h + t + 1])
                ins.then_inc(w_exp, 1)
            act.wait_ge(h_used, 1)
            for i in range(4):
                act.wait_ge(lin_mm, after(J_CO, i))
                act.activation(hbuf[:, i // 2, (i % 2) * BANK:(i % 2 + 1) * BANK],
                               bank[outputs[(J_CO, i)] % 2][:, :], ACT.Copy).then_inc(lin_evac, 1)
            rstd(small[:, 18:20], small[:, 16:18])
            rstd(small[:, 18:20], small[:, 16:18])
            act.wait_ge(h_used, 3)

            def ffn_silu(i):
                act.wait_ge(conv_done, i + 1)
                if i >= 2:
                    act.wait_ge(act_ready, i - 1)
                act.activation(siluT[:, i % 2, :, :], convT[:, i % 2, :, :], ACT.Silu).then_inc(silu_ready, 1)

            for i in range(FF_JOBS):
                act.wait_ge(lin_mm, after(J_FFN + i))
                if i >= 2:
                    act.wait_ge(conv_done, i - 1)
                act.activation(gateT[:, i % 2, :, 2:2 + T * P],
                               bank[outputs[(J_FFN + i, 0)] % 2][:, :].rearrange("p (i c) -> p i c", i=2),
                               ACT.Copy).then_inc(lin_evac, 1)
                if i:
                    ffn_silu(i - 1)
            ffn_silu(FF_JOBS - 1)
            for t in range(T):
                act.wait_ge(ffn_mm, 2 * t + 2)
                for h in range(2):
                    ins = act.activation(hbuf_f[:, t, h * BANK:(h + 1) * BANK], bank[2 + 2 * t + h][:, :], ACT.Copy)
                ins.then_inc(x2_ready, 1)
            rstd(small[:, 18:20], small[:, 16:18])

        @block.tensor
        def _(pe):
            full = [0] * RING
            lin_n = [0]
            tp_n = [0]
            sc_n = [0]

            def dense(j, lhs, tiles=T, bias=False):
                kind, lo, n, kt, parts, _ = jobs[j]
                full[j % RING] += 16 * len(parts)
                pe.wait_ge(w_full[j % RING], full[j % RING])
                for t in range(tiles):
                    o = outputs[(j, t)]
                    if o >= 2:
                        pe.wait_ge(lin_evac, o - 1)
                    for k in range(kt):
                        mm = pe.matmul(bank[o % 2][:, 0:n], lhs(k, t), ring[:, j % RING, k * n:(k + 1) * n],
                                       start=(k == 0), stop=(k == kt - 1 and not bias))
                    if bias:
                        mm = pe.matmul(bank[o % 2][:, 0:n], ones[0:1, :],
                                       ring[0:1, j % RING, KT * BANK:KT * BANK + n], start=False, stop=True)
                    mm.then_inc(lin_mm, 1)
                pe.wait_ge(lin_mm, outputs[(j, tiles - 1)] + 1)
                pe.sem_inc(w_used, 1)

            def transposes(items):
                n = tp_n[0]
                tp_n[0] += 1
                if n >= 2:
                    pe.wait_ge(tp_evac, n - 1)
                for (lo, hi, rows, src) in items:
                    m = src.shape[0]
                    mm = pe.transpose(bank[4 + n % 2][0:rows, lo:hi], src, cst["ident"][0:m, 0:m])
                mm.then_inc(tp_mm, 1)

            def score_bank():
                n = sc_n[0]
                sc_n[0] += 1
                if n >= 2:
                    pe.wait_ge(sc_evac, n - 1)
                return bank[6 + n % 2]

            def transpose_all(src, kt=KT):
                for t in range(T):
                    for g in range(kt // 4):
                        transposes([(i * P, (i + 1) * P, P, src[:, t, (4 * g + i) * P:(4 * g + i + 1) * P])
                                    for i in range(4)])

            pe.wait_ge(ones_ready, 1)
            pe.wait_ge(cb_ready, 1)
            cb = lambda k, t: silu_c[:, k, :]
            for j in range(4):
                dense(J_ADA1 + j, cb, 1, True)
            pe.wait_ge(const_loaded, 16 * len(CONST_0 + CONST_1))
            pe.wait_ge(xn_ready, 1)
            transpose_all(xn)
            pe.wait_ge(tp_evac, TP_H + 4)
            xTk = lambda k, t: xT[:, k, t * P:(t + 1) * P]
            for j in range(len(FOX_JOBS) + len(RW_JOBS)):
                dense(J_FOX + j, xTk)
            pe.wait_ge(logf_ready, 1)
            b = score_bank()
            pe.matmul(b[:, 0:8], cst["triu"][:, :], fs[:, 5, 0:8], start=True, stop=True)
            pe.matmul(b[:, 8:16], cst["triu"][:, :], fs[:, 5, 8:16], start=True, stop=False)
            pe.matmul(b[:, 8:16], ones_pp[:, :], fs[:, 5, 0:8], start=False, stop=True).then_inc(sc_mm, 1)
            for j in range(6):
                dense(J_GATE + j, cb, 1, True)
            pe.wait_ge(aug_ready, 1)
            for aug in (q_aug, k_aug):
                for hp in range(HEADS // 2):
                    transposes([((2 * i + t) * P, (2 * i + t + 1) * P, AUG, aug[:, t, 2 * hp + i, :])
                                for i in range(2) for t in range(T)])
            pe.wait_ge(tp_evac, TP_AUG + 8)

            def scores(h):
                b = score_bank()
                pe.matmul(b[:, 0:P], q_augT[:, h, 0:P], k_augT[:, h, 0:P], start=True, stop=True)
                pe.matmul(b[:, P:3 * P], q_augT[:, h, P:2 * P], k_augT[:, h, :], start=True, stop=True)\
                    .then_inc(sc_mm, 1)

            def attend(h):
                pe.wait_ge(prob_ready, h + 1)
                transposes([(i * P, (i + 1) * P, P, pr_sb[:, h % 2, i * P:(i + 1) * P]) for i in range(3)])
                pe.wait_ge(tp_evac, TP_PROB + h + 1)
                c = slice(h * HD, (h + 1) * HD)
                v = lambda t: z_fox[:, t, 1024 + h * HD:1024 + (h + 1) * HD]
                pe.matmul(bank[2][:, c], prT[:, h % 2, 0:P], v(0), start=True, stop=True)
                pe.matmul(bank[3][:, c], prT[:, h % 2, P:2 * P], v(0), start=True, stop=False)
                pe.matmul(bank[3][:, c], prT[:, h % 2, 2 * P:3 * P], v(1), start=False, stop=True)\
                    .then_inc(pv_mm, 1)

            scores(0)
            for h in range(HEADS):
                if h + 1 < HEADS:
                    scores(h + 1)
                attend(h)
            pe.wait_ge(rw_tanh, 1)
            for t in range(T):
                transposes([(0, P, P, z_rw[:, t, 1536:1664]), (P, 2 * P, P, z_rw[:, t, 1664:1792]),
                            (2 * P, 3 * P, GATE_R - P, z_rw[:, t, 1792:1824])])
            pe.wait_ge(par_loaded, 16 * 16)
            pe.wait_ge(tp_evac, TP_LORA + 2)
            for t in range(T):
                c = slice(t * P, (t + 1) * P)
                pe.matmul(score_bank()[:, :], loraT[0:HD, 0, c], lora_up[0:HD, :], start=True, stop=True)\
                    .then_inc(sc_mm, 1)
                pe.matmul(score_bank()[:, :], loraT[HD:P, 0, c], lora_up[HD:P, :], start=True, stop=True)\
                    .then_inc(sc_mm, 1)
                b = score_bank()
                pe.matmul(b[:, :], loraT[:, 1, c], gate_up[:, 0, :], start=True, stop=False)
                pe.matmul(b[:, :], loraT[0:GATE_R - P, 2, c], gate_up[0:GATE_R - P, 1, :], start=False, stop=True)\
                    .then_inc(sc_mm, 1)
            for t in range(T):
                pe.wait_ge(logw_ready, t + 1)
                pe.matmul(score_bank()[:, :], cst["mid"][:, :], logw[:, t, :], start=True, stop=True)\
                    .then_inc(sc_mm, 1)
            b = score_bank()
            for pair in range(4):
                c = slice(pair * P, (pair + 1) * P)
                pe.matmul(b[:, pair:pair + 1], logw[:, 0, c], cst["halves"][:, 0:1], start=True, stop=False)
                mm = pe.matmul(b[:, pair:pair + 1], logw[:, 1, c], cst["halves"][:, 1:2], start=False, stop=True)
            mm.then_inc(sc_mm, 1)
            for t in range(T):
                pe.wait_ge(til_ready, T)
                for pair in range(4):
                    transposes([(i * P, (i + 1) * P, P, til[:, i, t, pair * P:(pair + 1) * P]) for i in range(4)])
                pe.wait_ge(tp_evac, TP_TIL + 4 * t + 4)
                for h in range(HEADS):
                    lo = HD * (h % 2)
                    tt = lambda i, n=1: tilT[lo:lo + HD, h // 2, i:i + n, :]
                    b = score_bank()
                    pe.matmul(b[:, 0:P], tt(BT_), tt(AT_), start=True, stop=True)
                    pe.matmul(b[:, P:2 * P], tt(BT_), tt(RT_), start=True, stop=True)
                    pe.matmul(b[:, 2 * P:3 * P], tt(KTT_), tt(AT_), start=True, stop=True)
                    pe.matmul(b[:, 3 * P:4 * P], tt(KTT_), tt(RT_), start=True, stop=True).then_inc(sc_mm, 1)
                for g in range(2):
                    b = score_bank()
                    for i in range(4):
                        lo = HD * g
                        mm = pe.matmul(b[:, i * P:(i + 1) * P], tilT[lo:lo + HD, i, AT_, :],
                                       tilT[lo:lo + HD, i, BT_, :], start=True, stop=True)
                    mm.then_inc(sc_mm, 1)
                pe.wait_ge(lin_evac, after(J_ADA2 + 3))
                for level in range(LEVELS):
                    for g in range(2):
                        slots = range(4 * g, 4 * g + 4)
                        step = (LEVELS * t + level) * 2 + g
                        if level:
                            pe.wait_ge(wkv_upd, step - 1)
                            for i, h in enumerate(slots):
                                mm = pe.matmul(bank[6 + g][:, i * P:(i + 1) * P], gram[:, h, 0, :], inv[:, h, :],
                                               start=True, stop=True)
                            mm.then_inc(wkv_mm, 1)
                        pe.wait_ge(wkv_w, step + 1)
                        for i, h in enumerate(slots):
                            mm = pe.matmul(bank[4 + g][:, i * P:(i + 1) * P], amat[:, h, :], invT[:, h, :],
                                           start=True, stop=True)
                        if 0 < level < LEVELS - 1:
                            for i, h in enumerate(slots):
                                mm = pe.matmul(bank[g][:, i * P:(i + 1) * P], invT[:, h, :], amat[:, h, :],
                                               start=True, stop=True)
                        mm.then_inc(wkv_mm, 1)
                pe.wait_ge(wkv_upd, 2 * LEVELS * (t + 1))
                if t:
                    pe.wait_ge(state_ready, 1)
                V = lambda h: z_rw[:, t, 1024 + h * HD:1024 + (h + 1) * HD]

                def with_state(b, i):
                    if t == 0:
                        return
                    for pair in range(4):
                        pe.matmul(b[:, pair * P:(pair + 1) * P], tilT[:, pair, i, :], stateT[:, pair, :],
                                  start=(pair == 0), stop=False, skip_group_check=True)

                if t == 0:
                    pe.wait_ge(pv_evac, 1)
                else:
                    pe.wait_ge(u_evac, 3)
                with_state(bank[2], AT_)
                for h in range(HEADS):
                    c = slice(h * HD, (h + 1) * HD)
                    mm = pe.matmul(bank[2][:, c], gram[:, slot(h), 2, :], V(h), start=(t == 0), stop=True,
                                   skip_group_check=True)
                mm.then_inc(u_mm, 1)
                pe.wait_ge(u_evac, 3 * t + 1)
                for h in range(HEADS):
                    c = slice(h * HD, (h + 1) * HD)
                    mm = pe.matmul(bank[3][:, c], invT[:, slot(h), :], rhs_u[:, 0, c], start=True, stop=True)
                mm.then_inc(u_mm, 1)
                pe.wait_ge(u_evac, 3 * t + 2)
                with_state(bank[2], RT_)
                for h in range(HEADS):
                    c = slice(h * HD, (h + 1) * HD)
                    pe.matmul(bank[2][:, c], gram[:, slot(h), 1, :], rhs_u[:, 1, c], start=(t == 0), stop=False,
                              skip_group_check=True)
                    mm = pe.matmul(bank[2][:, c], gram[:, slot(h), 3, :], V(h), start=False, stop=True,
                                   skip_group_check=True)
                mm.then_inc(u_mm, 1)
                if t == 0:
                    b = score_bank()
                    for pair in range(4):
                        c = slice(pair * P, (pair + 1) * P)
                        pe.matmul(b[:, c], til[:, BT_, 0, c], rhs_u[:, 1, c], start=True, stop=False)
                        mm = pe.matmul(b[:, c], til[:, KTT_, 0, c], z_rw[:, 0, 1024 + pair * P:1024 + (pair + 1) * P],
                                       start=False, stop=True)
                    mm.then_inc(sc_mm, 1)
            pe.wait_ge(y_ready, 1)
            transpose_all(xn)
            pe.wait_ge(tp_evac, TP_Y + 4)
            for j in range(2):
                dense(J_OUT + j, xTk)
            pe.sem_inc(mixer_read, 1)
            for j in range(2):
                dense(J_GATE2 + j, cb, 1, True)
            pe.wait_ge(xn_ready, 2)
            transpose_all(xn)
            pe.wait_ge(tp_evac, TP_H2 + 4)
            pe.wait_ge(router_loaded, 48)
            b = score_bank()
            for t in range(T):
                for k in range(KT):
                    mm = pe.matmul(b[:, t * EXPERTS:(t + 1) * EXPERTS], xTk(k, t), router_w[:, k, :],
                                   start=(k == 0), stop=(k == KT - 1))
            mm.then_inc(sc_mm, 1)
            pe.wait_ge(lin_evac, after(J_GATE2 + 1))
            pe.wait_ge(sc_evac, SC_ROUTER + 1)

            pe.wait_ge(sh_full, 48)
            for t in range(T):
                for k in range(KT):
                    mm = pe.matmul(bank[4 + t][:, :], xTk(k, t), gu_odd[:, 0, k * BANK:(k + 1) * BANK],
                                   start=(k == 0), stop=(k == KT - 1))
                mm.then_inc(gu_mm, 1)

            mask = rt[:, 2, :, :]
            pe.wait_ge(routed, 1)
            b = score_bank()
            for t in range(T):
                pe.matmul(b[0:EXPERTS, t * P:(t + 1) * P], mask[:, t, :], cst["ident"][:, :], start=True, stop=True)
            pe.matmul(b[0:EXPERTS, 2 * P:3 * P], mask[:, 0, :], cst["triu"][:, :], start=True, stop=True)
            pe.matmul(b[0:EXPERTS, 3 * P:4 * P], mask[:, 1, :], cst["triu"][:, :], start=True, stop=False)
            pe.matmul(b[0:EXPERTS, 3 * P:4 * P], mask[:, 0, :], ones_pp[:, :], start=False, stop=True).then_inc(sc_mm, 1)
            b = score_bank()
            for t in range(T):
                mm = pe.transpose(b[0:EXPERTS, t * P:(t + 1) * P], wts[:, t, :], cst["ident"][:, :])
            mm.then_inc(sc_mm, 1)
            pe.wait_ge(routed, 2)
            b = score_bank()
            pe.matmul(b[0:EXPERTS, 0:1], cst["triu"][0:EXPERTS, 0:EXPERTS], rc[0:EXPERTS, 0:1], start=True, stop=True)
            pe.matmul(b[:, 1:2], ones_pp[0:EXPERTS, :], rc[0:EXPERTS, 0:1], start=True, stop=True).then_inc(sc_mm, 1)
            pe.wait_ge(routed, 3)
            b = score_bank()
            for t in range(T):
                tok = slice(t * P, (t + 1) * P)
                c = slice(t * NC, (t + 1) * NC)
                pe.matmul(b[:, c], rankT[:, tok], of_chunk[:, 0, :], start=True, stop=False)
                pe.matmul(b[:, c], ones_pp[0:EXPERTS, :], of_chunk[:, 1, :], start=False, stop=True)
                c = slice((2 + t) * NC, (3 + t) * NC)
                pe.matmul(b[:, c], wtsT[:, tok], of_chunk[:, 0, :], start=True, stop=True)
            pe.matmul(b[0:1, 4 * NC:5 * NC], expert_no, of_chunk[:, 0, :], start=True, stop=True).then_inc(sc_mm, 1)
            pe.wait_ge(sc_evac, SC_ROUTE + 4)

            for t in range(T):
                pe.wait_ge(act_made, t + 1)
                for i in range(D_E // P):
                    mm = pe.transpose(bank[6 + t][:, i * P:(i + 1) * P], act_e[:, t, i * P:(i + 1) * P],
                                      cst["ident"][:, :])
                mm.then_inc(actT_mm, 1)
            for t in range(T):
                pe.wait_ge(actT_copied, t + 1)
                for h in range(2):
                    for k in range(D_E // P):
                        lo = k * D + h * BANK
                        mm = pe.matmul(bank[2 * t + h][:, :], act_eT[:, t, k, :], dn[:, 2, lo:lo + BANK],
                                       start=(k == 0), stop=False, skip_group_check=True)
                mm.then_inc(spread_mm, 1)

            CHUNKS = (slice(0, CS), slice(CS, 2 * CS))

            def gather(p, parity):
                pe.wait_ge(pick_ready, p * 8 + 8)
                pe.wait_ge(y_copied, p * 2 + 2)
                for k in range(KT):
                    for t in range(T):
                        mm = pe.matmul(bank[6 + k // 4][:, k % 4 * P:(k % 4 + 1) * P], xn[:, t, k * P:(k + 1) * P],
                                       pick[:, parity, t, :], start=(t == 0), stop=(t == T - 1))
                    if k % 4 == 3:
                        mm.then_inc(gather_mm, 1)

            def put_transpose(p, parity):
                pe.wait_ge(actT_copied, p + 2)
                for t in range(T):
                    mm = pe.transpose(bank[5][:, (2 + t) * P:(3 + t) * P], put[:, parity, t, :], cst["ident"][:, :])
                mm.then_inc(put_mm, 1)

            def spread(p, parity, last=False):
                pe.wait_ge(y_copied, p * 2 + 4)
                pe.wait_ge(put_copied, p + 1)
                for t in range(T):
                    for h in range(2):
                        mm = pe.matmul(bank[2 * t + h][:, :], putT[:, 1 - parity, t, :],
                                       y_sb[:, h * BANK:(h + 1) * BANK], start=False, stop=last,
                                       skip_group_check=True)
                return mm

            gather(0, 0)
            put_transpose(0, 0)
            quads = pe.value_load(quads_i[0:1, 0:1], min_val=1, max_val=MAX_QUADS)
            with pe.Fori(0, quads) as i:
                for parity in range(2):
                    p = i * 2 + parity
                    gu_w = (lambda c: ring[:, c, 0:GU_W]) if parity == 0 else (lambda c: gu_odd[:, c, :])
                    pe.wait_ge(gather_copied, p * 2 + 2)
                    pe.wait_ge(act_made, p + 2)
                    pe.wait_ge(gu_full[parity], i * 64 + 64)
                    for k in range(KT):
                        for c in range(2):
                            mm = pe.matmul(bank[4][CHUNKS[c], :], hgT[:, k, CHUNKS[c]],
                                           gu_w(c)[:, k * BANK:(k + 1) * BANK], start=(k == 0), stop=(k == KT - 1))
                    mm.then_inc(gu_mm, 1)
                    gather(p + 1, 1 - parity)
                    pe.wait_ge(put_copied, p + 1)
                    pe.wait_ge(act_made, p + 3)
                    for k in range(D_E // P):
                        mm = pe.transpose(bank[5][:, k * P:(k + 1) * P], act_e[:, 0, k * P:(k + 1) * P],
                                          cst["ident"][:, :])
                    mm.then_inc(actT_mm, 1)
                    spread(p, parity).then_inc(spread_mm, 1)
                    pe.wait_ge(dn_full[parity], i * 32 + 32)
                    pe.wait_ge(actT_copied, p + 3)
                    for h in range(2):
                        pe.wait_ge(gather_copied, p * 2 + 3 + h)
                        for k in range(D_E // P):
                            for c in range(2):
                                lo = k * D + h * BANK
                                mm = pe.matmul(bank[6 + h][CHUNKS[c], :], act_eT[:, 0, k, CHUNKS[c]],
                                               dn[:, 2 * parity + c, lo:lo + BANK], start=(k == 0),
                                               stop=(k == D_E // P - 1))
                        mm.then_inc(down_mm, 1)
                    put_transpose(p + 1, 1 - parity)
            spread(quads * 2, 0, last=True).then_inc(experts_added, 1)
            pe.wait_ge(experts_copied, 1)
            pe.wait_ge(p2_loaded, 16 * N_P2)
            pe.wait_ge(router_sig, 1)
            pe.wait_ge(x2_ready, 1)
            pe.matmul(bank[2][0:GH, 0:3 * P], rel[:, :], cst["bucket"][:, :], start=True, stop=True).then_inc(rel_mm, 1)
            pe.wait_ge(xn_ready, 3)
            transpose_all(xn)
            pe.wait_ge(tp_evac, TP_IN2 + 4)
            for j in range(N_IN2):
                dense(J_IN2 + j, xTk, bias=True)
            pe.wait_ge(ml_logf, 1)
            b = score_bank()
            pe.matmul(b[:, 0:GH], cst["triu"][:, :], ms[:, 3, 0:GH], start=True, stop=True)
            pe.matmul(b[:, GH:2 * GH], cst["triu"][:, :], ms[:, 3, GH:2 * GH], start=True, stop=False)
            pe.matmul(b[:, GH:2 * GH], ones_pp[:, :], ms[:, 3, 0:GH], start=False, stop=True).then_inc(sc_mm, 1)
            pe.wait_ge(e_ready, 1)
            transposes([(t * P, (t + 1) * P, GH, ms[:, 5, t * GH:(t + 1) * GH]) for t in range(T)])

            def pair_transposes(lo):
                transposes([((2 * pair + t) * P, (2 * pair + t + 1) * P, P, z2[:, t, lo + pair * P:lo + (pair + 1) * P])
                            for pair in range(2) for t in range(T)])

            pair_transposes(M_Q)
            pair_transposes(M_K)
            pe.wait_ge(m_row, 1)
            n = tp_n[0]
            tp_n[0] += 1
            pe.wait_ge(tp_evac, n - 1)
            for t in range(T):
                mm = pe.transpose(bank[4 + n % 2][:, t * GH:(t + 1) * GH], e_row[0:GH, 1, t * P:(t + 1) * P],
                                  cst["ident"][0:GH, 0:GH])
            mm.then_inc(tp_mm, 1)
            pe.wait_ge(tp_evac, TP_ML + 3)

            def head_of(a, h, lo=0, hi=T * P):
                return a[HD * (h % 2):HD * (h % 2) + HD, h // 2, lo:hi]

            def weights(h):
                pe.matmul(score_bank()[:, 0:2 * P], cst["neg_head"][:, h * P:(h + 1) * P], e_row[0:GH, 1, :],
                          start=True, stop=True).then_inc(sc_mm, 1)
                b = score_bank()
                pe.matmul(b[:, 0:2 * P], head_of(kT2, h, 0, P), head_of(qT2, h), start=True, stop=True)
                pe.matmul(b[:, 2 * P:3 * P], head_of(kT2, h, P, 2 * P), head_of(qT2, h, P, 2 * P),
                          start=True, stop=True).then_inc(sc_mm, 1)

            def weighted(h):
                pe.wait_ge(w_ready, h + 1)
                c = slice(h * (HD + 1), (h + 1) * (HD + 1))
                w = lambda i: wT2[:, h % 2, i * P:(i + 1) * P]
                pe.matmul(bank[2][:, c], w(0), v_aug[:, 0, h, :], start=True, stop=True)
                pe.matmul(bank[3][:, c], w(1), v_aug[:, 0, h, :], start=True, stop=False)
                pe.matmul(bank[3][:, c], w(2), v_aug[:, 1, h, :], start=False, stop=True).then_inc(o_mm, 1)

            pe.wait_ge(hankel_made, 1)
            weights(0)
            for h in range(GH):
                if h + 1 < GH:
                    weights(h + 1)
                weighted(h)
            pe.wait_ge(qk_ready, 1)
            pair_transposes(A_Q)
            pair_transposes(A_K)
            pe.wait_ge(rel_copied, 16 * GH)
            pe.wait_ge(tp_evac, TP_MOBA + 2)

            def moba_scores(h):
                b = score_bank()
                pe.matmul(b[:, 0:P], head_of(qT2, h, 0, P), head_of(kT2, h, 0, P), start=True, stop=False)
                pe.matmul(b[:, 0:P], cst["anti"][:, :], hankel[:, h, P:2 * P], start=False, stop=True)
                pe.matmul(b[:, P:3 * P], head_of(qT2, h, P, 2 * P), head_of(kT2, h), start=True, stop=False)
                pe.matmul(b[:, P:3 * P], cst["anti"][:, :], hankel[:, h, :], start=False, stop=True).then_inc(sc_mm, 1)

            def moba_attend(h):
                pe.wait_ge(w_exp, GH + h + 1)
                transposes([(i * P, (i + 1) * P, P, pr2[:, h % 2, i * P:(i + 1) * P]) for i in range(3)])
                pe.wait_ge(tp_evac, TP_P2 + h + 1)
                c = slice(h * HD, (h + 1) * HD)
                v = lambda t: z2[:, t, A_V + h * HD:A_V + (h + 1) * HD]
                w = lambda i: wT2[:, h % 2, i * P:(i + 1) * P]
                pe.matmul(bank[2][:, c], w(0), v(0), start=True, stop=True)
                pe.matmul(bank[3][:, c], w(1), v(0), start=True, stop=False)
                pe.matmul(bank[3][:, c], w(2), v(1), start=False, stop=True).then_inc(o_mm, 1)

            moba_scores(0)
            pe.wait_ge(o_used, 1)
            for h in range(GH):
                if h + 1 < GH:
                    moba_scores(h + 1)
                moba_attend(h)
            pe.wait_ge(hg_act, 3)
            for level in range(LEVELS + 1):
                b = score_bank()
                if level < LEVELS:
                    span = cst["span"][:, level * P:(level + 1) * P]
                    spans = (span, span)
                else:
                    spans = (cst["tril_strict"][:, :], cst["triu"][:, :])
                for t in range(T):
                    mm = pe.matmul(b[:, t * GW:(t + 1) * GW], spans[t], hg[:, LF, t, :], start=True, stop=True)
                mm.then_inc(sc_mm, 1)
                pe.wait_ge(ft_src, level + 1)
                transposes([((2 * pair + t) * P, (2 * pair + t + 1) * P, P, hg[:, HS, t, pair * P:(pair + 1) * P])
                            for pair in range(2) for t in range(T)])
                pe.wait_ge(tp_evac, TP_HG + level + 1)
                for parity in range(2):
                    b = score_bank()
                    r = slice(HD * parity, HD * parity + HD)
                    for pair in range(2):
                        if level < LEVELS:
                            for t in range(T):
                                i = 2 * pair + t
                                f = fT[r, pair, t * P:(t + 1) * P]
                                mm = pe.matmul(b[:, i * P:(i + 1) * P], f, f, start=True, stop=True)
                        else:
                            mm = pe.matmul(b[:, pair * P:(pair + 1) * P], fT[r, pair, 0:P], fT[r, pair, P:2 * P],
                                           start=True, stop=True)
                    mm.then_inc(sc_mm, 1)
            pe.wait_ge(sc_evac, SC_HG + 3 * (LEVELS + 1))
            pe.wait_ge(o_used, 2)
            for h in range(GH):
                c = slice(h * HD, (h + 1) * HD)
                v = lambda t: z2[:, t, H_I + h * HD:H_I + (h + 1) * HD]
                a = lambda t: at[:, h % 2, 2 * (h // 2) + t, :]
                pe.matmul(bank[2][:, c], a(0), v(0), start=True, stop=True)
                pe.matmul(bank[3][:, c], atx[:, h % 2, h // 2, :], v(0), start=True, stop=False)
                mm = pe.matmul(bank[3][:, c], a(1), v(1), start=False, stop=True)
            mm.then_inc(o_mm, 1)
            pe.wait_ge(y_ready, 2)
            transpose_all(xn)
            pe.wait_ge(tp_evac, TP_Y2 + 4)
            for j in range(2):
                dense(J_MIX + j, xTk)
            pe.wait_ge(xn_ready, 4)
            transpose_all(mem)
            pe.wait_ge(tp_evac, TP_MEM + 4)

            def dense_T(j, src):
                full[j % RING] += 16 * len(jobs[j][4])
                pe.wait_ge(w_full[j % RING], full[j % RING])
                for i in range(2):
                    o = outputs[(j, i)]
                    pe.wait_ge(lin_evac, o - 1)
                    for h in range(2):
                        for k in range(KT):
                            lo = k * CW + (2 * i + h) * CHD
                            mm = pe.matmul(bank[o % 2][:, h * 2 * P:(h + 1) * 2 * P],
                                           ring[:, j % RING, lo:lo + CHD], src[:, k, :],
                                           start=(k == 0), stop=(k == KT - 1))
                    mm.then_inc(lin_mm, 1)
                pe.wait_ge(lin_mm, outputs[(j, 1)] + 1)
                pe.sem_inc(w_used, 1)

            dense_T(J_CK, memT)
            dense(J_CV, lambda k, t: memT[:, k, t * P:(t + 1) * P])
            pe.wait_ge(xn_ready, 5)
            transpose_all(xn)
            pe.wait_ge(tp_evac, TP_XN + 4)
            dense_T(J_CQ, xT)
            pe.wait_ge(lin_evac, after(J_CQ, 1))

            def cross_scores(h):
                b = score_bank()
                for t in range(T):
                    mm = pe.matmul(b[:, t * 2 * P:(t + 1) * 2 * P], cqT[:, h, t * P:(t + 1) * P], ckT[:, h, :],
                                   start=True, stop=True)
                mm.then_inc(sc_mm, 1)

            cross_scores(0)
            for h in range(CH):
                if h + 1 < CH:
                    cross_scores(h + 1)
                pe.wait_ge(w_exp, 2 * GH + h + 1)
                transposes([((2 * t + m) * P, (2 * t + m + 1) * P, P, prx[:, h % 2, t, m * P:(m + 1) * P])
                            for t in range(T) for m in range(2)])
                pe.wait_ge(tp_evac, TP_PX + h + 1)
                for t in range(T):
                    for m in range(2):
                        mm = pe.matmul(bank[2 + t][:, h * CHD:(h + 1) * CHD],
                                       prxT[:, h % 2, (2 * t + m) * P:(2 * t + m + 1) * P],
                                       cv[:, m, h * CHD:(h + 1) * CHD], start=(m == 0), stop=(m == 1))
                mm.then_inc(o_mm, 1)
            pe.wait_ge(y_ready, 3)
            transpose_all(xn, CW // P)
            pe.wait_ge(tp_evac, TP_O + 2)
            full[J_CO % RING] += 16
            pe.wait_ge(w_full[J_CO % RING], full[J_CO % RING])
            for t in range(T):
                for h in range(2):
                    o = outputs[(J_CO, 2 * t + h)]
                    pe.wait_ge(lin_evac, o - 1)
                    for k in range(CW // P):
                        lo = k * D + h * BANK
                        mm = pe.matmul(bank[o % 2][:, :], xTk(k, t), ring[:, J_CO % RING, lo:lo + BANK],
                                       start=(k == 0), stop=(k == CW // P - 1))
                    mm.then_inc(lin_mm, 1)
            pe.wait_ge(lin_mm, after(J_CO, 3))
            pe.sem_inc(w_used, 1)
            pe.wait_ge(xn_ready, 6)
            transpose_all(xn)
            pe.wait_ge(tp_evac, TP_FF + 4)
            for i in range(FF_JOBS):
                j = J_FFN + i
                full[j % RING] += 32
                pe.wait_ge(w_full[j % RING], full[j % RING])
                o = outputs[(j, 0)]
                pe.wait_ge(lin_evac, o - 1)
                for part in range(2):
                    b = bank[o % 2] if part == 0 else bank[6 + i % 2]
                    if part and i >= 2:
                        pe.wait_ge(act_ready, i - 1)
                    for half in range(2):
                        for k in range(KT):
                            lo = k * BANK + part * 256 + half * P
                            mm = pe.matmul(b[:, half * 2 * P:(half + 1) * 2 * P], ring[:, j % RING, lo:lo + P],
                                           xT[:, k, :], start=(k == 0), stop=(k == KT - 1))
                    mm.then_inc(up_mm if part else lin_mm, 1)
                pe.wait_ge(up_mm, i + 1)
                pe.sem_inc(w_used, 1)
            for i in range(0, FT_TILES, 4):
                j = J_FFO + i // 4
                n = min(4, FT_TILES - i)
                full[j % RING] += 16
                pe.wait_ge(w_full[j % RING], full[j % RING])
                pe.wait_ge(act_ready, min(FF_JOBS, (i + n + 1) // 2))
                for t in range(T):
                    for h in range(2):
                        for k in range(n):
                            lo = k * D + h * BANK
                            mm = pe.matmul(bank[2 + 2 * t + h][:, :], actT[:, i + k, t * P:(t + 1) * P],
                                           ring[:, j % RING, lo:lo + BANK], start=(i + k == 0),
                                           stop=(i + k == FT_TILES - 1), skip_group_check=True)
                        if i + n == FT_TILES:
                            mm.then_inc(ffn_mm, 1)
                if i + n < FT_TILES:
                    mm.then_inc(w_done, 1)
                    pe.wait_ge(w_done, i // 4 + 1)
                    pe.sem_inc(w_used, 1)

        @block.gpsimd
        def _(pool):
            n = [0]

            def link(ins):
                n[0] += 1
                ins.then_inc(pool_chain, 1)
                pool.wait_ge(pool_chain, n[0])

            pool.wait_ge(pad_zero, 1)
            pool.wait_ge(lin_evac, after(J_FOX + 1, 1))
            src = z_fox[:, :, 512:1536]
            pool.dma_start(kv_prev[1:P, :, :], src[0:P - 1, :, :]).then_inc(kv_shifted, 16)
            pool.dma_start(kv_prev[0:1, 1, :], src[P - 1:P, 0, :]).then_inc(kv_shifted, 16)
            pool.wait_ge(lin_evac, after(J_RW + 3, 1))
            pool.dma_start(z_prev[1:P, :, :], z_rw[0:P - 1, :, :]).then_inc(zr_shifted, 16)
            pool.dma_start(z_prev[0:1, 1, :], z_rw[P - 1:P, 0, :]).then_inc(zr_shifted, 16)
            pool.wait_ge(zr_shifted, 32)
            pool.wait_ge(par_loaded, 16 * 16)
            for t in range(T):
                link(pool.tensor_tensor(z_prev[:, t, :], z_prev[:, t, :], z_rw[:, t, :], ALU.subtract))
                link(pool.tensor_tensor(z_prev[:, t, :], z_prev[:, t, :], mu[:, :], ALU.mult))
                pool.tensor_tensor(z_rw[:, t, :], z_rw[:, t, :], z_prev[:, t, :], ALU.add).then_inc(lerp_done, 1)
            pool.wait_ge(conv_prod, 1)
            pool.dma_start(conv[1:P, 1, :, :], conv[0:P - 1, 0, :, :]).then_inc(conv_shift, 16)
            pool.dma_start(conv[0:1, 1, 1, :], conv[P - 1:P, 0, 0, :]).then_inc(conv_shift, 16)
            pool.dma_start(conv[2:P, 2, :, :], conv[0:P - 2, 0, :, :]).then_inc(conv_shift, 16)
            pool.dma_start(conv[0:2, 2, 1, :], conv[P - 2:P, 0, 0, :]).then_inc(conv_shift, 16)

        @block.vector
        def _(dve):
            chain = [0]

            def link(ins):
                chain[0] += 1
                ins.then_inc(vec_chain, 1)
                dve.wait_ge(vec_chain, chain[0])

            rstd_n = [0]

            def rsqrt_mean(src, dst, n, eps):
                link(dve.tensor_scalar(dst, src, 1.0 / n, eps, ALU.mult, ALU.add))
                dve.reciprocal(dst, dst).then_inc(inv_var, 1)
                rstd_n[0] += 1
                dve.wait_ge(rstd_done, rstd_n[0])

            tp_n = [0]

            def tp_copy(dst, rows, n, split=4):
                g = tp_n[0]
                tp_n[0] += 1
                dve.wait_ge(tp_mm, g + 1)
                src = bank[4 + g % 2][0:rows, 0:n]
                dve.tensor_copy(dst, src.rearrange("p (i c) -> p i c", i=split)).then_inc(tp_evac, 1)

            def untranspose(kt=KT):
                for t in range(T):
                    for g in range(kt // 4):
                        tp_copy(xT[:, 4 * g:4 * g + 4, t * P:(t + 1) * P], P, BANK)

            def heads(ap, n=HEADS):
                return ap.rearrange("p (h d) -> p h d", d=HD)

            def per_head(ap, n=HEADS):
                return ap.unsqueeze(2).broadcast_to([P, n, HD])

            dve.memset(ones_pp[:, :], 1.0)
            dve.memset(ones[:, :], 1.0).then_inc(ones_ready, 1)
            dve.memset(kv_prev[0:1, 0, :], 0.0)
            dve.memset(z_prev[0:1, 0, :], 0.0).then_inc(pad_zero, 1)
            dve.wait_ge(silu_done, 1)
            dve.tensor_copy(silu_c[:, :, :], small[:, KT:2 * KT].unsqueeze(2).broadcast_to([P, KT, P]))\
                .then_inc(cb_ready, 1)
            dve.wait_ge(x_loaded, 16)
            for t in range(T):
                link(dve.tensor_tensor_reduce(tmp[:, :], x[:, t, :], x[:, t, :], 1.0, 0.0, ALU.mult, ALU.add,
                                              small[:, 16 + t:17 + t]))
            rsqrt_mean(small[:, 16:18], small[:, 16:18], D, RMS_EPS)
            dve.wait_ge(gain_loaded[0], 16)
            dve.wait_ge(lin_evac, after(J_ADA1 + 3))
            link(dve.scalar_tensor_tensor(mod[:, SC, :], mod[:, SC, :], 1.0, gain[:, 0, :], ALU.add, ALU.mult))
            for t in range(T):
                link(dve.scalar_tensor_tensor(xn[:, t, :], x[:, t, :], small[:, 18 + t:19 + t], mod[:, SC, :],
                                              ALU.mult, ALU.mult))
                ins = dve.tensor_tensor(xn[:, t, :], xn[:, t, :], mod[:, SH, :], ALU.add)
                if t == 0:
                    link(ins)
                else:
                    link(ins)
            dve.sem_inc(xn_ready, 1)
            dve.sem_inc(mod_used, 1)
            untranspose()
            dve.wait_ge(par_loaded, 16 * 16)
            dve.wait_ge(lin_evac, after(J_FOX + 2, 1))
            for t in range(T):
                ins = dve.tensor_tensor(fs[:, 1, 8 * t:8 * t + 8], z_fox[:, t, 2048:2056], forget_b[:, :], ALU.add)
            ins.then_inc(fox_in, 1)
            dve.wait_ge(fox_gates, 1)
            dve.wait_ge(kv_shifted, 32)
            for t in range(T):
                kv = z_fox[:, t, 512:1536]
                prev = kv_prev[:, t, :]
                link(dve.tensor_tensor(prev, prev, kv, ALU.subtract))
                link(dve.tensor_tensor(heads(prev), heads(prev), per_head(fs[:, 0, 16 * t:16 * t + 16], 16), ALU.mult))
                link(dve.tensor_tensor(kv, kv, prev, ALU.add))
            dve.wait_ge(fox_ln, 1)
            link(dve.tensor_scalar(fs[:, 1, 0:16], fs[:, 1, 0:16], 0.0, None, ALU.min))
            dve.tensor_tensor(fs[:, 5, 0:16], fs[:, 1, 0:16], fs[:, 4, 0:16], ALU.subtract).then_inc(logf_ready, 1)
            dve.wait_ge(lin_evac, after(J_FOX + 3, 1))
            dve.wait_ge(sc_mm, SC_CUMF + 1)
            link(dve.tensor_copy(fs[:, 1, 0:16], bank[6][:, 0:16]))
            dve.sem_inc(sc_evac, 1)
            for t in range(T):
                qk = z_fox[:, t, 0:1024]
                link(dve.tensor_tensor(kv_prev[:, t, :], qk, qk, ALU.mult))
                link(dve.tensor_reduce(fs[:, 5 + 2 * t, 0:16], heads(kv_prev[:, t, :]), AX.X, ALU.add))
                link(dve.tensor_scalar(fs[:, 5 + 2 * t, 0:16], fs[:, 5 + 2 * t, 0:16], 1.0 / HD, RMS_EPS, ALU.mult, ALU.add))
                rstd_n[0] += 1
                dve.reciprocal(fs[:, 5 + 2 * t, :][:, 0:16], fs[:, 5 + 2 * t, 0:16]).then_inc(inv_var, 1)
            dve.wait_ge(rstd_done, rstd_n[0])
            for t in range(T):
                qk = z_fox[:, t, 0:1024]
                link(dve.tensor_tensor(heads(qk), heads(qk), per_head(fs[:, 6 + 2 * t, 0:16], 16), ALU.mult))
                link(dve.scalar_tensor_tensor(q_aug[:, t, :, 0:HD], heads(z_fox[:, t, 0:W1]), HD ** -0.5,
                                              heads(fxp[:, 0, :]), ALU.mult, ALU.mult))
                link(dve.tensor_tensor(k_aug[:, t, :, 0:HD], heads(z_fox[:, t, W1:2 * W1]), heads(fxp[:, 1, :]), ALU.mult))
                cum = fs[:, 1, 8 * t:8 * t + 8].unsqueeze(2)
                link(dve.tensor_copy(q_aug[:, t, :, HD:HD + 1], cum))
                link(dve.memset(q_aug[:, t, :, HD + 1:HD + 2], 1.0))
                link(dve.memset(k_aug[:, t, :, HD:HD + 1], 1.0))
                link(dve.tensor_scalar(k_aug[:, t, :, HD + 1:HD + 2], cum, -1.0, None, ALU.mult))
            dve.sem_inc(aug_ready, 1)
            dve.wait_ge(lerp_done, 2)
            for dst in (q_augT, k_augT):
                for hp in range(HEADS // 2):
                    g = tp_n[0]
                    tp_n[0] += 1
                    dve.wait_ge(tp_mm, g + 1)
                    dve.tensor_copy(dst[:, 2 * hp:2 * hp + 2, :],
                                    bank[4 + g % 2][0:AUG, :].rearrange("p (h c) -> p h c", h=2)).then_inc(tp_evac, 1)

            def prob_copy(h):
                g = tp_n[0]
                tp_n[0] += 1
                dve.wait_ge(tp_mm, g + 1)
                if h >= 2:
                    dve.wait_ge(pv_mm, h - 1)
                dve.tensor_copy(prT[:, h % 2, :], bank[4 + g % 2][:, 0:3 * P]).then_inc(tp_evac, 1)

            for h in range(HEADS):
                n = SC_FOX + h
                dve.wait_ge(sc_mm, n + 1)
                if h >= 2:
                    dve.wait_ge(prob_ready, h - 1)
                dve.tensor_tensor(sc_sb[:, h % 2, :], bank[6 + n % 2][:, 0:3 * P], cst["causal"][:, :], ALU.add)\
                    .then_inc(sc_evac, 1)
                dve.wait_ge(sc_evac, n + 1)
                dve.tensor_reduce(fs[:, 9, 2 * h:2 * h + 1], sc_sb[:, h % 2, 0:P], AX.X, ALU.max, negate=True)
                dve.tensor_reduce(fs[:, 9, 2 * h + 1:2 * h + 2], sc_sb[:, h % 2, P:3 * P], AX.X, ALU.max, negate=True)\
                    .then_inc(negmax_ready, 1)
                if h:
                    prob_copy(h - 1)
            prob_copy(HEADS - 1)
            dve.wait_ge(prob_ready, HEADS)
            link(dve.reciprocal(fs[:, 11, 0:16], fs[:, 10, 0:16]))
            dve.wait_ge(pv_mm, HEADS)
            dve.wait_ge(fox_sig, 1)
            inv_sum = fs[:, 11, 0:16].rearrange("p (h t) -> p t h", t=T)
            for t in range(T):
                o = xn[:, t, 0:W1]
                link(dve.tensor_tensor(heads(o), heads(bank[2 + t][:, :]), per_head(inv_sum[:, t, :]), ALU.mult))
                link(dve.tensor_tensor(kv_prev[:, t, 0:W1], o, o, ALU.mult))
                link(dve.tensor_reduce(fs[:, 5, 8 * t:8 * t + 8], heads(kv_prev[:, t, 0:W1]), AX.X, ALU.add))
            dve.sem_inc(pv_evac, 1)
            rsqrt_mean(fs[:, 5, 0:16], fs[:, 5, 0:16], HD, RMS_EPS)
            for t in range(T):
                o = xn[:, t, 0:W1]
                link(dve.tensor_tensor(heads(o), heads(o), per_head(fs[:, 6, 8 * t:8 * t + 8]), ALU.mult))
                link(dve.tensor_tensor(o, o, fxp[:, 2, :], ALU.mult))
                link(dve.tensor_tensor(o, o, z_fox[:, t, 1536:2048], ALU.mult))
            for t in range(T):
                g = tp_n[0]
                tp_n[0] += 1
                dve.wait_ge(tp_mm, g + 1)
                dve.tensor_copy(loraT[:, 0:2, t * P:(t + 1) * P],
                                bank[4 + g % 2][:, 0:2 * P].rearrange("p (i c) -> p i c", i=2))
                dve.tensor_copy(loraT[0:GATE_R - P, 2, t * P:(t + 1) * P], bank[4 + g % 2][0:GATE_R - P, 2 * P:3 * P])\
                    .then_inc(tp_evac, 1)
            for t in range(T):
                n = SC_LORA + 3 * t
                b = lambda i: bank[6 + (n + i) % 2][:, :]
                dve.wait_ge(sc_mm, n + 1)
                link(dve.tensor_tensor(logw[:, t, :], b(0), rwp[:, W0, :], ALU.add))
                dve.sem_inc(sc_evac, 1)
                dve.sem_inc(lora_in, 1)
                dve.wait_ge(sc_mm, n + 2)
                link(dve.tensor_tensor(iclr[:, t, :], b(1), rwp[:, A0, :], ALU.add))
                dve.sem_inc(sc_evac, 1)
                dve.sem_inc(lora_in, 1)
                dve.wait_ge(sc_mm, n + 3)
                dve.tensor_copy(gate[:, t, :], b(2)).then_inc(sc_evac, 1)
            dve.wait_ge(lerp_done, 2)
            R = lambda t: z_rw[:, t, 0:W1]
            K = lambda t: z_rw[:, t, W1:2 * W1]
            for t in range(T):
                link(dve.tensor_tensor(til[:, AT_, t, :], K(t), rwp[:, KK_, :], ALU.mult))
                link(dve.tensor_tensor(til[:, RT_, t, :], til[:, AT_, t, :], til[:, AT_, t, :], ALU.mult))
                link(dve.tensor_reduce(ws[:, 0, 8 * t:8 * t + 8], heads(til[:, RT_, t, :]), AX.X, ALU.add))
            link(dve.tensor_scalar(ws[:, 0, :], ws[:, 0, :], 1e-24, None, ALU.max))
            dve.reciprocal(ws[:, 0, :], ws[:, 0, :]).then_inc(inv_var, 1)
            rstd_n[0] += 1
            dve.wait_ge(rstd_done, rstd_n[0])
            for t in range(T):
                dve.wait_ge(rw_sig, 2 * t + 1)
                link(dve.tensor_scalar(logw[:, t, :], logw[:, t, :], -math.exp(-0.5), None, ALU.mult))
                dve.sem_inc(logw_ready, 1)
            for t in range(T):
                dve.wait_ge(rw_sig, 2 * t + 2)
                kk = til[:, AT_, t, :]
                link(dve.scalar_tensor_tensor(heads(kk), heads(kk), -1.0, per_head(ws[:, 1, 8 * t:8 * t + 8]),
                                              ALU.mult, ALU.mult))
                link(dve.scalar_tensor_tensor(til[:, BT_, t, :], kk, -1.0, iclr[:, t, :], ALU.mult, ALU.mult))
                link(dve.scalar_tensor_tensor(iclr[:, t, :], iclr[:, t, :], -1.0, rwp[:, KA_, :], ALU.add, ALU.mult))
                link(dve.scalar_tensor_tensor(K(t), iclr[:, t, :], 1.0, K(t), ALU.add, ALU.mult))
                link(dve.tensor_tensor(til[:, RT_, t, :], R(t), K(t), ALU.mult))
                link(dve.tensor_tensor(til[:, RT_, t, :], til[:, RT_, t, :], rwp[:, RK_, :], ALU.mult))
                link(dve.tensor_reduce(ws[:, 3, 8 * t:8 * t + 8], heads(til[:, RT_, t, :]), AX.X, ALU.add))
            for t in range(T):
                n = SC_CUM + t
                dve.wait_ge(rw_exp, 2 * t + 1)
                link(dve.tensor_tensor(y_rw[:, t, :], bank[6 + n % 2][:, :], logw[:, t, :], ALU.subtract))
                dve.sem_inc(logw_ready, 1)
                dve.sem_inc(sc_evac, 1)
                link(dve.tensor_tensor(til[:, RT_, t, :], R(t), rhs_u[:, 0, :], ALU.mult))
                link(dve.tensor_tensor(til[:, BT_, t, :], til[:, BT_, t, :], rhs_u[:, 1, :], ALU.mult))
                link(dve.tensor_tensor(til[:, KTT_, t, :], K(t), rhs_u[:, 1, :], ALU.mult))
                dve.wait_ge(rw_exp, 2 * t + 2)
                link(dve.tensor_tensor(til[:, AT_, t, :], til[:, AT_, t, :], y_rw[:, t, :], ALU.mult))
                dve.sem_inc(til_ready, 1)
            dve.wait_ge(rw_exp, 5)
            dve.sem_inc(sc_evac, 1)
            level_mask = lambda l: cst["level"][:, l * P:(l + 1) * P].unsqueeze(1).broadcast_to([P, 4, P])
            ident4 = cst["ident"][:, :].unsqueeze(1).broadcast_to([P, 4, P])
            four = lambda b: b[:, :].rearrange("p (i c) -> p i c", i=4)
            for t in range(T):
                for pair in range(4):
                    tp_copy(tilT[:, pair, :, :], P, BANK)
                base = SC_GRAM + 11 * t
                for h in range(HEADS):
                    n = base + h
                    dve.wait_ge(sc_mm, n + 1)
                    dve.tensor_tensor(gram[:, slot(h), :, :], four(bank[6 + n % 2]),
                                      cst["wkv_mask"][:, :].rearrange("p (i c) -> p i c", i=4), ALU.mult)\
                        .then_inc(sc_evac, 1)
                for level in range(LEVELS):
                    for g in range(2):
                        hs = slice(4 * g, 4 * g + 4)
                        if level == 0:
                            n = base + HEADS + g
                            dve.wait_ge(sc_mm, n + 1)
                            link(dve.tensor_tensor(amat[:, hs, :], four(bank[6 + n % 2]), level_mask(0), ALU.mult))
                            dve.sem_inc(sc_evac, 1)
                            link(dve.tensor_tensor(inv[:, hs, :], amat[:, hs, :], ident4, ALU.add))
                            link(dve.tensor_copy(invT[:, hs, :], ident4))
                            dve.sem_inc(wkv_w, 1)
                        else:
                            dve.wait_ge(wkv_mm, wkv_count(t, level, g, 0))
                            dve.tensor_tensor(amat[:, hs, :], four(bank[6 + g]), level_mask(level), ALU.mult)\
                                .then_inc(wkv_w, 1)
                    for g in range(2):
                        hs = slice(4 * g, 4 * g + 4)
                        dve.wait_ge(wkv_mm, wkv_count(t, level, g, 1))
                        ins = dve.tensor_tensor(invT[:, hs, :], invT[:, hs, :], four(bank[4 + g]), ALU.add)
                        if 0 < level < LEVELS - 1:
                            ins = dve.tensor_tensor(inv[:, hs, :], inv[:, hs, :], four(bank[g]), ALU.add)
                        link(ins)
                        dve.sem_inc(wkv_upd, 1)
                if t == 0:
                    n = base + HEADS + 2
                    dve.wait_ge(sc_mm, n + 1)
                    for pair in range(4):
                        link(dve.scalar_tensor_tensor(stateT[:, pair, :], bank[6 + n % 2][:, pair * P:(pair + 1) * P],
                                                      ws[:, 2, pair:pair + 1], cst["pairs"][:, :], ALU.mult, ALU.mult))
                    dve.sem_inc(sc_evac, 1)
                    dve.sem_inc(state_ready, 1)
            for t in range(T):
                dve.wait_ge(u_evac, 3 * t + 3)
                y = y_rw[:, t, :]
                link(dve.tensor_reduce(ws[:, 4, 8 * t:8 * t + 8], heads(y), AX.X, ALU.add))
                link(dve.tensor_scalar(ws[:, 4, 8 * t:8 * t + 8], ws[:, 4, 8 * t:8 * t + 8], 1.0 / HD, None, ALU.mult))
                link(dve.tensor_tensor(heads(y), heads(y), per_head(ws[:, 4, 8 * t:8 * t + 8]), ALU.subtract))
                link(dve.tensor_tensor(iclr[:, t, :], y, y, ALU.mult))
                link(dve.tensor_reduce(ws[:, 0, 8 * t:8 * t + 8], heads(iclr[:, t, :]), AX.X, ALU.add))
            rsqrt_mean(ws[:, 0, :], ws[:, 0, :], HD, LNX_EPS)
            for t in range(T):
                y = y_rw[:, t, :]
                link(dve.tensor_tensor(heads(y), heads(y), per_head(ws[:, 1, 8 * t:8 * t + 8]), ALU.mult))
                link(dve.tensor_tensor(y, y, rwp[:, LG, :], ALU.mult))
                link(dve.tensor_tensor(y, y, rwp[:, LB, :], ALU.add))
                link(dve.tensor_tensor(heads(iclr[:, t, :]), heads(z_rw[:, t, 1024:1536]),
                                       per_head(ws[:, 3, 8 * t:8 * t + 8]), ALU.mult))
                link(dve.tensor_tensor(y, y, iclr[:, t, :], ALU.add))
                link(dve.tensor_tensor(xn[:, t, W1:2 * W1], y, gate[:, t, :], ALU.mult))
            dve.sem_inc(y_ready, 1)
            link(dve.memset(rel[:, :], MASKED))
            dve.sem_inc(rel_made, 1)
            untranspose()
            for j in range(2):
                for t in range(T):
                    o = outputs[(J_OUT + j, t)]
                    c = slice(j * BANK, (j + 1) * BANK)
                    dve.wait_ge(lin_mm, o + 1)
                    dve.tensor_tensor(tmp[:, 0:BANK], bank[o % 2][:, :], mod[:, GT, c], ALU.mult).then_inc(lin_evac, 1)
                    dve.wait_ge(lin_evac, o + 1)
                    link(dve.tensor_tensor(x[:, t, c], x[:, t, c], tmp[:, 0:BANK], ALU.add))
                dve.sem_inc(x1_ready, 1)
            def sum_squares(dst, src):
                link(dve.tensor_tensor_reduce(tmp[:, :], src, src, 1.0, 0.0, ALU.mult, ALU.add, dst))

            for t in range(T):
                sum_squares(small[:, 16 + t:17 + t], x[:, t, :])
            rsqrt_mean(small[:, 16:18], small[:, 16:18], D, RMS_EPS)
            dve.wait_ge(gain_loaded[1], 16)
            link(dve.scalar_tensor_tensor(mod[:, SC, :], mod[:, SC, :], 1.0, gain[:, 1, :], ALU.add, ALU.mult))
            for t in range(T):
                link(dve.scalar_tensor_tensor(xn[:, t, :], x[:, t, :], small[:, 18 + t:19 + t], mod[:, SC, :],
                                              ALU.mult, ALU.mult))
                link(dve.tensor_tensor(xn[:, t, :], xn[:, t, :], mod[:, SH, :], ALU.add))
            dve.sem_inc(xn_ready, 1)
            untranspose()
            dve.wait_ge(router_loaded, 48)
            dve.wait_ge(router_sig, 1)
            dve.sem_inc(sc_evac, 1)
            best8, group, picked, eq, cum, masked = (rt[:, i, :, :] for i in range(6))

            def top(values, n, k, mask):
                for t in range(T):
                    dve.max(best8[:, t, 0:8], values[:, t, 0:n])
                link(dve.memset(cum[:, :, :], 1.0))
                for t in range(T):
                    v, least = values[:, t, 0:n], best8[:, t, k - 1:k]
                    link(dve.tensor_scalar(mask[:, t, 0:n], v, least, None, ALU.is_gt))
                    link(dve.tensor_reduce(best8[:, t, 8:9], mask[:, t, 0:n], AX.X, ALU.add))
                    link(dve.tensor_scalar(best8[:, t, 8:9], best8[:, t, 8:9], -1.0, float(k), ALU.mult, ALU.add))
                    link(dve.tensor_scalar(eq[:, t, 0:n], v, least, None, ALU.is_equal))
                    link(dve.tensor_tensor_scan(cum[:, t, 0:n], cum[:, t, 0:n], eq[:, t, 0:n], 0.0, ALU.mult, ALU.add))
                    link(dve.scalar_tensor_tensor(eq[:, t, 0:n], cum[:, t, 0:n], best8[:, t, 8:9], eq[:, t, 0:n],
                                                  ALU.is_le, ALU.mult))
                    link(dve.tensor_tensor(mask[:, t, 0:n], mask[:, t, 0:n], eq[:, t, 0:n], ALU.add))

            link(dve.tensor_tensor(sel[:, :, :], score[:, :, :], router_b[:, :].unsqueeze(1).broadcast_to([P, T, EXPERTS]),
                                   ALU.add))
            for t in range(T):
                for g in range(GROUPS):
                    c = slice(g * GROUP_SIZE, (g + 1) * GROUP_SIZE)
                    link(dve.max(picked[:, t, c], sel[:, t, c]))
            best = picked.rearrange("p t (g i) -> p t g i", i=GROUP_SIZE)
            link(dve.tensor_tensor(group[:, :, 0:GROUPS].unsqueeze(3), best[:, :, :, 0:1], best[:, :, :, 1:2], ALU.add))
            top(group, GROUPS, TOP_GROUPS, picked)
            for t in range(T):
                gmask = picked[:, t, 0:GROUPS]
                link(dve.tensor_scalar(group[:, t, 0:GROUPS], gmask, -MASKED, MASKED, ALU.mult, ALU.add))
                by_group = lambda a: a.rearrange("p (g i) -> p g i", i=GROUP_SIZE)
                wide = lambda a: a.unsqueeze(2).broadcast_to([P, GROUPS, GROUP_SIZE])
                link(dve.tensor_tensor(by_group(masked[:, t, :]), by_group(sel[:, t, :]), wide(gmask), ALU.mult))
                link(dve.tensor_tensor(by_group(masked[:, t, :]), by_group(masked[:, t, :]),
                                       wide(group[:, t, 0:GROUPS]), ALU.add))
            top(masked, EXPERTS, TOP_K, picked)
            for t in range(T):
                link(dve.tensor_tensor(wts[:, t, :], score[:, t, :], picked[:, t, :], ALU.mult))
                link(dve.tensor_reduce(best8[:, t, 9:10], wts[:, t, :], AX.X, ALU.add))
                link(dve.reciprocal(best8[:, t, 9:10], best8[:, t, 9:10]))
                link(dve.tensor_scalar(wts[:, t, :], wts[:, t, :], best8[:, t, 9:10], ROUTED_SCALE, ALU.mult, ALU.mult))

            dve.sem_inc(routed, 1)
            for t in range(T):
                dve.wait_ge(gate_act, t + 1)
                dve.tensor_tensor(act_e[:, t, :], silu_g[:, t, :], bank[4 + t][:, D_E:2 * D_E], ALU.mult)\
                    .then_inc(act_made, 1)
            n = SC_ROUTE
            dve.wait_ge(sc_mm, n + 1)
            ranks = bank[6 + n % 2]
            link(dve.tensor_copy(maskT[:, :], ranks[0:EXPERTS, 0:T * P]))
            link(dve.tensor_scalar(rc[0:EXPERTS, 4:4 + len(TH)], thresholds, ranks[0:EXPERTS, 4 * P - 1:4 * P], None,
                                   ALU.is_lt))
            link(dve.tensor_reduce(rc[0:EXPERTS, 0:1], rc[0:EXPERTS, 4:4 + len(TH)], AX.X, ALU.add))
            dve.sem_inc(routed, 1)
            link(dve.scalar_tensor_tensor(rankT[:, :], ranks[0:EXPERTS, T * P:2 * T * P], UNMATCHED, maskT[:, :],
                                          ALU.add, ALU.mult))
            link(dve.tensor_scalar(rankT[:, :], rankT[:, :], -UNMATCHED, None, ALU.add))
            dve.sem_inc(sc_evac, 1)
            dve.wait_ge(sc_mm, n + 2)
            link(dve.tensor_copy(wtsT[:, :], bank[6 + (n + 1) % 2][0:EXPERTS, 0:T * P]))
            dve.sem_inc(sc_evac, 1)
            dve.wait_ge(sc_mm, n + 3)
            link(dve.tensor_copy(rc[0:EXPERTS, 2:3], bank[6 + (n + 2) % 2][0:EXPERTS, 0:1]))
            link(dve.tensor_copy(rc[:, 3:4], bank[6 + (n + 2) % 2][:, 1:2]))
            dve.sem_inc(sc_evac, 1)
            link(dve.tensor_tensor(rc[0:EXPERTS, 1:2], rc[0:EXPERTS, 2:3], rc[0:EXPERTS, 0:1], ALU.subtract))
            mine, minus = of_chunk[:, 0, :], of_chunk[:, 1, :]
            link(dve.tensor_scalar(mine, chunk_no[0:EXPERTS, :], rc[0:EXPERTS, 1:2], None, ALU.is_ge))
            link(dve.scalar_tensor_tensor(mine, chunk_no[0:EXPERTS, :], rc[0:EXPERTS, 2:3], mine, ALU.is_lt, ALU.mult))
            link(dve.scalar_tensor_tensor(minus, chunk_no[0:EXPERTS, :], rc[0:EXPERTS, 1:2], mine, ALU.subtract,
                                          ALU.mult))
            link(dve.tensor_scalar(minus, minus, -float(CS), None, ALU.mult))
            dve.sem_inc(routed, 1)
            first_of_quad = chunk_no[:, 0:NC].rearrange("p (q c) -> p q c", c=4)[:, :, 0]
            link(dve.tensor_scalar(mod[:, SC, 0:NC // 4], first_of_quad, rc[:, 3:4], None, ALU.is_lt))
            link(dve.tensor_reduce(rc[:, 8:9], mod[:, SC, 0:NC // 4], AX.X, ALU.add))
            link(dve.tensor_copy(quads_i[:, :], rc[0:1, 8:9]))
            dve.wait_ge(sc_mm, n + 4)
            tables = bank[6 + (n + 3) % 2]
            link(dve.tensor_copy(expert_of[:, :], tables[0:1, 4 * NC:5 * NC]))
            link(dve.tensor_copy(place[:, :, :], tables[:, 0:2 * NC].rearrange("p (t c) -> p t c", t=T)))
            link(dve.tensor_copy(weight[:, :, :], tables[:, 2 * NC:4 * NC].rearrange("p (t c) -> p t c", t=T)))
            dve.sem_inc(sc_evac, 1)
            dve.sem_inc(quads_ready, 1)

            def make_pick(p, parity):
                for t in range(T):
                    for c in range(2):
                        at_chunk = bass.ds(p * 2 + c, 1)
                        dve.tensor_scalar(pick[:, parity, t, c * CS:(c + 1) * CS], slot_no, place[:, t, at_chunk],
                                          None, ALU.is_equal).then_inc(pick_ready, 1)
                        dve.tensor_scalar(put[:, parity, t, c * CS:(c + 1) * CS], slot_no, place[:, t, at_chunk],
                                          weight[:, t, at_chunk], ALU.is_equal, ALU.mult).then_inc(pick_ready, 1)

            link(dve.memset(y_sb, 0.0))
            link(dve.memset(putT[:, 1, :, :], 0.0))
            dve.sem_inc(y_copied, 4)
            make_pick(0, 0)
            make_pick(1, 1)
            quads = dve.value_load(quads_i[0:1, 0:1], min_val=1, max_val=MAX_QUADS)
            with dve.Fori(0, quads) as i:
                for parity in range(2):
                    p = i * 2 + parity
                    dve.wait_ge(gate_act, p + 3)
                    dve.wait_ge(actT_mm, p + 2)
                    dve.tensor_tensor(act_e[:, 0, :], silu_g[:, 0, :], bank[4][:, D_E:2 * D_E], ALU.mult)\
                        .then_inc(act_made, 1)
                    dve.wait_ge(put_mm, p + 1)
                    make_pick(p + 2, parity)
            dve.wait_ge(experts_added, 1)
            for t in range(T):
                for h in range(2):
                    c = slice(h * BANK, (h + 1) * BANK)
                    link(dve.tensor_tensor(tmp[:, c], bank[2 * t + h][:, :], mod[:, GT, c], ALU.mult))
                link(dve.tensor_tensor(x[:, t, :], x[:, t, :], tmp[:, :], ALU.add))
            dve.sem_inc(x2_ready, 1)

            FINAL, MIX_PRE, MIX_POST, MEM, CROSS_PRE, CROSS_POST, FFN_PRE, FFN_POST = range(8)

            def norm_into(dst, src, g):
                for t in range(T):
                    sum_squares(small[:, 16 + t:17 + t], src[:, t, :])
                rsqrt_mean(small[:, 16:18], small[:, 16:18], D, RMS_EPS)
                for t in range(T):
                    link(dve.scalar_tensor_tensor(dst[:, t, :], src[:, t, :], small[:, 18 + t:19 + t],
                                                  gain_of(g), ALU.mult, ALU.mult))

            def add_normed(src, g):
                norm_into(src, src, g)
                for t in range(T):
                    link(dve.tensor_tensor(x[:, t, :], x[:, t, :], src[:, t, :], ALU.add))

            dve.wait_ge(rel_mm, 1)
            link(dve.tensor_copy(rel_row[:, :], bank[2][0:GH, 0:3 * P]))
            dve.sem_inc(hankel_made, 1)
            dve.wait_ge(p2_loaded, 16 * N_P2)
            norm_into(x, x, FINAL)
            norm_into(xn, x, MIX_PRE)
            dve.sem_inc(xn_ready, 1)
            untranspose()
            col = lambda i: ms[:, i, :].rearrange("p (t h) -> p t h", t=T)
            link(dve.memset(conv[:, :, 0, :], 0.0))
            dve.wait_ge(ml_ln, 1)
            link(dve.tensor_scalar(col(3), z2[:, :, M_F:M_F + GH], 0.0, None, ALU.min))
            link(dve.tensor_tensor(ms[:, 3, :], ms[:, 3, :], ms[:, 2, :], ALU.subtract))
            dve.sem_inc(ml_logf, 1)
            dve.wait_ge(lin_evac, after(J_IN2 + C_H // BANK + (C_H % BANK + GW > BANK), 1))
            link(dve.tensor_tensor(conv[:, 0, :, :], z2[:, :, C_C:C_C + GW], z2[:, :, C_H:C_H + GW], ALU.mult))
            dve.sem_inc(conv_prod, 1)
            dve.wait_ge(sc_mm, SC_G2 + 1)
            link(dve.tensor_copy(ms[:, 4, :], bank[6 + SC_G2 % 2][:, 0:T * GH]))
            dve.sem_inc(sc_evac, 1)
            link(dve.tensor_tensor(col(5), z2[:, :, M_I:M_I + GH], col(4), ALU.subtract))
            dve.sem_inc(e_ready, 1)

            def next_tp():
                g = tp_n[0]
                tp_n[0] += 1
                dve.wait_ge(tp_mm, g + 1)
                return bank[4 + g % 2]

            def pair_copy(dst):
                dve.tensor_copy(dst[:, :, :], next_tp()[:, :].rearrange("p (i c) -> p i c", i=2)).then_inc(tp_evac, 1)

            link(dve.tensor_copy(e_row[:, 0, :], next_tp()[0:GH, 0:T * P]))
            dve.sem_inc(tp_evac, 1)
            link(dve.tensor_tensor_scan(e_row[:, 1, :], e_row[:, 0, :], e_row[:, 0, :], 0.0, ALU.max, ALU.max))
            dve.sem_inc(m_row, 1)
            pair_copy(qT2)
            pair_copy(kT2)
            link(dve.tensor_copy(ms[:, 6, :], next_tp()[:, 0:T * GH]))
            dve.sem_inc(tp_evac, 1)
            link(dve.tensor_tensor(ms[:, 7, :], ms[:, 6, :], ms[:, 4, :], ALU.add))
            dve.sem_inc(m_ready, 1)
            lb = rows2[:, 2, :]
            link(dve.tensor_tensor(lb, lb, lb, ALU.subtract))
            dve.sem_inc(f_ready, 1)
            for t in range(T):
                link(dve.tensor_copy(v_aug[:, t, :, 0:HD], z2[:, t, M_V:M_V + GW].rearrange("p (h d) -> p h d", d=HD)))
            link(dve.memset(v_aug[:, :, :, HD:HD + 1], 1.0))
            dve.wait_ge(hg_act, 2)
            link(dve.reciprocal(tmp[:, 0:GW], lb))
            link(dve.tensor_tensor(tmp[:, 0:GW], tmp[:, 0:GW], lb, ALU.mult))
            link(dve.tensor_tensor(lb, tmp[:, 0:GW], tmp[:, 0:GW], ALU.subtract))
            link(dve.tensor_scalar(tmp[:, 0:GW], lb, -1.0, 1.0, ALU.mult, ALU.add))
            both = lambda a: a.unsqueeze(1).broadcast_to([P, T, GW])
            f = hg[:, LF, :, :]
            link(dve.tensor_tensor(f, f, both(tmp[:, 0:GW]), ALU.mult))
            link(dve.tensor_tensor(f, f, both(lb), ALU.add))
            link(dve.tensor_scalar(hg[:, HK, :, :], f, -1.0, 1.0, ALU.mult, ALU.add))
            link(dve.tensor_scalar(f, f, TINY, None, ALU.max))
            dve.sem_inc(f_ready, 1)
            link(dve.tensor_tensor(hg[:, QK, :, :], hg[:, HQ, :, :], hg[:, HK, :, :], ALU.subtract))
            for h in range(GH):
                n = SC_ML + 2 * h
                dve.wait_ge(sc_mm, n + 1)
                if h >= 2:
                    dve.wait_ge(w_exp, h - 1)
                a = bank[6 + n % 2]
                dve.tensor_tensor(sc2[:, h % 2, 0:2 * P], a[:, 0:2 * P], cst["causal_t"][:, 0:2 * P], ALU.add)
                link(dve.tensor_tensor(sc2[:, h % 2, 2 * P:3 * P], a[:, P:2 * P], cst["causal_t"][:, 2 * P:3 * P], ALU.add))
                dve.sem_inc(sc_evac, 1)
                dve.sem_inc(d_ready, 1)
                dve.wait_ge(sc_mm, n + 2)
                dve.wait_ge(w_exp, h + 1)
                if h >= 2:
                    dve.wait_ge(o_mm, h - 1)
                link(dve.scalar_tensor_tensor(wT2[:, h % 2, :], bank[6 + (n + 1) % 2][:, 0:3 * P], HD ** -0.5,
                                              pr2[:, h % 2, :], ALU.mult, ALU.mult))
                dve.sem_inc(sc_evac, 1)
                dve.sem_inc(w_ready, 1)
            heads4 = lambda a: a.rearrange("p (h d) -> p h d", d=HD)
            wide4 = lambda a: a.unsqueeze(2).broadcast_to([P, GH, HD])

            def head_norm(row, lo, gain_row, gate_lo):
                for t in range(T):
                    o = xn[:, t, lo:lo + GW]
                    link(dve.tensor_tensor(tmp[:, t * GW:(t + 1) * GW], o, o, ALU.mult))
                link(dve.tensor_reduce(ms[:, row, :], tmp[:, 0:T * GW].rearrange("p (h d) -> p h d", d=HD), AX.X, ALU.add))
                rsqrt_mean(ms[:, row, :], ms[:, row, :], HD, RMS_EPS)
                for t in range(T):
                    o = xn[:, t, lo:lo + GW]
                    link(dve.tensor_tensor(heads4(o), heads4(o), wide4(ms[:, row + 1, t * GH:(t + 1) * GH]), ALU.mult))
                    link(dve.tensor_tensor(o, o, gain_row, ALU.mult))
                    link(dve.tensor_tensor(o, o, z2[:, t, gate_lo:gate_lo + GW], ALU.mult))

            dve.wait_ge(o_mm, GH)
            aug = lambda t: bank[2 + t][:, 0:GH * (HD + 1)].rearrange("p (h d) -> p h d", d=HD + 1)
            for t in range(T):
                link(dve.tensor_copy(ms[:, 9, t * GH:(t + 1) * GH].unsqueeze(2), aug(t)[:, :, HD:HD + 1]))
            dve.sem_inc(den_ready, 1)
            dve.wait_ge(m_exp, 2)
            link(dve.tensor_tensor(ms[:, 10, :], ms[:, 10, :], ms[:, 8, :], ALU.max))
            link(dve.reciprocal(ms[:, 10, :], ms[:, 10, :]))
            for t in range(T):
                link(dve.tensor_tensor(heads4(xn[:, t, 0:GW]), aug(t)[:, :, 0:HD], wide4(ms[:, 10, t * GH:(t + 1) * GH]),
                                       ALU.mult))
            dve.sem_inc(o_used, 1)
            dve.wait_ge(z2_act, 1)
            link(dve.tensor_scalar(z2[:, :, A_Q:A_Q + GW], z2[:, :, A_Q:A_Q + GW], HD ** -0.5, None, ALU.mult))
            dve.sem_inc(qk_ready, 1)
            head_norm(11, 0, rows2[:, 0, :], M_O)
            dve.wait_ge(conv_shift, 64)
            for t in range(T):
                taps = [conv[:, i, t, :] for i in range(3)]
                for i in range(3):
                    link(dve.tensor_tensor(taps[i], taps[i], rows2[:, 5 - i, :], ALU.mult))
                link(dve.tensor_tensor(taps[1], taps[1], taps[2], ALU.add))
                link(dve.tensor_tensor(taps[0], taps[0], taps[1], ALU.add))
                link(dve.tensor_tensor(xn[:, t, GW:2 * GW], taps[0], z2[:, t, C_B:C_B + GW], ALU.mult))
            pair_copy(qT2)
            pair_copy(kT2)

            def moba_copy(h):
                b = next_tp()
                if h >= 2:
                    dve.wait_ge(o_mm, GH + h - 1)
                dve.tensor_copy(wT2[:, h % 2, :], b[:, 0:3 * P]).then_inc(tp_evac, 1)

            for h in range(GH):
                n = SC_MOBA + h
                dve.wait_ge(sc_mm, n + 1)
                if h >= 2:
                    dve.wait_ge(w_exp, GH + h - 1)
                link(dve.tensor_copy(sc2[:, h % 2, :], bank[6 + n % 2][:, 0:3 * P]))
                dve.sem_inc(sc_evac, 1)
                dve.tensor_reduce(ms[:, 13, 2 * h:2 * h + 1], sc2[:, h % 2, 0:P], AX.X, ALU.max, negate=True)
                dve.tensor_reduce(ms[:, 13, 2 * h + 1:2 * h + 2], sc2[:, h % 2, P:3 * P], AX.X, ALU.max, negate=True)\
                    .then_inc(d_ready, 1)
                if h:
                    moba_copy(h - 1)
            moba_copy(GH - 1)
            dve.wait_ge(w_exp, 2 * GH)
            link(dve.reciprocal(ms[:, 15, :], ms[:, 14, :]))
            dve.wait_ge(o_mm, 2 * GH)
            inv2 = ms[:, 15, :].rearrange("p (h t) -> p t h", t=T)
            for t in range(T):
                link(dve.tensor_tensor(heads4(xn[:, t, 2 * GW:3 * GW]), heads4(bank[2 + t][:, 0:GW]),
                                       wide4(inv2[:, t, :]), ALU.mult))
            dve.sem_inc(o_used, 1)
            dve.wait_ge(hg_act, 3)
            fs2 = hg[:, HS, :, :]
            for level in range(LEVELS + 1):
                n = SC_HG + 3 * level
                if level:
                    dve.wait_ge(tp_mm, TP_HG + level)
                if level < LEVELS:
                    link(dve.scalar_tensor_tensor(fs2, hg[:, QK, :, :], cst["upper"][:, level:level + 1],
                                                  hg[:, HK, :, :], ALU.mult, ALU.add))
                    src = fs2
                dve.wait_ge(hg_exp, level + 1)
                e2 = ex2[:, level % 2, :].rearrange("p (t d) -> p t d", t=T)
                if level < LEVELS:
                    link(dve.tensor_tensor(fs2, fs2, e2, ALU.mult))
                else:
                    link(dve.tensor_tensor(fs2[:, 0, :], hg[:, HK, 0, :], e2[:, 0, :], ALU.mult))
                    link(dve.tensor_tensor(fs2[:, 1, :], hg[:, HQ, 1, :], e2[:, 1, :], ALU.mult))
                dve.sem_inc(sc_evac, 1)
                dve.sem_inc(ft_src, 1)
                if level:
                    dve.wait_ge(sc_mm, n)
                pair_copy(fT)
                for parity in range(2):
                    dve.wait_ge(sc_mm, n + 2 + parity)
                    b = bank[6 + (n + 1 + parity) % 2]
                    a = at[:, parity, :, :]
                    if level < LEVELS:
                        mask = cst["level_t"][:, level * P:(level + 1) * P].unsqueeze(1).broadcast_to([P, 4, P])
                        dst = a if level == 0 else tmp[:, 0:BANK].rearrange("p (i c) -> p i c", i=4)
                        link(dve.tensor_tensor(dst, four(b), mask, ALU.mult))
                        if level:
                            link(dve.tensor_tensor(a, a, dst, ALU.add))
                    else:
                        link(dve.tensor_copy(atx[:, parity, :, :], b[:, 0:2 * P].rearrange("p (i c) -> p i c", i=2)))
                    dve.sem_inc(sc_evac, 1)
            link(dve.tensor_tensor(hg[:, QK, :, :], hg[:, HQ, :, :], hg[:, HK, :, :], ALU.mult))
            link(dve.tensor_reduce(ms[:, 18, :], hg[:, QK, :, :].rearrange("p t (h d) -> p (t h) d", d=HD), AX.X, ALU.add))
            dve.wait_ge(o_mm, 2 * GH + 1)
            for t in range(T):
                o = xn[:, t, 3 * GW:4 * GW]
                link(dve.tensor_tensor(heads4(o), heads4(z2[:, t, H_I:H_I + GW]), wide4(ms[:, 18, t * GH:(t + 1) * GH]),
                                       ALU.mult))
                link(dve.tensor_tensor(o, o, bank[2 + t][:, 0:GW], ALU.add))
            head_norm(16, 3 * GW, rows2[:, 1, :], H_G)
            dve.sem_inc(y_ready, 1)
            untranspose()
            dve.wait_ge(mem_loaded, 16)
            norm_into(mem, mem, MEM)
            dve.sem_inc(xn_ready, 1)
            for t in range(T):
                for g in range(KT // 4):
                    tp_copy(memT[:, 4 * g:4 * g + 4, t * P:(t + 1) * P], P, BANK)
            dve.wait_ge(lin_evac, after(J_MIX + 1, 1))
            add_normed(hbuf, MIX_POST)
            dve.sem_inc(h_used, 1)
            norm_into(xn, x, CROSS_PRE)
            dve.sem_inc(xn_ready, 1)
            untranspose()

            def cross_copy(h):
                b = next_tp()
                if h >= 2:
                    dve.wait_ge(o_mm, 2 * GH + h)
                dve.tensor_copy(prxT[:, h % 2, :], b[:, :]).then_inc(tp_evac, 1)

            for h in range(CH):
                n = SC_X + h
                dve.wait_ge(sc_mm, n + 1)
                if h >= 2:
                    dve.wait_ge(w_exp, 2 * GH + h - 1)
                link(dve.tensor_copy(scx[:, h % 2, :, :], bank[6 + n % 2][:, :].rearrange("p (t m) -> p t m", t=T)))
                dve.sem_inc(sc_evac, 1)
                c = slice(T * h, T * h + T)
                link(dve.tensor_reduce(cs[:, 2, c], scx[:, h % 2, :, :], AX.X, ALU.max, negate=True))
                dve.tensor_scalar(cs[:, 0, c], cs[:, 2, c], CHD ** -0.5, None, ALU.mult).then_inc(d_ready, 1)
                if h:
                    cross_copy(h - 1)
            cross_copy(CH - 1)
            dve.wait_ge(w_exp, 2 * GH + CH)
            link(dve.reciprocal(cs[:, 3, :], cs[:, 1, :]))
            dve.wait_ge(o_mm, 2 * GH + 1 + CH)
            invx = cs[:, 3, :].rearrange("p (h t) -> p t h", t=T)
            for t in range(T):
                link(dve.tensor_tensor(xn[:, t, 0:CW].rearrange("p (h d) -> p h d", d=CHD),
                                       bank[2 + t][:, :].rearrange("p (h d) -> p h d", d=CHD),
                                       invx[:, t, :].unsqueeze(2).broadcast_to([P, CH, CHD]), ALU.mult))
            dve.sem_inc(y_ready, 1)
            untranspose(CW // P)
            dve.wait_ge(lin_evac, after(J_CO, 3))
            add_normed(hbuf, CROSS_POST)
            dve.sem_inc(h_used, 1)
            norm_into(xn, x, FFN_PRE)
            dve.sem_inc(xn_ready, 1)
            for i in range(2):
                link(dve.memset(gateT[:, i, :, 0:2], 0.0))
            dve.sem_inc(h_used, 1)
            untranspose()

            def ffn_act(i):
                dve.wait_ge(silu_ready, i + 1)
                dve.wait_ge(up_mm, i + 1)
                dve.tensor_tensor(actT[:, 2 * i:2 * i + 2, :], siluT[:, i % 2, :, :],
                                  bank[6 + i % 2][:, :].rearrange("p (i c) -> p i c", i=2), ALU.mult)\
                    .then_inc(act_ready, 1)

            for i in range(FF_JOBS):
                dve.wait_ge(lin_evac, after(J_FFN + i))
                if i >= 2:
                    dve.wait_ge(silu_ready, i - 1)
                for half in range(2):
                    c, tile = convT[:, i % 2, half, :], 2 * i + half
                    g = lambda shift: gateT[:, i % 2, half, 2 - shift:2 - shift + T * P]
                    link(dve.tensor_scalar(c, g(0), conv_w[:, 2, tile:tile + 1], conv_b[:, tile:tile + 1],
                                           ALU.mult, ALU.add))
                    link(dve.scalar_tensor_tensor(c, g(1), conv_w[:, 1, tile:tile + 1], c, ALU.mult, ALU.add))
                    link(dve.scalar_tensor_tensor(c, g(2), conv_w[:, 0, tile:tile + 1], c, ALU.mult, ALU.add))
                dve.sem_inc(conv_done, 1)
                if i:
                    ffn_act(i - 1)
            ffn_act(FF_JOBS - 1)
            dve.wait_ge(x2_ready, 3)
            add_normed(hbuf_f, FFN_POST)
            dve.sem_inc(out_ready, 1)

    return nc


def kernel(**inputs):
    import concourse.bacc as bacc
    from concourse.bass_utils import run_bass_kernel_spmd as run

    nc = bacc.Bacc("TRN2", target_bir_lowering=False, num_devices=1)
    arrays, A = {}, {}
    for name in INPUTS:
        a = np.asarray(inputs[name])
        if name not in UNLAYERED:
            a = a[0]
        if name in FLAT:
            a = a.reshape(-1)
        if name == "ffn_conv_w_2":
            a = a.reshape(3, FT_TILES, P).transpose(2, 0, 1)
        if name == "ffn_conv_b_2":
            a = a.reshape(FT_TILES, P).T
        if name == "c":
            a = a.reshape(KT, P).T
        a = np.ascontiguousarray(a)
        arrays["in_" + name] = a
        A[name] = nc.dram_tensor("in_" + name, a.shape, mybir.dt.from_np(a.dtype), kind="ExternalInput").ap()
    consts = {}
    for name, a in shape_constants().items():
        arrays["const_" + name] = a
        consts[name] = nc.dram_tensor("const_" + name, a.shape, F32, kind="ExternalInput").ap()
    out = nc.dram_tensor("out_0_dram", (T * P, D), F32, kind="ExternalOutput").ap()
    build(nc, A, consts, out)
    r = run(nc, [arrays], core_ids=[0])
    return r.results[0]["out_0_dram"].reshape(1, T * P, D)
```

```python
import math
from contextlib import ExitStack

import concourse.bass as bass
import numpy as np
from concourse import mybir

F32 = mybir.dt.float32
I32 = mybir.dt.int32
F32R = mybir.dt.float32r
ALU = mybir.AluOpType
ACT = mybir.ActivationFunctionType
AX = mybir.AxisListType

P = 128
T = 2
D = 1024
KT = D // P
BANK = 512
HD = 64
HEADS = 8
W1 = HEADS * HD
FOX_COLS = 4 * W1 + 3 * HEADS
DECAY_R, ICLR_R, GATE_R = 64, 64, 160
RW_COLS = 3 * W1 + DECAY_R + ICLR_R + GATE_R
EXPERTS, GROUPS, TOP_GROUPS, TOP_K = 64, 8, 4, 6
GROUP_SIZE = EXPERTS // GROUPS
D_E = 256
ROUTED_SCALE = 2.5
CS = 64
TH = [CS * i for i in range(T * P // CS)]
MAX_CHUNKS = (T * P * TOP_K + EXPERTS * (CS - 1)) // CS
MAX_QUADS = -(-MAX_CHUNKS // 4)
NC = 4 * MAX_QUADS + 4
UNMATCHED = 4096.0
GH = 4
GW = GH * HD
IN2 = 14 * GW + 2 * GH
(M_Q, M_K, M_V, M_O) = (i * GW for i in range(4))
M_I, M_F = 4 * GW, 4 * GW + GH
(C_B, C_C, C_H, A_Q, A_K, A_V, H_Q, H_F, H_I, H_G) = (4 * GW + 2 * GH + i * GW for i in range(10))
CH, CHD = 4, 128
CW = CH * CHD
BUCKETS, MAX_DIST = 32, 128
D_FF = 2816
FT_TILES = D_FF // P
FF_JOBS = D_FF // 256
TINY = 2.0 ** -64
RMS_EPS = 1e-6
LNX_EPS = 64e-5
MASKED = -1e30
LEVELS = 7



def shape_constants():
    row = np.arange(P)[:, None]
    col = np.arange(P)[None, :]
    f = lambda a: np.ascontiguousarray(a.astype(np.float32))
    c = {}
    c["ident"] = f(row == col)
    c["triu"] = f(row <= col)
    c["mid"] = f((row <= col)) - f((row <= P // 2 - 1) & (col >= 0))
    causal = np.where(row >= col, 0.0, MASKED)
    c["causal"] = f(np.concatenate([causal, np.zeros((P, P)), causal], 1))
    strict, incl = f(row < col), f(row <= col)
    c["wkv_mask"] = f(np.concatenate([strict, incl, strict, incl], 1))
    lv = []
    for level in range(LEVELS):
        n = 1 << level
        lv.append(((row // (2 * n)) == (col // (2 * n))) & ((row // n) % 2 == 1) & ((col // n) % 2 == 0))
    c["level"] = f(np.concatenate(lv, 1))
    half = f((row >= P // 2) & (np.arange(2)[None, :] == 0)) + f((row < P // 2) & (np.arange(2)[None, :] == 1))
    c["halves"] = half
    c["pairs"] = f((row // HD) == (col // HD))
    idx = np.concatenate([np.arange(NC), TH, np.arange(1, CS + 1)])[None, :] + np.zeros((P, 1))
    c["moe_idx"] = f(np.concatenate([idx, row], 1))
    c["anti"] = f(row + col == P - 1)
    causal_t = np.where(row <= col, 0.0, MASKED)
    c["causal_t"] = f(np.concatenate([causal_t, np.zeros((P, P)), causal_t], 1))
    c["tril_strict"] = f(row > col)
    lt, span = [], []
    for level in range(LEVELS):
        n = 1 << level
        lt.append(lv[level].T)
        same = (row // (2 * n)) == (col // (2 * n))
        up_r, up_c = (row // n) % 2 == 1, (col // n) % 2 == 1
        span.append(same & ((up_c & up_r & (row <= col)) | (~up_c & ~up_r & (row > col))))
    c["level_t"] = f(np.concatenate(lt, 1))
    c["span"] = f(np.concatenate(span, 1))
    c["upper"] = f(np.concatenate([(row // (1 << level)) % 2 == 1 for level in range(LEVELS)], 1))
    c["neg_head"] = f(-(np.arange(GH)[:, None] == np.arange(GH * P)[None, :] // P).astype(np.float32))
    j = np.arange(3 * P)
    dist = T * P - 1 - j
    exact = BUCKETS // 2
    nf = np.maximum(dist, 1).astype(np.float32)
    large = exact + (np.log(nf / exact) / math.log(MAX_DIST / exact) * (BUCKETS - exact)).astype(np.int32)
    bucket = np.where(dist < exact, dist, np.minimum(large, BUCKETS - 1))
    c["bucket"] = f(np.where(dist[None, :] >= 0, np.arange(BUCKETS + 1)[:, None] == bucket[None, :],
                             np.arange(BUCKETS + 1)[:, None] == BUCKETS))
    return c


INPUTS = ["x", "c", "norm1_g", "norm2_g", "ada_w", "ada_b", "w_in", "w_out", "fox_qn_g", "fox_kn_g", "fox_on_g",
          "fox_forget_b", "rw_mu", "rw_w0", "rw_decay_up", "rw_a0", "rw_iclr_up", "rw_gate_up", "rw_k_k", "rw_k_a",
          "rw_r_k", "rw_lnx_g", "rw_lnx_b", "router_w", "router_bias", "exp_w_gate", "exp_w_up", "exp_w_down",
          "sh_w_gate", "sh_w_up", "sh_w_down", "final_g", "mem_2", "w_in_2", "b_in_2", "mlstm_norm_2", "sconv_w_2",
          "rel_bias_2", "hgrn_lb_logits_2", "hgrn_norm_2", "w_mix_out_2", "norm_mix_pre_2", "norm_mix_post_2",
          "mem_norm_2", "w_cq_2", "w_ck_2", "w_cv_2", "w_co_2", "norm_cross_pre_2", "norm_cross_post_2",
          "w_ffn_in_2", "ffn_conv_w_2", "ffn_conv_b_2", "w_ffn_out_2", "norm_ffn_pre_2", "norm_ffn_post_2"]
UNLAYERED = ("final_g", "rel_bias_2")
FLAT = ("fox_qn_g", "fox_kn_g", "fox_on_g", "rw_r_k")
CONST_0 = ("ident", "triu")
CONST_1 = ("mid", "causal", "wkv_mask", "level", "halves", "pairs")


CONST_2 = ("anti", "causal_t", "tril_strict", "level_t", "span", "upper", "neg_head", "bucket")

def build(nc, A, consts, out):
    def load_cols(name, lo, n):
        return A[name].rearrange("(k p) n -> p k n", p=P)[:, :, lo:lo + n]

    def bcast(ap1d):
        return bass.AP(ap1d.tensor, ap1d.offset, [[0, P], [1, ap1d.shape[-1]]])

    ctx = ExitStack()

    def sb(name, shape, stack=ctx):
        return stack.enter_context(nc.sbuf_tensor(name, shape, F32))

    def stack_i32(stack, name, shape):
        return stack.enter_context(nc.sbuf_tensor(name, shape, I32))

    def stack_r(stack, name, shape):
        return stack.enter_context(nc.sbuf_tensor(name, shape, F32R))

    def sem(name):
        return ctx.enter_context(nc.semaphore(name))

    with ctx:
        RING = 2

        def with_low(name, shape, stack=ctx, low_shape=None):
            with ExitStack() as first:
                whole = sb(name, shape, first)
            return whole, stack_r(stack, name + "_12", low_shape or shape)

        ring, w_low = with_low("ring", [P, RING, KT * BANK + BANK])
        x = sb("x", [P, T, D])
        xn = sb("xn", [P, T, D])
        xT, xT_low = with_low("xT", [P, KT, T * P])
        mod, mod_12 = with_low("mod", [P, 3, D])
        gain = sb("gain", [P, 2, D])
        small = sb("small", [P, 64])
        ones = sb("ones", [1, P])
        cst = {}
        for name in CONST_0:
            cst[name] = sb("c_" + name, list(consts[name].shape))
        tmp = sb("tmp", [P, D])
        silu_c = sb("silu_c", [P, KT, P])
        ones_pp = sb("ones_pp", [P, P])

        SH, SC, GT = range(3)

        rw_stack = ExitStack()
        for name in CONST_1:
            cst[name] = sb("c_" + name, list(consts[name].shape), rw_stack)
        z_rw = sb("z_rw", [P, T, RW_COLS], rw_stack)
        lora_up = sb("lora_up", [P, BANK], rw_stack)
        gate_up = sb("gate_up", [P, 2, BANK], rw_stack)
        rwp = sb("rwp", [P, 7, W1], rw_stack)
        W0, A0, KK_, KA_, RK_, LG, LB = range(7)

        fox_stack = ExitStack()
        z_fox = sb("z_fox", [P, T, FOX_COLS], fox_stack)
        kv_prev = sb("kv_prev", [P, T, 2 * W1], fox_stack)
        fxp = sb("fxp", [P, 3, W1], fox_stack)
        forget_b = sb("forget_b", [P, HEADS], fox_stack)
        AUG = HD + 2
        q_aug = sb("q_aug", [P, T, HEADS, AUG], fox_stack)
        k_aug = sb("k_aug", [P, T, HEADS, AUG], fox_stack)
        sc_sb = tmp[:, 0:6 * P].rearrange("p (b c) -> p b c", b=2)
        pr_sb = sb("pr_sb", [P, 2, 3 * P], fox_stack)
        prT = xn[:, :, W1:W1 + 3 * P]
        fs = sb("fs", [P, 12, T * 16], fox_stack)
        q_augT = sb("q_augT", [AUG, HEADS, T * P], fox_stack)
        k_augT = sb("k_augT", [AUG, HEADS, T * P], fox_stack)
        z_prev = sb("z_prev", [P, RW_COLS], fox_stack)
        mu = sb("mu", [P, RW_COLS], fox_stack)
        fox_stack.close()

        wkv_stack = ExitStack()
        logw = sb("logw", [P, T, W1], wkv_stack)
        iclr = sb("iclr", [P, T, W1], wkv_stack)
        gate = sb("gate", [P, T, W1], wkv_stack)
        RT_, AT_, BT_, KTT_ = range(4)
        til = sb("til", [P, 4, T, W1], wkv_stack)
        tilT = sb("tilT", [P, 4, 4, P], wkv_stack)
        gram = sb("gram", [P, HEADS, 4, P], wkv_stack)
        lora_stack = ExitStack()
        loraT = sb("loraT", [P, 3, T * P], lora_stack)
        lora_stack.close()
        amat = sb("amat", [P, HEADS, P], wkv_stack)
        inv = sb("inv", [P, HEADS, P], wkv_stack)
        invT = sb("invT", [P, HEADS, P], wkv_stack)
        rhs_u = sb("rhs_u", [P, 2, W1], wkv_stack)
        stateT = sb("stateT", [P, 4, P], wkv_stack)
        ws = sb("ws", [P, 8, T * HEADS], wkv_stack)
        y_rw = sb("y_rw", [P, T, W1], wkv_stack)
        wkv_stack.close()
        rw_stack.close()

        p2_stack = ExitStack()
        GAINS = ("final_g", "norm_mix_pre_2", "norm_mix_post_2", "mem_norm_2", "norm_cross_pre_2",
                 "norm_cross_post_2", "norm_ffn_pre_2", "norm_ffn_post_2")
        gains2 = sb("gains2", [P, len(GAINS) - 2, D], p2_stack)

        def gain_of(i):
            return gain[:, i, :] if i < 2 else gains2[:, i - 2, :]

        conv_w = sb("conv_w", [P, 3, FT_TILES], p2_stack)
        conv_b = sb("conv_b", [P, FT_TILES], p2_stack)
        par_stack = ExitStack()
        ROWS = ("mlstm_norm_2", "hgrn_norm_2", "hgrn_lb_logits_2")
        rows2 = sb("rows2", [P, 3 + 3, GW], par_stack)
        rel = sb("rel", [BUCKETS + 1, GH], par_stack)
        for name in CONST_2:
            cst[name] = sb("c_" + name, list(consts[name].shape), par_stack)
        rel_row = sb("rel_row", [GH, 3 * P], par_stack)
        hankel = sb("hankel", [P, GH, 2 * P], par_stack)

        moe_stack = ExitStack()
        GU_W = KT * 2 * D_E
        DN_W = (D_E // P) * D
        gu_odd = sb("gu_odd", [P, 2, GU_W], moe_stack)
        dn = sb("dn", [P, 4, DN_W], moe_stack)
        moe_idx = sb("moe_idx", list(consts["moe_idx"].shape), moe_stack)
        chunk_no, thresholds = moe_idx[:, 0:NC], moe_idx[0:EXPERTS, NC:NC + len(TH)]
        slot_no = moe_idx[:, NC + len(TH):NC + len(TH) + CS]
        expert_no = moe_idx[0:EXPERTS, NC + len(TH) + CS:NC + len(TH) + CS + 1]
        taken = [0]

        def in_gu_odd(rows, *dims):
            n = math.prod(dims)
            a = gu_odd[0:rows, 1, taken[0]:taken[0] + n]
            taken[0] += n
            assert taken[0] <= GU_W
            return a if len(dims) == 1 else a.rearrange(("p (a b) -> p a b", "p (a b c) -> p a b c")[len(dims) - 2],
                                                        **dict(zip("ab", dims[:-1])))

        router_w = in_gu_odd(P, KT, EXPERTS)
        router_b = in_gu_odd(P, EXPERTS)
        score = in_gu_odd(P, T, EXPERTS)
        sel = in_gu_odd(P, T, EXPERTS)
        rt = in_gu_odd(P, 6, T, EXPERTS)
        wts = in_gu_odd(P, T, EXPERTS)
        maskT = in_gu_odd(EXPERTS, T * P)
        rankT = in_gu_odd(EXPERTS, T * P)
        wtsT = in_gu_odd(EXPERTS, T * P)
        of_chunk = in_gu_odd(EXPERTS, 2, NC)
        rc = sb("rc", [P, 16], moe_stack)
        place = sb("place", [P, T, NC], moe_stack)
        weight = sb("weight", [P, T, NC], moe_stack)
        expert_of = stack_i32(moe_stack, "expert_of", [1, NC])
        quads_i = stack_i32(moe_stack, "quads_i", [1, 1])
        hgT = xT[:, :, 0:P]
        y_sb = mod[:, SC, :]
        pick = mod[:, SH, 0:BANK].rearrange("p (b t c) -> p b t c", b=2, t=T)
        putT = mod[:, SH, BANK:D].rearrange("p (b t c) -> p b t c", b=2, t=T)
        silu_g = silu_c[:, 4:8, :].rearrange("p (t b) c -> p t (b c)", t=T)
        act_e = tmp[:, 0:BANK].rearrange("p (t c) -> p t c", t=T)
        act_eT = tmp[:, BANK:D].rearrange("p (t k c) -> p t k c", t=T, k=D_E // P)
        put = silu_c[:, 0:4, :].rearrange("p (b t) c -> p b t c", b=2)
        moe_stack.close()

        mix_stack = ExitStack()
        z2 = sb("z2", [P, T, IN2], mix_stack)
        ms = sb("ms", [P, 28, T * GH], mix_stack)
        conv = sb("conv", [P, 3, T, GW], mix_stack)
        with ExitStack() as projection:
            w_high_in = stack_r(projection, "w_high_in", [P, RING, KT * BANK])
        e_row = sb("e_row", [GH, 2, T * P], mix_stack)
        qT2 = sb("qT2", [P, 2, T * P], mix_stack)
        kT2 = sb("kT2", [P, 2, T * P], mix_stack)
        v_aug = sb("v_aug", [P, T, GH, HD + 1], mix_stack)
        sc2 = sb("sc2", [P, 2, 3 * P], mix_stack)
        pr2 = sb("pr2", [P, 2, 3 * P], mix_stack)
        wT2 = sb("wT2", [P, 2, 3 * P], mix_stack)
        hg = sb("hg", [P, 5, T, GW], mix_stack)
        LF, HQ, HK, QK, HS = range(5)
        ex2 = sb("ex2", [P, 2, T * GW], mix_stack)
        fT = sb("fT", [P, 2, T * P], mix_stack)
        at = mod[:, SH, :].rearrange("p (a i c) -> p a i c", a=2, i=4)
        atx = mod[:, SC, 0:BANK].rearrange("p (a i c) -> p a i c", a=2, i=2)
        mem = (silu_c[:, :, :].rearrange("p k c -> p (k c)"), mod[:, GT, :])
        ckT = silu_c[:, :, :].rearrange("p (h b) c -> p h (b c)", h=CH)
        cv = mod[:, GT, :].rearrange("p (t c) -> p t c", t=T)
        mix_stack.close()

        end_stack = ExitStack()
        hbuf = sb("hbuf", [P, T, D], end_stack)
        cqT = sb("cqT", [P, CH, T * P], end_stack)
        scx = sb("scx", [P, 2, T, 2 * P], end_stack)
        prx = sb("prx", [P, 2, T, 2 * P], end_stack)
        prxT = sb("prxT", [P, 2, 4 * P], end_stack)
        cs = sb("cs", [P, 6, T * CH], end_stack)
        end_stack.close()
        par_stack.close()
        ffn_stack = ExitStack()
        hbuf_f = xn
        gateT = sb("gateT", [P, 2, 2, 2 + T * P], ffn_stack)
        convT = silu_c[:, :, :].rearrange("p (b i c) x -> p b i (c x)", b=2, i=2)
        siluT = mod[:, GT, :].rearrange("p (b i c) -> p b i c", b=2, i=2)
        actT, act_low = with_low("actT", [P, FT_TILES, T * P], ffn_stack)
        w_high = stack_r(ffn_stack, "w_high", [P, RING, KT * BANK])
        act_high = stack_r(ffn_stack, "act_high", [P, FT_TILES, T * P])
        xT_high = mod_12[:, 0:2, :].rearrange("p a (k c) -> p (a k) c", c=T * P)
        ffn_stack.close()
        p2_stack.close()

        bank = [ctx.enter_context(nc.psum_tensor(f"bank{i}", [P, BANK], F32)) for i in range(8)]

        w_full = [sem(f"w_full{i}") for i in range(RING)]
        w_used = sem("w_used")
        lin_mm = sem("lin_mm")
        lin_evac = sem("lin_evac")
        tp_mm = sem("tp_mm")
        tp_evac = sem("tp_evac")
        sc_mm = sem("sc_mm")
        sc_evac = sem("sc_evac")
        x_loaded = sem("x_loaded")
        c_loaded = sem("c_loaded")
        const_loaded = sem("const_loaded")
        gain_loaded = [sem(f"gain_loaded{i}") for i in range(2)]
        par_loaded = sem("par_loaded")
        silu_done = sem("silu_done")
        cb_ready = sem("cb_ready")
        ones_ready = sem("ones_ready")
        inv_var = sem("inv_var")
        rstd_done = sem("rstd_done")
        xn_ready = sem("xn_ready")
        sq_ask = sem("sq_ask")
        sq_done = sem("sq_done")
        mod_used = sem("mod_used")
        pad_zero = sem("pad_zero")
        kv_shifted = sem("kv_shifted")
        zr_shifted = sem("zr_shifted")
        lerp_done = sem("lerp_done")
        pool_chain = sem("pool_chain")
        vec_chain = sem("vec_chain")
        act_chain = sem("act_chain")
        fox_gates = sem("fox_gates")
        fox_in = sem("fox_in")
        fox_ln = sem("fox_ln")
        logf_ready = sem("logf_ready")
        aug_ready = sem("aug_ready")
        negmax_ready = sem("negmax_ready")
        prob_ready = sem("prob_ready")
        pv_mm = sem("pv_mm")
        pv_evac = sem("pv_evac")
        fox_sig = sem("fox_sig")
        rw_tanh = sem("rw_tanh")
        lora_in = sem("lora_in")
        rw_sig = sem("rw_sig")
        logw_ready = sem("logw_ready")
        rw_exp = sem("rw_exp")
        til_ready = sem("til_ready")
        wkv_w = sem("wkv_w")
        wkv_mm = sem("wkv_mm")
        wkv_upd = sem("wkv_upd")
        u_mm = sem("u_mm")
        u_evac = sem("u_evac")
        state_ready = sem("state_ready")
        y_ready = sem("y_ready")
        router_loaded = sem("router_loaded")
        router_sig = sem("router_sig")
        sh_full = sem("sh_full")
        gu_full = [sem(f"gu_full{i}") for i in range(2)]
        dn_full = [sem(f"dn_full{i}") for i in range(2)]
        mixer_read = sem("mixer_read")
        routed = sem("routed")
        quads_ready = sem("quads_ready")
        pick_ready = sem("pick_ready")
        gather_mm = sem("gather_mm")
        gather_copied = sem("gather_copied")
        gu_mm = sem("gu_mm")
        gate_act = sem("gate_act")
        act_made = sem("act_made")
        actT_mm = sem("actT_mm")
        actT_copied = sem("actT_copied")
        down_mm = sem("down_mm")
        y_copied = sem("y_copied")
        put_mm = sem("put_mm")
        put_copied = sem("put_copied")
        spread_mm = sem("spread_mm")
        experts_added = sem("experts_added")
        experts_copied = sem("experts_copied")
        x2_ready = sem("x2_ready")
        w_done = sem("w_done")
        p2_loaded = sem("p2_loaded")
        rel_made = sem("rel_made")
        rel_mm = sem("rel_mm")
        rel_copied = sem("rel_copied")
        hankel_made = sem("hankel_made")
        ml_in = sem("ml_in")
        ml_ln = sem("ml_ln")
        ml_logf = sem("ml_logf")
        e_ready = sem("e_ready")
        m_row = sem("m_row")
        qk_ready = sem("qk_ready")
        m_ready = sem("m_ready")
        m_exp = sem("m_exp")
        d_ready = sem("d_ready")
        w_exp = sem("w_exp")
        w_ready = sem("w_ready")
        o_mm = sem("o_mm")
        o_used = sem("o_used")
        den_ready = sem("den_ready")
        z2_act = sem("z2_act")
        conv_prod = sem("conv_prod")
        conv_shift = sem("conv_shift")
        f_ready = sem("f_ready")
        hg_act = sem("hg_act")
        hg_exp = sem("hg_exp")
        ft_src = sem("ft_src")
        mem_loaded = sem("mem_loaded")
        up_mm = sem("up_mm")
        conv_done = sem("conv_done")
        silu_ready = sem("silu_ready")
        act_ready = sem("act_ready")
        ffn_mm = sem("ffn_mm")
        h_used = sem("h_used")
        in_full = [sem(f"in_full{i}") for i in range(4)]
        in_high_made = sem("in_high_made")
        in_low_made = sem("in_low_made")
        in_done = sem("in_done")
        unit_full = [sem(f"unit_full{i}") for i in range(4)]
        high_made = sem("high_made")
        low_made = sem("low_made")
        x_high_made = sem("x_high_made")
        x_low_made = sem("x_low_made")
        act_high_made = sem("act_high_made")
        act_low_made = sem("act_low_made")
        out_ready = sem("out_ready")
        store_done = sem("store_done")

        jobs = []

        def job(kind, w, lo, n, kt=KT, bias=None):
            dst = lambda slot: ring[:, slot, 0:kt * n].rearrange("p (k n) -> p k n", k=kt)
            parts = [(dst, A[w].rearrange("(k p) n -> p k n", p=P)[:, :, lo:lo + n])]
            if bias is not None:
                parts.append((lambda slot: ring[0:1, slot, KT * BANK:KT * BANK + n],
                              A[bias][lo:lo + n].rearrange("(a n) -> a n", a=1)))
            jobs.append((kind, lo, n, kt, parts, bias is not None))

        ADA_FIRST = [(SH, 0), (SH, 1), (SC, 0), (SC, 1)]
        ADA_GATE = [(GT, 0), (GT, 1)]
        for which, h in ADA_FIRST:
            job("ada", "ada_w", which * D + h * BANK, BANK, bias="ada_b")
        FOX_JOBS = [(512, 512), (1024, 512), (2048, 24), (0, 512), (1536, 512)]
        RW_JOBS = [(FOX_COLS, 512), (FOX_COLS + 512, 512), (FOX_COLS + 1024, 512), (FOX_COLS + 1536, 288)]
        for lo, n in FOX_JOBS + RW_JOBS:
            job("in", "w_in", lo, n)
        for which, h in ADA_GATE:
            job("ada", "ada_w", (3 + which) * D + h * BANK, BANK, bias="ada_b")
        for which, h in ADA_FIRST[0:2]:
            job("ada", "ada_w", (3 + which) * D + h * BANK, BANK, bias="ada_b")
        for which, h in ADA_GATE:
            job("ada", "ada_w", which * D + h * BANK, BANK, bias="ada_b")
        for which, h in ADA_FIRST[2:4]:
            job("ada", "ada_w", (3 + which) * D + h * BANK, BANK, bias="ada_b")
        for h in range(2):
            job("out", "w_out", h * BANK, BANK)
        N_IN2 = IN2 // BANK
        IN2_SLOT = len(jobs) + 1
        job("in2", "w_in_2", N_IN2 * BANK, IN2 - N_IN2 * BANK, bias="b_in_2")
        for w in ("w_ck_2", "w_cv_2"):
            job("cross", w, 0, CW)
        for h in range(2):
            job("mix", "w_mix_out_2", h * BANK, BANK)
        job("cross", "w_cq_2", 0, CW)
        job("co", "w_co_2", 0, D, kt=CW // P)
        N_OUT = dict(ada=1, co=4)
        outputs = {}
        for j, (kind, *_rest) in enumerate(jobs):
            for t in range(N_OUT.get(kind, T)):
                outputs[(j, t)] = len(outputs)
            if kind == "in2":
                for i in range(N_IN2):
                    for t in range(T):
                        outputs[(("in2", i), t)] = len(outputs)
        for i in range(FF_JOBS):
            outputs[(len(jobs) + i, 0)] = len(outputs)
        J_ADA1, J_FOX, J_RW = 0, 4, 4 + len(FOX_JOBS)
        J_GATE = J_RW + len(RW_JOBS)
        J_SHIFT2 = J_GATE + 2
        J_GATE1 = J_SHIFT2 + 2
        J_SCALE2 = J_GATE1 + 2
        J_OUT = J_SCALE2 + 2
        J_IN2 = J_OUT + 2
        J_ADA2 = (J_SHIFT2, J_SCALE2)
        N_P2 = len(GAINS) + len(ROWS) + 3 + 2 + 1 + len(CONST_2)
        J_CK, J_CV, J_MIX = (J_IN2 + 1 + i for i in range(3))
        J_CQ, J_CO = J_MIX + 2, J_MIX + 3
        J_FFN = J_CO + 1
        assert J_FFN == len(jobs)
        UNIT = KT * 256
        units = []
        for i in range(FF_JOBS):
            for part in range(2):
                lo = part * D_FF + i * 256
                units.append((KT, A["w_ffn_in_2"].rearrange("(k p) n -> p k n", p=P)[:, :, lo:lo + 256]))
        for i in range(0, FT_TILES, 2):
            units.append((2, A["w_ffn_out_2"].rearrange("(k p) n -> p k n", p=P)[:, i:i + 2, :]))
        PIECE = 1024
        PIECES = UNIT // PIECE

        def of_half(a, u, lo=0, n=UNIT):
            lo += u % 2 * UNIT
            return a[:, (IN2_SLOT + u // 2) % RING, lo:lo + n]

        def of_unit(a, u, lo=0, n=UNIT):
            lo += u % 2 * UNIT
            return a[:, (J_FFN + u // 2) % RING, lo:lo + n]

        FOX_FILL = [(J_RW + 2, 0), (J_RW + 2, 1), (J_RW + 3, 0), (J_RW + 3, 1), (J_GATE, 0), (J_GATE + 1, 0)]

        def lin_bank(o):
            return o % 2 + 2 * (o in [outputs[(j + i, 0)] for j in J_ADA2 for i in range(2)]
                                or o in [outputs[(J_OUT + 1, t)] for t in range(T)])

        def after(j, t=0):
            return outputs[(j, t)] + 1

        TP_H = 0
        TP_AUG = 4
        TP_PROB = TP_AUG + 8
        TP_LORA = TP_PROB + HEADS
        TP_TIL = TP_LORA + 2
        TP_Y = TP_TIL + 8
        SC_CUMF = 0
        SC_FOX = 1
        SC_LORA = SC_FOX + HEADS
        SC_CUM = SC_LORA + 6
        SC_GRAM = SC_CUM + 3
        SC_ROUTER = SC_GRAM + 21
        SC_ROUTE = SC_ROUTER + 1
        SC_G2 = SC_ROUTE + 4
        SC_ML = SC_G2 + 1
        SC_MOBA = SC_ML + 2 * GH
        SC_HG = SC_MOBA + GH
        SC_X = SC_HG + 3 * (LEVELS + 1)
        TP_H2 = TP_Y + 4
        TP_IN2 = TP_H2 + 4
        TP_MEM = TP_IN2 + 4
        TP_ML = TP_MEM + 4
        TP_MOBA = TP_ML + 4
        TP_P2 = TP_MOBA + 2
        TP_HG = TP_P2 + GH
        TP_Y2 = TP_HG + LEVELS + 1
        TP_XN = TP_Y2 + 4
        TP_PX = TP_XN + 4
        TP_O = TP_PX + CH
        TP_FF = TP_O + 2


        def slot(h):
            return 4 * (h % 2) + h // 2

        def wkv_count(t, level, g, which):
            base = t * (2 + 4 * (LEVELS - 1))
            return base + g + 1 if level == 0 else base + 2 + 4 * (level - 1) + 2 * g + 1 + which

        block = ctx.enter_context(nc.Block())

        @block.sync
        def _(sp):
            def stream(first, last):
                for j in range(first, last):
                    if j >= RING:
                        sp.wait_ge(w_used, j - RING + 1 if j <= J_IN2 else
                                   max(J_IN2 + 1, j - RING + 1) + 2 * N_IN2)
                    for dst, src in jobs[j][4]:
                        sp.dma_start(dst(j % RING), src).then_inc(w_full[j % RING], 16)

            stream(0, J_IN2)
            def gate_up(dst, gate_w, up_w, full):
                dst = dst.rearrange("p (k n) -> p k n", k=KT)
                sp.dma_start(dst[:, :, 0:D_E], gate_w.rearrange("(k p) n -> p k n", p=P)).then_inc(full, 16)
                sp.dma_start(dst[:, :, D_E:2 * D_E], up_w.rearrange("(k p) n -> p k n", p=P)).then_inc(full, 16)

            def down(dst, down_w, full):
                sp.dma_start(dst.rearrange("p (k n) -> p k n", k=D_E // P),
                             down_w.rearrange("(k p) n -> p k n", p=P)).then_inc(full, 16)

            sp.wait_ge(mixer_read, 1)
            gate_up(gu_odd[:, 0, :], A["sh_w_gate"], A["sh_w_up"], sh_full)
            down(dn[:, 2, :], A["sh_w_down"], sh_full)
            sp.wait_ge(quads_ready, 1)
            sp.wait_ge(w_used, J_IN2)
            quads = sp.value_load(quads_i[0:1, 0:1], min_val=1, max_val=MAX_QUADS)
            with sp.Fori(0, quads) as i:
                for parity in range(2):
                    p = i * 2 + parity
                    e = [sp.value_load(expert_of[0:1, bass.ds(i * 4 + 2 * parity + c, 1)], min_val=0,
                                       max_val=EXPERTS - 1) for c in range(2)]
                    sp.wait_ge(gu_mm, p + 1)
                    for c in range(2):
                        gate_up(ring[:, c, 0:GU_W] if parity == 0 else gu_odd[:, c, :],
                                A["exp_w_gate"][e[c]], A["exp_w_up"][e[c]], gu_full[parity])
                    sp.wait_ge(spread_mm, p + 2)
                    for c in range(2):
                        down(dn[:, 2 * parity + c, :], A["exp_w_down"][e[c]], dn_full[parity])
            sp.wait_ge(experts_copied, 1)
            stream(J_IN2, J_IN2 + 1)
            for u in range(2 * N_IN2):
                if u >= 2:
                    sp.wait_ge(w_used, J_IN2 + 1 if u < 4 else J_IN2 + 1 + u - 3)
                w = A["w_in_2"].rearrange("(k p) n -> p k n", p=P)
                c = slice(u // 2 * BANK, (u // 2 + 1) * BANK)
                full = in_full[u % 4]
                sp.dma_start(of_half(ring, u).rearrange("p (k n) -> p k n", n=BANK),
                             w[:, u % 2 * KT // 2:(u % 2 + 1) * KT // 2, c]).then_inc(full, 16)
                if u % 2:
                    sp.dma_start(ring[0:1, (IN2_SLOT + u // 2) % RING, KT * BANK:KT * BANK + BANK],
                                 A["b_in_2"][c].rearrange("(a n) -> a n", a=1)).then_inc(full, 16)
            stream(J_IN2 + 1, len(jobs))
            for u, (k, src) in enumerate(units):
                sp.wait_ge(w_used, 2 * N_IN2 + (J_FFN - 1 + u // 2 if u < 4 else J_FFN + u - 3))
                sp.dma_start(of_unit(ring, u).rearrange("p (k n) -> p k n", k=k), src).then_inc(unit_full[u % 4], 16)
            sp.wait_ge(out_ready, 1)
            sp.dma_start(out.rearrange("(t p) d -> p t d", p=P), x[:, :, :]).then_inc(store_done, 16)
            sp.wait_ge(store_done, 16)

        @block.scalar
        def _(act):
            chain = [0]

            def link(ins):
                chain[0] += 1
                ins.then_inc(act_chain, 1)
                act.wait_ge(act_chain, chain[0])

            asked = [0]

            def squares(rows, scratch, wait=True):
                if wait:
                    asked[0] += 1
                    act.wait_ge(sq_ask, asked[0])
                for i, row in enumerate(rows):
                    act.activation(scratch[i], row, ACT.Square,
                                   accum_out=small[:, 18 - len(rows) + i:19 - len(rows) + i]).then_inc(sq_done, 1)

            rstd_n = [0]

            def rstd(dst, src):
                rstd_n[0] += 1
                act.wait_ge(inv_var, rstd_n[0])
                act.activation(dst, src, ACT.Sqrt).then_inc(rstd_done, 1)

            def lin_copy(j, t, dst):
                act.wait_ge(lin_mm, after(j, t))
                act.activation(dst, bank[lin_bank(outputs[(j, t)])][:, 0:jobs[j][2]], ACT.Copy).then_inc(lin_evac, 1)

            def lin_copy_heads(j, i, dst):
                act.wait_ge(lin_mm, after(j, i))
                act.activation(dst[:, 2 * i:2 * i + 2, :],
                               bank[outputs[(j, i)] % 2][:, :].rearrange("p (h c) -> p h c", h=2), ACT.Copy)\
                    .then_inc(lin_evac, 1)

            act.dma_start(small[:, 0:KT], A["c"]).then_inc(c_loaded, 16)
            act.dma_start(x[:, :, :], A["x"].rearrange("(t p) d -> p t d", p=P)).then_inc(x_loaded, 16)
            act.dma_start(gain[:, 0, :], bcast(A["norm1_g"])).then_inc(gain_loaded[0], 16)
            for name in CONST_0:
                act.dma_start(cst[name][:, :], consts[name]).then_inc(const_loaded, 16)
            act.wait_ge(c_loaded, 16)
            act.activation(small[:, KT:2 * KT], small[:, 0:KT], ACT.Silu).then_inc(silu_done, 1)
            rstd(small[:, 18:20], small[:, 16:18])
            for j, (which, h) in enumerate(ADA_FIRST):
                lin_copy(J_ADA1 + j, 0, mod[:, which, h * BANK:(h + 1) * BANK])
                if j == 1:
                    act.dma_start(gain[:, 1, :], bcast(A["norm2_g"])).then_inc(gain_loaded[1], 16)
                    for name in CONST_1:
                        act.dma_start(cst[name][:, :], consts[name]).then_inc(const_loaded, 16)
                    for i, name in enumerate(("fox_qn_g", "fox_kn_g", "fox_on_g")):
                        act.dma_start(fxp[:, i, :], bcast(A[name])).then_inc(par_loaded, 16)
                    act.dma_start(forget_b[:, :], bcast(A["fox_forget_b"])).then_inc(par_loaded, 16)
                    act.dma_start(mu[:, :], bcast(A["rw_mu"])).then_inc(par_loaded, 16)
                    for i, name in enumerate(("rw_w0", "rw_a0", "rw_k_k", "rw_k_a", "rw_r_k", "rw_lnx_g", "rw_lnx_b")):
                        act.dma_start(rwp[:, i, :], bcast(A[name])).then_inc(par_loaded, 16)
                    act.dma_start(lora_up[0:DECAY_R, :], A["rw_decay_up"]).then_inc(par_loaded, 16)
                    act.dma_start(lora_up[DECAY_R:P, :], A["rw_iclr_up"]).then_inc(par_loaded, 16)
                    act.dma_start(gate_up[:, 0, :], A["rw_gate_up"][0:P, :]).then_inc(par_loaded, 16)
                    act.dma_start(gate_up[0:GATE_R - P, 1, :], A["rw_gate_up"][P:GATE_R, :]).then_inc(par_loaded, 16)
            for j, (lo, n) in enumerate(FOX_JOBS):
                for t in range(T):
                    lin_copy(J_FOX + j, t, z_fox[:, t, lo:lo + n])
                if lo == 2048:
                    act.wait_ge(lin_evac, after(J_FOX + j, 1))
                    act.activation(fs[:, 0, :].rearrange("p (t h) -> p t h", t=T), z_fox[:, :, 2056:2072],
                                   ACT.Sigmoid).then_inc(fox_gates, 1)
                    act.wait_ge(fox_in, 1)
                    link(act.activation(fs[:, 2, 0:16], fs[:, 1, 0:16], ACT.Abs))
                    link(act.activation(fs[:, 3, 0:16], fs[:, 2, 0:16], ACT.Exp, scale=-1.0))
                    act.activation(fs[:, 4, 0:16], fs[:, 3, 0:16], ACT.Ln, bias=1.0).then_inc(fox_ln, 1)

            def side_copy(j, t):
                if J_RW <= j < J_GATE:
                    lo, n = RW_JOBS[j - J_RW]
                    lin_copy(j, t, z_rw[:, t, lo - FOX_COLS:lo - FOX_COLS + n])
                else:
                    which, h = ((GT, j - J_GATE) if j < J_SHIFT2 else (SH, j - J_SHIFT2) if j < J_GATE1 else
                                (SC, j - J_SCALE2))
                    lin_copy(j, 0, mod[:, which, h * BANK:(h + 1) * BANK])

            for t in range(T):
                side_copy(J_RW, t)
            rstd(fs[:, 6, 0:16], fs[:, 5, 0:16])
            rstd(fs[:, 8, 0:16], fs[:, 7, 0:16])
            for t in range(T):
                side_copy(J_RW + 1, t)
            act.wait_ge(lin_evac, after(J_FOX + 4, 1))
            act.activation(z_fox[:, :, 1536:2048], z_fox[:, :, 1536:2048], ACT.Sigmoid).then_inc(fox_sig, 1)
            act.wait_ge(mod_used, 1)
            for h in range(HEADS):
                act.wait_ge(negmax_ready, h + 1)
                if h >= 2:
                    act.wait_ge(tp_evac, TP_PROB + h - 1)
                act.activation(pr_sb[:, h % 2, 0:P], sc_sb[:, h % 2, 0:P], ACT.Exp,
                               bias=fs[:, 9, 2 * h:2 * h + 1], accum_out=fs[:, 10, 2 * h:2 * h + 1])
                act.activation(pr_sb[:, h % 2, P:3 * P], sc_sb[:, h % 2, P:3 * P], ACT.Exp,
                               bias=fs[:, 9, 2 * h + 1:2 * h + 2], accum_out=fs[:, 10, 2 * h + 1:2 * h + 2])\
                    .then_inc(prob_ready, 1)
                if h < len(FOX_FILL):
                    side_copy(*FOX_FILL[h])
            rstd(fs[:, 6, 0:16], fs[:, 5, 0:16])
            act.wait_ge(lerp_done, 2)
            act.activation(z_rw[:, :, 1536:1600], z_rw[:, :, 1536:1600], ACT.Tanh)
            act.activation(z_rw[:, :, 1664:1824], z_rw[:, :, 1664:1824], ACT.Sigmoid).then_inc(rw_tanh, 1)
            for t in range(T):
                act.wait_ge(lora_in, 2 * t + 1)
                act.activation(logw[:, t, :], logw[:, t, :], ACT.Sigmoid).then_inc(rw_sig, 1)
                act.wait_ge(lora_in, 2 * t + 2)
                act.activation(iclr[:, t, :], iclr[:, t, :], ACT.Sigmoid).then_inc(rw_sig, 1)
            rstd(ws[:, 1, :], ws[:, 0, :])
            for t in range(T):
                act.wait_ge(sc_mm, SC_CUM + t + 1)
                act.activation(rhs_u[:, 0, :], bank[6 + (SC_CUM + t) % 2][:, :], ACT.Exp)
                act.activation(rhs_u[:, 1, :], bank[6 + (SC_CUM + t) % 2][:, :], ACT.Exp, scale=-1.0)\
                    .then_inc(rw_exp, 1)
                act.wait_ge(logw_ready, 2 + t + 1)
                act.activation(y_rw[:, t, :], y_rw[:, t, :], ACT.Exp).then_inc(rw_exp, 1)
                act.wait_ge(til_ready, t + 1)
            act.wait_ge(sc_mm, SC_CUM + 3)
            act.activation(ws[:, 2, 0:4], bank[6 + (SC_CUM + 2) % 2][:, 0:4], ACT.Exp).then_inc(rw_exp, 1)
            for t in range(T):
                side_copy(J_ADA2[t], 0)
                side_copy(J_ADA2[t] + 1, 0)
                act.wait_ge(u_mm, 3 * t + 1)
                act.activation(rhs_u[:, 0, :], bank[2][:, :], ACT.Copy).then_inc(u_evac, 1)
                act.wait_ge(u_mm, 3 * t + 2)
                act.activation(rhs_u[:, 1, :], bank[3][:, :], ACT.Copy).then_inc(u_evac, 1)
                act.wait_ge(u_mm, 3 * t + 3)
                act.activation(y_rw[:, t, :], bank[2][:, :], ACT.Copy).then_inc(u_evac, 1)
                if t == 0:
                    for h in range(2):
                        lin_copy(J_GATE1 + h, 0, tmp[:, h * BANK:(h + 1) * BANK])
            rstd(ws[:, 1, :], ws[:, 0, :])
            act.wait_ge(y_ready, 1)
            act.dma_start(router_w[:, :, :], A["router_w"].rearrange("(k p) n -> p k n", p=P)).then_inc(router_loaded, 16)
            act.dma_start(router_b[:, :], bcast(A["router_bias"])).then_inc(router_loaded, 16)
            act.dma_start(moe_idx[:, :], consts["moe_idx"]).then_inc(router_loaded, 16)
            squares([x[:, 1, :]], [xn[:, 1, :]])
            rstd(small[:, 18:20], small[:, 16:18])
            act.wait_ge(xn_ready, 4)
            for i in range(2):
                act.dma_start(gain_of(i), bcast(A[GAINS[i]])).then_inc(p2_loaded, 16)
            act.wait_ge(sc_mm, SC_ROUTER + 1)
            act.activation(score[:, :, :], bank[6 + SC_ROUTER % 2][:, 0:T * EXPERTS].rearrange("p (t e) -> p t e", t=T),
                           ACT.Sigmoid).then_inc(router_sig, 1)
            for i, name in enumerate(GAINS):
                if i >= 2:
                    act.dma_start(gain_of(i), bcast(A[name])).then_inc(p2_loaded, 16)
            for i, name in enumerate(ROWS):
                act.dma_start(rows2[:, i, :], bcast(A[name])).then_inc(p2_loaded, 16)
            for i in range(3):
                act.dma_start(rows2[:, 3 + i, :], bcast(A["sconv_w_2"][i])).then_inc(p2_loaded, 16)
            act.dma_start(conv_w[:, :, :], A["ffn_conv_w_2"]).then_inc(p2_loaded, 16)
            act.dma_start(conv_b[:, :], A["ffn_conv_b_2"]).then_inc(p2_loaded, 16)
            act.wait_ge(rel_made, 1)
            act.dma_start(rel[0:BUCKETS, :], A["rel_bias_2"]).then_inc(p2_loaded, 16)
            for name in CONST_2:
                act.dma_start(cst[name][:, :], consts[name]).then_inc(p2_loaded, 16)

            for t in range(T):
                act.wait_ge(gu_mm, t + 1)
                act.activation(silu_g[:, t, :], bank[4 + t][:, 0:D_E], ACT.Silu).then_inc(gate_act, 1)
            for t in range(T):
                act.wait_ge(actT_mm, t + 1)
                act.activation(act_eT[:, t, :, :], bank[6 + t][:, 0:D_E].rearrange("p (k c) -> p k c", c=P),
                               ACT.Copy).then_inc(actT_copied, 1)

            def gathered(p):
                act.wait_ge(gu_mm, p + 2)
                for h in range(2):
                    act.wait_ge(gather_mm, p * 2 + h + 1)
                    act.activation(hgT[:, 4 * h:4 * h + 4, :], bank[6 + h][:, :].rearrange("p (k c) -> p k c", c=P),
                                   ACT.Copy).then_inc(gather_copied, 1)

            def put_copy(p, parity):
                act.wait_ge(put_mm, p + 1)
                act.activation(putT[:, parity, :, :], bank[5][:, 2 * P:4 * P].rearrange("p (t c) -> p t c", t=T),
                               ACT.Copy).then_inc(put_copied, 1)

            gathered(0)
            put_copy(0, 0)
            act.wait_ge(quads_ready, 1)
            quads = act.value_load(quads_i[0:1, 0:1], min_val=1, max_val=MAX_QUADS)
            with act.Fori(0, quads) as i:
                for parity in range(2):
                    p = i * 2 + parity
                    act.wait_ge(gu_mm, p + 3)
                    act.activation(silu_g[:, 0, :], bank[4][:, 0:D_E], ACT.Silu).then_inc(gate_act, 1)
                    gathered(p + 1)
                    act.wait_ge(actT_mm, p + 3)
                    act.activation(act_eT[:, 0, :, :], bank[5][:, 0:D_E].rearrange("p (k c) -> p k c", c=P),
                                   ACT.Copy).then_inc(actT_copied, 1)
                    act.wait_ge(spread_mm, p + 3)
                    for h in range(2):
                        act.wait_ge(down_mm, p * 2 + 1 + h)
                        act.activation(y_sb[:, h * BANK:(h + 1) * BANK], bank[6 + h][:, :], ACT.Copy)\
                            .then_inc(y_copied, 1)
                    put_copy(p + 1, 1 - parity)
            act.sem_inc(experts_copied, 1)
            act.wait_ge(hankel_made, 1)
            for h in range(GH):
                row = rel_row[h:h + 1, :]
                act.dma_start(hankel[:, h, :], bass.AP(row.tensor, row.offset, [list(row.ap[0]), [1, P], [1, 2 * P]]))\
                    .then_inc(rel_copied, 16)
            squares([x[:, 1, :]], [xn[:, 1, :]])
            rstd(small[:, 18:20], small[:, 16:18])
            act.wait_ge(x2_ready, 1)
            for t in range(T):
                act.dma_start(mem[t], A["mem_2"][t * P:(t + 1) * P, :]).then_inc(mem_loaded, 16)
            squares([x[:, 1, :]], [xn[:, 1, :]])
            rstd(small[:, 18:20], small[:, 16:18])

            def in_high(u):
                act.wait_ge(in_full[u % 4], (u // 4 + 1) * (32 if u % 2 else 16))
                for q in range(0, UNIT, PIECE):
                    act.activation(of_half(w_high_in, u, q, PIECE), of_half(ring, u, q, PIECE), ACT.Copy)\
                        .then_inc(in_high_made, 1)

            act.wait_ge(tp_evac, TP_IN2 + 4)
            act.activation(xT_high, xT[:, :, :], ACT.Copy).then_inc(x_high_made, 1)
            for t in range(T):
                lin_copy(J_IN2, t, z2[:, t, N_IN2 * BANK:IN2])
            in_high(0)
            in_high(1)
            for i in range(N_IN2):
                if i < N_IN2 - 1:
                    in_high(2 * i + 2)
                    in_high(2 * i + 3)
                if i == 0:
                    rstd(small[:, 18:20], small[:, 16:18])
                for t in range(T):
                    act.wait_ge(lin_mm, after(("in2", i), t))
                    act.activation(z2[:, t, i * BANK:(i + 1) * BANK], bank[lin_bank(outputs[(("in2", i), t)])][:, :],
                                   ACT.Copy).then_inc(lin_evac, 1)
                if i == M_F // BANK:
                    act.wait_ge(lin_evac, after(("in2", i), 1))
                    f = ms[:, 0, :].rearrange("p (t h) -> p t h", t=T)
                    link(act.activation(f, z2[:, :, M_F:M_F + GH], ACT.Abs))
                    link(act.activation(ms[:, 1, :], ms[:, 0, :], ACT.Exp, scale=-1.0))
                    act.activation(ms[:, 2, :], ms[:, 1, :], ACT.Ln, bias=1.0).then_inc(ml_ln, 1)
            act.wait_ge(lin_evac, after(("in2", N_IN2 - 1), 1))
            act.activation(z2[:, :, M_O:M_O + GW], z2[:, :, M_O:M_O + GW], ACT.Sigmoid).then_inc(z2_act, 1)
            act.activation(hg[:, LF, :, :], z2[:, :, H_F:H_F + GW], ACT.Sigmoid)
            act.activation(hg[:, HQ, :, :], z2[:, :, H_Q:H_Q + GW], ACT.Silu)
            act.activation(z2[:, :, H_G:H_G + GW], z2[:, :, H_G:H_G + GW], ACT.Silu).then_inc(hg_act, 1)
            act.wait_ge(m_ready, 1)
            act.activation(ms[:, 8, :], ms[:, 7, :], ACT.Exp, scale=-1.0).then_inc(m_exp, 1)
            for h in range(GH):
                act.wait_ge(d_ready, h + 1)
                if h >= 2:
                    act.wait_ge(w_ready, h - 1)
                act.activation(pr2[:, h % 2, 0:2 * P], sc2[:, h % 2, 0:2 * P], ACT.Exp, bias=ms[:, 5, h:h + 1])
                act.activation(pr2[:, h % 2, 2 * P:3 * P], sc2[:, h % 2, 2 * P:3 * P], ACT.Exp,
                               bias=ms[:, 5, GH + h:GH + h + 1]).then_inc(w_exp, 1)
            act.wait_ge(den_ready, 1)
            act.activation(ms[:, 10, :], ms[:, 9, :], ACT.Abs).then_inc(m_exp, 1)
            for h in range(GH):
                act.wait_ge(d_ready, GH + h + 1)
                if h >= 2:
                    act.wait_ge(tp_evac, TP_P2 + h - 1)
                act.activation(pr2[:, h % 2, 0:P], sc2[:, h % 2, 0:P], ACT.Exp,
                               bias=ms[:, 13, 2 * h:2 * h + 1], accum_out=ms[:, 14, 2 * h:2 * h + 1])
                act.activation(pr2[:, h % 2, P:3 * P], sc2[:, h % 2, P:3 * P], ACT.Exp,
                               bias=ms[:, 13, 2 * h + 1:2 * h + 2], accum_out=ms[:, 14, 2 * h + 1:2 * h + 2])\
                    .then_inc(w_exp, 1)
                if h == 0:
                    act.wait_ge(f_ready, 1)
                    act.activation(rows2[:, 2, :], rows2[:, 2, :], ACT.Exp).then_inc(hg_act, 1)
                    act.wait_ge(f_ready, 2)
                    act.activation(hg[:, LF, :, :], hg[:, LF, :, :], ACT.Ln).then_inc(hg_act, 1)
                elif h == 1:
                    rstd(ms[:, 12, :], ms[:, 11, :])
            for level in range(LEVELS + 1):
                n = SC_HG + 3 * level
                act.wait_ge(sc_mm, n + 1)
                if level >= 2:
                    act.wait_ge(ft_src, level - 1)
                act.activation(ex2[:, level % 2, :], bank[6 + n % 2][:, :], ACT.Exp).then_inc(hg_exp, 1)
                if level in (1, 3):
                    lin_copy_heads(J_CK, level // 2, ckT)
                elif level in (5, 7):
                    lin_copy(J_CV, level // 2 - 2, cv[:, level // 2 - 2, :])
            rstd(ms[:, 17, :], ms[:, 16, :])
            act.wait_ge(y_ready, 2)
            for j in range(2):
                for t in range(T):
                    lin_copy(J_MIX + j, t, hbuf[:, t, j * BANK:(j + 1) * BANK])
            act.wait_ge(lin_evac, after(J_MIX + 1, 1))
            squares([hbuf[:, t, :] for t in range(T)], [xn[:, t, :] for t in range(T)], wait=False)
            rstd(small[:, 18:20], small[:, 16:18])
            squares([x[:, 1, :]], [xn[:, 1, :]])
            rstd(small[:, 18:20], small[:, 16:18])
            for i in range(2):
                lin_copy_heads(J_CQ, i, cqT)
            for h in range(CH):
                act.wait_ge(d_ready, 2 * GH + h + 1)
                if h >= 2:
                    act.wait_ge(tp_evac, TP_PX + h - 1)
                for t in range(T):
                    ins = act.activation(prx[:, h % 2, t, :], scx[:, h % 2, t, :], ACT.Exp, scale=CHD ** -0.5,
                                         bias=cs[:, 0, T * h + t:T * h + t + 1],
                                         accum_out=cs[:, 1, T * h + t:T * h + t + 1])
                ins.then_inc(w_exp, 1)
            act.wait_ge(h_used, 1)
            for i in range(4):
                act.wait_ge(lin_mm, after(J_CO, i))
                act.activation(hbuf[:, i // 2, (i % 2) * BANK:(i % 2 + 1) * BANK],
                               bank[outputs[(J_CO, i)] % 2][:, :], ACT.Copy).then_inc(lin_evac, 1)
            act.wait_ge(lin_evac, after(J_CO, 3))
            squares([hbuf[:, t, :] for t in range(T)], [xn[:, t, :] for t in range(T)], wait=False)
            rstd(small[:, 18:20], small[:, 16:18])
            squares([x[:, 1, :]], [xn[:, 1, :]])
            rstd(small[:, 18:20], small[:, 16:18])
            act.wait_ge(h_used, 3)

            def ffn_silu(i):
                act.wait_ge(conv_done, i + 1)
                if i >= 2:
                    act.wait_ge(act_ready, i - 1)
                act.activation(siluT[:, i % 2, :, :], convT[:, i % 2, :, :], ACT.Silu).then_inc(silu_ready, 1)

            def split_high(u):
                act.wait_ge(unit_full[u % 4], 16 * (u // 4 + 1))
                for q in range(0, UNIT, PIECE):
                    act.activation(of_unit(w_high, u, q, PIECE), of_unit(ring, u, q, PIECE), ACT.Copy)\
                        .then_inc(high_made, 1)

            def act_split_high(i):
                act.wait_ge(act_ready, i + 1)
                act.activation(act_high[:, 2 * i:2 * i + 2, :], actT[:, 2 * i:2 * i + 2, :], ACT.Copy)\
                    .then_inc(act_high_made, 1)

            split_high(0)
            act.wait_ge(tp_evac, TP_FF + 4)
            act.activation(xT_high, xT[:, :, :], ACT.Copy).then_inc(x_high_made, 1)
            split_high(1)
            for i in range(FF_JOBS):
                act.wait_ge(lin_mm, after(J_FFN + i))
                if i >= 2:
                    act.wait_ge(conv_done, i - 1)
                act.activation(gateT[:, i % 2, :, 2:2 + T * P],
                               bank[outputs[(J_FFN + i, 0)] % 2][:, :].rearrange("p (i c) -> p i c", i=2),
                               ACT.Copy).then_inc(lin_evac, 1)
                split_high(2 * i + 2)
                if i:
                    ffn_silu(i - 1)
                if i >= 2:
                    act_split_high(i - 2)
                split_high(2 * i + 3)
            ffn_silu(FF_JOBS - 1)
            act_split_high(FF_JOBS - 2)
            act_split_high(FF_JOBS - 1)
            for u in range(2 * FF_JOBS + 2, len(units)):
                split_high(u)
            for t in range(T):
                act.wait_ge(ffn_mm, 2 * t + 2)
                for h in range(2):
                    ins = act.activation(hbuf_f[:, t, h * BANK:(h + 1) * BANK], bank[2 + 2 * t + h][:, :], ACT.Copy)
                ins.then_inc(x2_ready, 1)
            act.wait_ge(x2_ready, 3)
            squares([hbuf_f[:, t, :] for t in range(T)], [xT[:, 4 * t:4 * t + 4, :].rearrange("p k c -> p (k c)") for t in range(T)], wait=False)
            rstd(small[:, 18:20], small[:, 16:18])

        @block.tensor
        def _(pe):
            full = [0] * RING
            lin_n = [0]
            tp_n = [0]
            sc_n = [0]

            def dense_tile(j, t, lhs, tiles=T, bias=False, part=(0, 1), bank_free=False):
                kind, lo, n, kt, parts, _ = jobs[j]
                if t == 0 and part[0] == 0:
                    full[j % RING] += 16 * len(parts)
                    pe.wait_ge(w_full[j % RING], full[j % RING])
                o = outputs[(j, t)]
                if o >= 2 and part[0] == 0 and not bank_free:
                    pe.wait_ge(lin_evac, o - 1)
                for k in range(kt * part[0] // part[1], kt * (part[0] + 1) // part[1]):
                    mm = pe.matmul(bank[lin_bank(o)][:, 0:n], lhs(k, t), ring[:, j % RING, k * n:(k + 1) * n],
                                   start=(k == 0), stop=(k == kt - 1 and not bias))
                if part[0] < part[1] - 1:
                    return
                if bias:
                    mm = pe.matmul(bank[lin_bank(o)][:, 0:n], ones[0:1, :],
                                   ring[0:1, j % RING, KT * BANK:KT * BANK + n], start=False, stop=True)
                mm.then_inc(lin_mm, 1)
                if t == tiles - 1:
                    pe.wait_ge(lin_mm, outputs[(j, t)] + 1)
                    pe.sem_inc(w_used, 1)

            def dense(j, lhs, tiles=T, bias=False):
                for t in range(tiles):
                    dense_tile(j, t, lhs, tiles, bias)

            def product(out, w, x, start, stop):
                pe.matmul(out, w[0], x[0], start=start, stop=False, skip_group_check=True)
                pe.matmul(out, w[0], x[1], start=False, stop=False, skip_group_check=True)
                return pe.matmul(out, w[1], x[0], start=False, stop=stop, skip_group_check=True)

            def transposes(items):
                n = tp_n[0]
                tp_n[0] += 1
                if n >= 2:
                    pe.wait_ge(tp_evac, n - 1)
                for (lo, hi, rows, src) in items:
                    m = src.shape[0]
                    mm = pe.transpose(bank[4 + n % 2][0:rows, lo:hi], src, cst["ident"][0:m, 0:m])
                mm.then_inc(tp_mm, 1)

            def score_bank():
                n = sc_n[0]
                sc_n[0] += 1
                if n >= 2:
                    pe.wait_ge(sc_evac, n - 1)
                return bank[6 + n % 2]

            def transpose_all(src, kt=KT, layer=None):
                for t in range(T):
                    if layer:
                        pe.wait_ge(xn_ready, T * (layer - 1) + t + 1)
                    for g in range(kt // 4):
                        rows = src[t] if isinstance(src, tuple) else src[:, t, :]
                        transposes([(i * P, (i + 1) * P, P, rows[:, (4 * g + i) * P:(4 * g + i + 1) * P])
                                    for i in range(4)])

            pe.wait_ge(ones_ready, 1)
            pe.wait_ge(cb_ready, 1)
            cb = lambda k, t: silu_c[:, k, :]
            for j in range(4):
                dense(J_ADA1 + j, cb, 1, True)
            pe.wait_ge(const_loaded, 16 * len(CONST_0 + CONST_1))
            transpose_all(xn, layer=1)
            pe.wait_ge(tp_evac, TP_H + 4)
            xTk = lambda k, t: xT[:, k, t * P:(t + 1) * P]
            for j in range(len(FOX_JOBS) + 1):
                dense(J_FOX + j, xTk)

            def side(j, t):
                if j < J_GATE:
                    dense_tile(j, t, xTk)
                else:
                    dense_tile(j, 0, cb, 1, True)

            pe.wait_ge(logf_ready, 1)
            b = score_bank()
            pe.matmul(b[:, 0:8], cst["triu"][:, :], fs[:, 5, 0:8], start=True, stop=True)
            pe.matmul(b[:, 8:16], cst["triu"][:, :], fs[:, 5, 8:16], start=True, stop=False)
            pe.matmul(b[:, 8:16], ones_pp[:, :], fs[:, 5, 0:8], start=False, stop=True).then_inc(sc_mm, 1)
            dense(J_RW + 1, xTk)
            pe.wait_ge(aug_ready, 1)
            for aug in (q_aug, k_aug):
                for hp in range(HEADS // 2):
                    transposes([((2 * i + t) * P, (2 * i + t + 1) * P, AUG, aug[:, t, 2 * hp + i, :])
                                for i in range(2) for t in range(T)])
            pe.wait_ge(tp_evac, TP_AUG + 8)

            def scores(h):
                b = score_bank()
                pe.matmul(b[:, 0:P], q_augT[:, h, 0:P], k_augT[:, h, 0:P], start=True, stop=True)
                pe.matmul(b[:, P:3 * P], q_augT[:, h, P:2 * P], k_augT[:, h, :], start=True, stop=True)\
                    .then_inc(sc_mm, 1)

            def attend(h):
                pe.wait_ge(prob_ready, h + 1)
                transposes([(i * P, (i + 1) * P, P, pr_sb[:, h % 2, i * P:(i + 1) * P]) for i in range(3)])
                pe.wait_ge(tp_evac, TP_PROB + h + 1)
                c = slice(h * HD, (h + 1) * HD)
                v = lambda t: z_fox[:, t, 1024 + h * HD:1024 + (h + 1) * HD]
                pe.matmul(bank[2][:, c], prT[:, h % 2, 0:P], v(0), start=True, stop=True)
                pe.matmul(bank[3][:, c], prT[:, h % 2, P:2 * P], v(0), start=True, stop=False)
                pe.matmul(bank[3][:, c], prT[:, h % 2, 2 * P:3 * P], v(1), start=False, stop=True)\
                    .then_inc(pv_mm, 1)

            scores(0)
            for h in range(HEADS):
                if h + 1 < HEADS:
                    scores(h + 1)
                if h < len(FOX_FILL):
                    side(*FOX_FILL[h])
                attend(h)
            pe.wait_ge(rw_tanh, 1)
            for t in range(T):
                transposes([(0, P, P, z_rw[:, t, 1536:1664]), (P, 2 * P, P, z_rw[:, t, 1664:1792]),
                            (2 * P, 3 * P, GATE_R - P, z_rw[:, t, 1792:1824])])
            pe.wait_ge(par_loaded, 16 * 16)
            pe.wait_ge(tp_evac, TP_LORA + 2)
            for t in range(T):
                c = slice(t * P, (t + 1) * P)
                pe.matmul(score_bank()[:, :], loraT[0:HD, 0, c], lora_up[0:HD, :], start=True, stop=True)\
                    .then_inc(sc_mm, 1)
                pe.matmul(score_bank()[:, :], loraT[HD:P, 0, c], lora_up[HD:P, :], start=True, stop=True)\
                    .then_inc(sc_mm, 1)
                b = score_bank()
                pe.matmul(b[:, :], loraT[:, 1, c], gate_up[:, 0, :], start=True, stop=False)
                pe.matmul(b[:, :], loraT[0:GATE_R - P, 2, c], gate_up[0:GATE_R - P, 1, :], start=False, stop=True)\
                    .then_inc(sc_mm, 1)
            for t in range(T):
                pe.wait_ge(logw_ready, t + 1)
                pe.matmul(score_bank()[:, :], cst["mid"][:, :], logw[:, t, :], start=True, stop=True)\
                    .then_inc(sc_mm, 1)
            b = score_bank()
            for pair in range(4):
                c = slice(pair * P, (pair + 1) * P)
                pe.matmul(b[:, pair:pair + 1], logw[:, 0, c], cst["halves"][:, 0:1], start=True, stop=False)
                mm = pe.matmul(b[:, pair:pair + 1], logw[:, 1, c], cst["halves"][:, 1:2], start=False, stop=True)
            mm.then_inc(sc_mm, 1)
            for t in range(T):
                pe.wait_ge(til_ready, T)
                for pair in range(4):
                    transposes([(i * P, (i + 1) * P, P, til[:, i, t, pair * P:(pair + 1) * P]) for i in range(4)])
                pe.wait_ge(tp_evac, TP_TIL + 4 * t + 4)
                for h in range(HEADS):
                    lo = HD * (h % 2)
                    tt = lambda i, n=1: tilT[lo:lo + HD, h // 2, i:i + n, :]
                    b = score_bank()
                    pe.matmul(b[:, 0:P], tt(BT_), tt(AT_), start=True, stop=True)
                    pe.matmul(b[:, P:2 * P], tt(BT_), tt(RT_), start=True, stop=True)
                    pe.matmul(b[:, 2 * P:3 * P], tt(KTT_), tt(AT_), start=True, stop=True)
                    pe.matmul(b[:, 3 * P:4 * P], tt(KTT_), tt(RT_), start=True, stop=True).then_inc(sc_mm, 1)
                for g in range(2):
                    b = score_bank()
                    for i in range(4):
                        lo = HD * g
                        mm = pe.matmul(b[:, i * P:(i + 1) * P], tilT[lo:lo + HD, i, AT_, :],
                                       tilT[lo:lo + HD, i, BT_, :], start=True, stop=True)
                    mm.then_inc(sc_mm, 1)
                pe.wait_ge(lin_evac, after(J_GATE1 + 1 if t else J_GATE + 1))
                if t == 0:
                    pe.wait_ge(pv_evac, 1)
                else:
                    pe.wait_ge(u_evac, 3)
                for level in range(LEVELS):
                    for g in range(2):
                        slots = range(4 * g, 4 * g + 4)
                        step = (LEVELS * t + level) * 2 + g
                        if level:
                            pe.wait_ge(wkv_upd, step - 1)
                            for i, h in enumerate(slots):
                                mm = pe.matmul(bank[6 + g][:, i * P:(i + 1) * P], gram[:, h, 0, :], inv[:, h, :],
                                               start=True, stop=True)
                            mm.then_inc(wkv_mm, 1)
                        if 1 <= level <= 4:
                            n = 2 * (level - 1) + g
                            dense_tile(J_ADA2[t] + n // 4, 0, cb, 1, True, part=(n % 4, 4))
                        pe.wait_ge(wkv_w, step + 1)
                        for i, h in enumerate(slots):
                            mm = pe.matmul(bank[4 + g][:, i * P:(i + 1) * P], amat[:, h, :], invT[:, h, :],
                                           start=True, stop=True)
                        if 0 < level < LEVELS - 1:
                            for i, h in enumerate(slots):
                                mm = pe.matmul(bank[g][:, i * P:(i + 1) * P], invT[:, h, :], amat[:, h, :],
                                               start=True, stop=True)
                        mm.then_inc(wkv_mm, 1)
                pe.wait_ge(wkv_upd, 2 * LEVELS * (t + 1))
                if t:
                    pe.wait_ge(state_ready, 1)
                V = lambda h: z_rw[:, t, 1024 + h * HD:1024 + (h + 1) * HD]

                def with_state(b, i):
                    if t == 0:
                        return
                    for pair in range(4):
                        pe.matmul(b[:, pair * P:(pair + 1) * P], tilT[:, pair, i, :], stateT[:, pair, :],
                                  start=(pair == 0), stop=False, skip_group_check=True)

                pe.wait_ge(lin_evac, after(J_ADA2[t] + 1))
                with_state(bank[2], AT_)
                for h in range(HEADS):
                    c = slice(h * HD, (h + 1) * HD)
                    mm = pe.matmul(bank[2][:, c], gram[:, slot(h), 2, :], V(h), start=(t == 0), stop=True,
                                   skip_group_check=True)
                mm.then_inc(u_mm, 1)
                if t == 0:
                    dense_tile(J_GATE1, 0, cb, 1, True, part=(0, 2))
                pe.wait_ge(u_evac, 3 * t + 1)
                for h in range(HEADS):
                    c = slice(h * HD, (h + 1) * HD)
                    mm = pe.matmul(bank[3][:, c], invT[:, slot(h), :], rhs_u[:, 0, c], start=True, stop=True)
                mm.then_inc(u_mm, 1)
                if t == 0:
                    dense_tile(J_GATE1, 0, cb, 1, True, part=(1, 2))
                pe.wait_ge(u_evac, 3 * t + 2)
                with_state(bank[2], RT_)
                for h in range(HEADS):
                    c = slice(h * HD, (h + 1) * HD)
                    pe.matmul(bank[2][:, c], gram[:, slot(h), 1, :], rhs_u[:, 1, c], start=(t == 0), stop=False,
                              skip_group_check=True)
                    mm = pe.matmul(bank[2][:, c], gram[:, slot(h), 3, :], V(h), start=False, stop=True,
                                   skip_group_check=True)
                mm.then_inc(u_mm, 1)
                if t == 0:
                    b = score_bank()
                    for pair in range(4):
                        c = slice(pair * P, (pair + 1) * P)
                        pe.matmul(b[:, c], til[:, BT_, 0, c], rhs_u[:, 1, c], start=True, stop=False)
                        mm = pe.matmul(b[:, c], til[:, KTT_, 0, c], z_rw[:, 0, 1024 + pair * P:1024 + (pair + 1) * P],
                                       start=False, stop=True)
                    mm.then_inc(sc_mm, 1)
                    dense(J_GATE1 + 1, cb, 1, True)
            for half in range(2):
                if half:
                    pe.wait_ge(y_ready, 1)
                for t in range(T):
                    transposes([(i * P, (i + 1) * P, P, xn[:, t, (4 * half + i) * P:(4 * half + i + 1) * P])
                                for i in range(4)])
                pe.wait_ge(tp_evac, TP_Y + 2 * half + 2)
                pe.wait_ge(u_evac, 6)
                for j in range(2):
                    for t in range(T):
                        dense_tile(J_OUT + j, t, xTk, part=(half, 2), bank_free=(j == 1))
            pe.sem_inc(mixer_read, 1)
            transpose_all(xn, layer=2)
            pe.wait_ge(tp_evac, TP_H2 + 4)
            pe.wait_ge(router_loaded, 48)
            b = score_bank()
            for t in range(T):
                for k in range(KT):
                    mm = pe.matmul(b[:, t * EXPERTS:(t + 1) * EXPERTS], xTk(k, t), router_w[:, k, :],
                                   start=(k == 0), stop=(k == KT - 1))
            mm.then_inc(sc_mm, 1)
            pe.wait_ge(lin_evac, after(J_OUT + 1, 1))
            pe.wait_ge(sc_evac, SC_ROUTER + 1)

            pe.wait_ge(sh_full, 48)
            for t in range(T):
                for k in range(KT):
                    mm = pe.matmul(bank[4 + t][:, :], xTk(k, t), gu_odd[:, 0, k * BANK:(k + 1) * BANK],
                                   start=(k == 0), stop=(k == KT - 1))
                mm.then_inc(gu_mm, 1)

            mask = rt[:, 2, :, :]
            pe.wait_ge(routed, 1)
            b = score_bank()
            for t in range(T):
                pe.matmul(b[0:EXPERTS, t * P:(t + 1) * P], mask[:, t, :], cst["ident"][:, :], start=True, stop=True)
            pe.matmul(b[0:EXPERTS, 2 * P:3 * P], mask[:, 0, :], cst["triu"][:, :], start=True, stop=True)
            pe.matmul(b[0:EXPERTS, 3 * P:4 * P], mask[:, 1, :], cst["triu"][:, :], start=True, stop=False)
            pe.matmul(b[0:EXPERTS, 3 * P:4 * P], mask[:, 0, :], ones_pp[:, :], start=False, stop=True).then_inc(sc_mm, 1)
            b = score_bank()
            for t in range(T):
                mm = pe.transpose(b[0:EXPERTS, t * P:(t + 1) * P], wts[:, t, :], cst["ident"][:, :])
            mm.then_inc(sc_mm, 1)
            pe.wait_ge(routed, 2)
            b = score_bank()
            pe.matmul(b[0:EXPERTS, 0:1], cst["triu"][0:EXPERTS, 0:EXPERTS], rc[0:EXPERTS, 0:1], start=True, stop=True)
            pe.matmul(b[:, 1:2], ones_pp[0:EXPERTS, :], rc[0:EXPERTS, 0:1], start=True, stop=True).then_inc(sc_mm, 1)
            pe.wait_ge(routed, 3)
            b = score_bank()
            for t in range(T):
                tok = slice(t * P, (t + 1) * P)
                c = slice(t * NC, (t + 1) * NC)
                pe.matmul(b[:, c], rankT[:, tok], of_chunk[:, 0, :], start=True, stop=False)
                pe.matmul(b[:, c], ones_pp[0:EXPERTS, :], of_chunk[:, 1, :], start=False, stop=True)
                c = slice((2 + t) * NC, (3 + t) * NC)
                pe.matmul(b[:, c], wtsT[:, tok], of_chunk[:, 0, :], start=True, stop=True)
            pe.matmul(b[0:1, 4 * NC:5 * NC], expert_no, of_chunk[:, 0, :], start=True, stop=True).then_inc(sc_mm, 1)
            pe.wait_ge(sc_evac, SC_ROUTE + 4)

            for t in range(T):
                pe.wait_ge(act_made, t + 1)
                for i in range(D_E // P):
                    mm = pe.transpose(bank[6 + t][:, i * P:(i + 1) * P], act_e[:, t, i * P:(i + 1) * P],
                                      cst["ident"][:, :])
                mm.then_inc(actT_mm, 1)
            for t in range(T):
                pe.wait_ge(actT_copied, t + 1)
                for h in range(2):
                    for k in range(D_E // P):
                        lo = k * D + h * BANK
                        mm = pe.matmul(bank[2 * t + h][:, :], act_eT[:, t, k, :], dn[:, 2, lo:lo + BANK],
                                       start=(k == 0), stop=False, skip_group_check=True)
                mm.then_inc(spread_mm, 1)

            CHUNKS = (slice(0, CS), slice(CS, 2 * CS))

            def gather(p, parity):
                pe.wait_ge(pick_ready, p * 8 + 8)
                pe.wait_ge(y_copied, p * 2 + 2)
                for k in range(KT):
                    for t in range(T):
                        mm = pe.matmul(bank[6 + k // 4][:, k % 4 * P:(k % 4 + 1) * P], xn[:, t, k * P:(k + 1) * P],
                                       pick[:, parity, t, :], start=(t == 0), stop=(t == T - 1))
                    if k % 4 == 3:
                        mm.then_inc(gather_mm, 1)

            def put_transpose(p, parity):
                pe.wait_ge(actT_copied, p + 2)
                for t in range(T):
                    mm = pe.transpose(bank[5][:, (2 + t) * P:(3 + t) * P], put[:, parity, t, :], cst["ident"][:, :])
                mm.then_inc(put_mm, 1)

            def spread(p, parity, last=False):
                pe.wait_ge(y_copied, p * 2 + 4)
                pe.wait_ge(put_copied, p + 1)
                for t in range(T):
                    for h in range(2):
                        mm = pe.matmul(bank[2 * t + h][:, :], putT[:, 1 - parity, t, :],
                                       y_sb[:, h * BANK:(h + 1) * BANK], start=False, stop=last,
                                       skip_group_check=True)
                return mm

            gather(0, 0)
            put_transpose(0, 0)
            quads = pe.value_load(quads_i[0:1, 0:1], min_val=1, max_val=MAX_QUADS)
            with pe.Fori(0, quads) as i:
                for parity in range(2):
                    p = i * 2 + parity
                    gu_w = (lambda c: ring[:, c, 0:GU_W]) if parity == 0 else (lambda c: gu_odd[:, c, :])
                    pe.wait_ge(gather_copied, p * 2 + 2)
                    pe.wait_ge(act_made, p + 2)
                    pe.wait_ge(gu_full[parity], i * 64 + 64)
                    for k in range(KT):
                        for c in range(2):
                            mm = pe.matmul(bank[4][CHUNKS[c], :], hgT[:, k, CHUNKS[c]],
                                           gu_w(c)[:, k * BANK:(k + 1) * BANK], start=(k == 0), stop=(k == KT - 1))
                    mm.then_inc(gu_mm, 1)
                    gather(p + 1, 1 - parity)
                    pe.wait_ge(put_copied, p + 1)
                    pe.wait_ge(act_made, p + 3)
                    for k in range(D_E // P):
                        mm = pe.transpose(bank[5][:, k * P:(k + 1) * P], act_e[:, 0, k * P:(k + 1) * P],
                                          cst["ident"][:, :])
                    mm.then_inc(actT_mm, 1)
                    spread(p, parity).then_inc(spread_mm, 1)
                    pe.wait_ge(dn_full[parity], i * 32 + 32)
                    pe.wait_ge(actT_copied, p + 3)
                    for h in range(2):
                        pe.wait_ge(gather_copied, p * 2 + 3 + h)
                        for k in range(D_E // P):
                            for c in range(2):
                                lo = k * D + h * BANK
                                mm = pe.matmul(bank[6 + h][CHUNKS[c], :], act_eT[:, 0, k, CHUNKS[c]],
                                               dn[:, 2 * parity + c, lo:lo + BANK], start=(k == 0),
                                               stop=(k == D_E // P - 1))
                        mm.then_inc(down_mm, 1)
                    put_transpose(p + 1, 1 - parity)
            spread(quads * 2, 0, last=True).then_inc(experts_added, 1)
            pe.wait_ge(experts_copied, 1)
            pe.wait_ge(p2_loaded, 16 * N_P2)
            pe.wait_ge(router_sig, 1)
            pe.wait_ge(x2_ready, 1)
            pe.matmul(bank[2][0:GH, 0:3 * P], rel[:, :], cst["bucket"][:, :], start=True, stop=True).then_inc(rel_mm, 1)
            transpose_all(xn, layer=3)
            pe.wait_ge(tp_evac, TP_IN2 + 4)
            dense(J_IN2, xTk, bias=True)
            pe.wait_ge(x_low_made, 1)
            for u in range(2 * N_IN2):
                for t in range(T):
                    o = outputs[(("in2", u // 2), t)]
                    b = bank[lin_bank(o)]
                    if u % 2 == 0:
                        pe.wait_ge(lin_evac, o - 1)
                    for i in range(KT // 2):
                        k = u % 2 * KT // 2 + i
                        if t == 0 and i * BANK % PIECE == 0:
                            pe.wait_ge(in_low_made, u * PIECES + i * BANK // PIECE + 1)
                        mm = product(b[:, :], [a[:, k, t * P:(t + 1) * P] for a in (xT_high, xT_low)],
                                     [of_half(w, u, i * BANK, BANK) for w in (w_high_in, w_low)], k == 0, False)
                    if u % 2:
                        mm = pe.matmul(b[:, :], ones[0:1, :],
                                       ring[0:1, (IN2_SLOT + u // 2) % RING, KT * BANK:KT * BANK + BANK],
                                       start=False, stop=True, skip_group_check=True)
                        mm.then_inc(lin_mm, 1)
                if u % 2:
                    pe.wait_ge(lin_mm, o + 1)
                else:
                    mm.then_inc(in_done, 1)
                    pe.wait_ge(in_done, u // 2 + 1)
                pe.sem_inc(w_used, 1)

            def dense_T_quarter(j, i, quarter):
                h, first = quarter // 2, quarter % 2 * KT // 2
                o = outputs[(j, i)]
                if quarter == 0:
                    if i == 0:
                        full[j % RING] += 16 * len(jobs[j][4])
                        pe.wait_ge(w_full[j % RING], full[j % RING])
                    pe.wait_ge(lin_evac, o - 1)
                for k in range(first, first + KT // 2):
                    lo = k * CW + (2 * i + h) * CHD
                    mm = pe.matmul(bank[o % 2][:, h * 2 * P:(h + 1) * 2 * P], ring[:, j % RING, lo:lo + CHD],
                                   xT[:, k, :], start=(k == 0), stop=(k == KT - 1))
                if quarter == 3:
                    mm.then_inc(lin_mm, 1)
                    if i:
                        pe.wait_ge(lin_mm, o + 1)
                        pe.sem_inc(w_used, 1)

            def keys_values_part(n):
                i, quarter = n // 4, n % 4
                if i < 2:
                    dense_T_quarter(J_CK, i, quarter)
                else:
                    dense_tile(J_CV, i - 2, xTk, part=(quarter, 4))

            pe.wait_ge(ml_logf, 1)
            b = score_bank()
            pe.matmul(b[:, 0:GH], cst["triu"][:, :], ms[:, 3, 0:GH], start=True, stop=True)
            pe.matmul(b[:, GH:2 * GH], cst["triu"][:, :], ms[:, 3, GH:2 * GH], start=True, stop=False)
            pe.matmul(b[:, GH:2 * GH], ones_pp[:, :], ms[:, 3, 0:GH], start=False, stop=True).then_inc(sc_mm, 1)
            transpose_all(mem, layer=4)
            pe.wait_ge(e_ready, 1)
            transposes([(t * P, (t + 1) * P, GH, ms[:, 5, t * GH:(t + 1) * GH]) for t in range(T)])

            def pair_transposes(lo):
                transposes([((2 * pair + t) * P, (2 * pair + t + 1) * P, P, z2[:, t, lo + pair * P:lo + (pair + 1) * P])
                            for pair in range(2) for t in range(T)])

            pair_transposes(M_Q)
            pair_transposes(M_K)
            pe.wait_ge(m_row, 1)
            n = tp_n[0]
            tp_n[0] += 1
            pe.wait_ge(tp_evac, n - 1)
            for t in range(T):
                mm = pe.transpose(bank[4 + n % 2][:, t * GH:(t + 1) * GH], e_row[0:GH, 1, t * P:(t + 1) * P],
                                  cst["ident"][0:GH, 0:GH])
            mm.then_inc(tp_mm, 1)
            pe.wait_ge(tp_evac, TP_ML + 3)

            def head_of(a, h, lo=0, hi=T * P):
                return a[HD * (h % 2):HD * (h % 2) + HD, h // 2, lo:hi]

            def weights(h):
                pe.matmul(score_bank()[:, 0:2 * P], cst["neg_head"][:, h * P:(h + 1) * P], e_row[0:GH, 1, :],
                          start=True, stop=True).then_inc(sc_mm, 1)
                b = score_bank()
                pe.matmul(b[:, 0:2 * P], head_of(kT2, h, 0, P), head_of(qT2, h), start=True, stop=True)
                pe.matmul(b[:, 2 * P:3 * P], head_of(kT2, h, P, 2 * P), head_of(qT2, h, P, 2 * P),
                          start=True, stop=True).then_inc(sc_mm, 1)

            def weighted(h):
                pe.wait_ge(w_ready, h + 1)
                c = slice(h * (HD + 1), (h + 1) * (HD + 1))
                w = lambda i: wT2[:, h % 2, i * P:(i + 1) * P]
                pe.matmul(bank[2][:, c], w(0), v_aug[:, 0, h, :], start=True, stop=True)
                pe.matmul(bank[3][:, c], w(1), v_aug[:, 0, h, :], start=True, stop=False)
                pe.matmul(bank[3][:, c], w(2), v_aug[:, 1, h, :], start=False, stop=True).then_inc(o_mm, 1)

            pe.wait_ge(hankel_made, 1)
            weights(0)
            for h in range(GH):
                if h + 1 < GH:
                    weights(h + 1)
                weighted(h)
            pe.wait_ge(qk_ready, 1)
            pair_transposes(A_Q)
            pair_transposes(A_K)
            pe.wait_ge(rel_copied, 16 * GH)
            pe.wait_ge(tp_evac, TP_MOBA + 2)

            def moba_scores(h):
                b = score_bank()
                pe.matmul(b[:, 0:P], head_of(qT2, h, 0, P), head_of(kT2, h, 0, P), start=True, stop=False)
                pe.matmul(b[:, 0:P], cst["anti"][:, :], hankel[:, h, P:2 * P], start=False, stop=True)
                pe.matmul(b[:, P:3 * P], head_of(qT2, h, P, 2 * P), head_of(kT2, h), start=True, stop=False)
                pe.matmul(b[:, P:3 * P], cst["anti"][:, :], hankel[:, h, :], start=False, stop=True).then_inc(sc_mm, 1)

            def moba_attend(h):
                pe.wait_ge(w_exp, GH + h + 1)
                transposes([(i * P, (i + 1) * P, P, pr2[:, h % 2, i * P:(i + 1) * P]) for i in range(3)])
                pe.wait_ge(tp_evac, TP_P2 + h + 1)
                c = slice(h * HD, (h + 1) * HD)
                v = lambda t: z2[:, t, A_V + h * HD:A_V + (h + 1) * HD]
                w = lambda i: wT2[:, h % 2, i * P:(i + 1) * P]
                pe.matmul(bank[2][:, c], w(0), v(0), start=True, stop=True)
                pe.matmul(bank[3][:, c], w(1), v(0), start=True, stop=False)
                pe.matmul(bank[3][:, c], w(2), v(1), start=False, stop=True).then_inc(o_mm, 1)

            moba_scores(0)
            pe.wait_ge(o_used, 1)
            for h in range(GH):
                if h + 1 < GH:
                    moba_scores(h + 1)
                moba_attend(h)
            pe.wait_ge(hg_act, 3)
            for level in range(LEVELS + 1):
                b = score_bank()
                if level < LEVELS:
                    span = cst["span"][:, level * P:(level + 1) * P]
                    spans = (span, span)
                else:
                    spans = (cst["tril_strict"][:, :], cst["triu"][:, :])
                for t in range(T):
                    mm = pe.matmul(b[:, t * GW:(t + 1) * GW], spans[t], hg[:, LF, t, :], start=True, stop=True)
                mm.then_inc(sc_mm, 1)
                keys_values_part(2 * level)
                pe.wait_ge(ft_src, level + 1)
                transposes([((2 * pair + t) * P, (2 * pair + t + 1) * P, P, hg[:, HS, t, pair * P:(pair + 1) * P])
                            for pair in range(2) for t in range(T)])
                keys_values_part(2 * level + 1)
                pe.wait_ge(tp_evac, TP_HG + level + 1)
                for parity in range(2):
                    b = score_bank()
                    r = slice(HD * parity, HD * parity + HD)
                    for pair in range(2):
                        if level < LEVELS:
                            for t in range(T):
                                i = 2 * pair + t
                                f = fT[r, pair, t * P:(t + 1) * P]
                                mm = pe.matmul(b[:, i * P:(i + 1) * P], f, f, start=True, stop=True)
                        else:
                            mm = pe.matmul(b[:, pair * P:(pair + 1) * P], fT[r, pair, 0:P], fT[r, pair, P:2 * P],
                                           start=True, stop=True)
                    mm.then_inc(sc_mm, 1)
            pe.wait_ge(sc_evac, SC_HG + 3 * (LEVELS + 1))
            pe.wait_ge(o_used, 2)
            for h in range(GH):
                c = slice(h * HD, (h + 1) * HD)
                v = lambda t: z2[:, t, H_I + h * HD:H_I + (h + 1) * HD]
                a = lambda t: at[:, h % 2, 2 * (h // 2) + t, :]
                pe.matmul(bank[2][:, c], a(0), v(0), start=True, stop=True)
                pe.matmul(bank[3][:, c], atx[:, h % 2, h // 2, :], v(0), start=True, stop=False)
                mm = pe.matmul(bank[3][:, c], a(1), v(1), start=False, stop=True)
            mm.then_inc(o_mm, 1)
            pe.wait_ge(y_ready, 2)
            transpose_all(xn)
            pe.wait_ge(tp_evac, TP_Y2 + 4)
            for j in range(2):
                dense(J_MIX + j, xTk)
            transpose_all(xn, layer=5)
            pe.wait_ge(tp_evac, TP_XN + 4)
            for i in range(2):
                for quarter in range(4):
                    dense_T_quarter(J_CQ, i, quarter)
            pe.wait_ge(lin_evac, after(J_CQ, 1))

            def cross_scores(h):
                b = score_bank()
                for t in range(T):
                    mm = pe.matmul(b[:, t * 2 * P:(t + 1) * 2 * P], cqT[:, h, t * P:(t + 1) * P], ckT[:, h, :],
                                   start=True, stop=True)
                mm.then_inc(sc_mm, 1)

            cross_scores(0)
            for h in range(CH):
                if h + 1 < CH:
                    cross_scores(h + 1)
                pe.wait_ge(w_exp, 2 * GH + h + 1)
                transposes([((2 * t + m) * P, (2 * t + m + 1) * P, P, prx[:, h % 2, t, m * P:(m + 1) * P])
                            for t in range(T) for m in range(2)])
                pe.wait_ge(tp_evac, TP_PX + h + 1)
                for t in range(T):
                    for m in range(2):
                        mm = pe.matmul(bank[2 + t][:, h * CHD:(h + 1) * CHD],
                                       prxT[:, h % 2, (2 * t + m) * P:(2 * t + m + 1) * P],
                                       cv[:, m, h * CHD:(h + 1) * CHD], start=(m == 0), stop=(m == 1))
                mm.then_inc(o_mm, 1)
            pe.wait_ge(y_ready, 3)
            transpose_all(xn, CW // P)
            pe.wait_ge(tp_evac, TP_O + 2)
            full[J_CO % RING] += 16
            pe.wait_ge(w_full[J_CO % RING], full[J_CO % RING])
            for t in range(T):
                for h in range(2):
                    o = outputs[(J_CO, 2 * t + h)]
                    pe.wait_ge(lin_evac, o - 1)
                    for k in range(CW // P):
                        lo = k * D + h * BANK
                        mm = pe.matmul(bank[o % 2][:, :], xTk(k, t), ring[:, J_CO % RING, lo:lo + BANK],
                                       start=(k == 0), stop=(k == CW // P - 1))
                    mm.then_inc(lin_mm, 1)
            pe.wait_ge(lin_mm, after(J_CO, 3))
            pe.sem_inc(w_used, 1)
            transpose_all(xn, layer=6)
            pe.wait_ge(tp_evac, TP_FF + 4)
            pe.wait_ge(x_low_made, 2)

            for i in range(FF_JOBS):
                o = outputs[(J_FFN + i, 0)]
                pe.wait_ge(lin_evac, o - 1)
                for part in range(2):
                    u = 2 * i + part
                    b = bank[o % 2] if part == 0 else bank[6 + i % 2]
                    if part and i >= 2:
                        pe.wait_ge(act_ready, i - 1)
                    for half in range(2):
                        for k in range(KT):
                            if half == 0 and k * 256 % PIECE == 0:
                                pe.wait_ge(low_made, u * PIECES + k * 256 // PIECE + 1)
                            mm = product(b[:, half * 2 * P:(half + 1) * 2 * P],
                                         [of_unit(w, u, k * 256 + half * P, P) for w in (w_high, w_low)],
                                         (xT_high[:, k, :], xT_low[:, k, :]), k == 0, k == KT - 1)
                    if part:
                        mm.then_inc(up_mm, 1)
                        pe.wait_ge(up_mm, i + 1)
                    else:
                        mm.then_inc(lin_mm, 1)
                        pe.wait_ge(lin_mm, o + 1)
                    pe.sem_inc(w_used, 1)
            for i in range(0, FT_TILES, 2):
                u = 2 * FF_JOBS + i // 2
                pe.wait_ge(act_low_made, i // 2 + 1)
                for t in range(T):
                    for h in range(2):
                        for k in range(2):
                            if t == h == 0:
                                pe.wait_ge(low_made, u * PIECES + k + 1)
                            mm = product(bank[2 + 2 * t + h][:, :],
                                         [a[:, i + k, t * P:(t + 1) * P] for a in (act_high, act_low)],
                                         [of_unit(w, u, k * D + h * BANK, BANK) for w in (w_high, w_low)],
                                         i + k == 0, i + k == FT_TILES - 1)
                        if i + 2 == FT_TILES:
                            mm.then_inc(ffn_mm, 1)
                if i + 2 < FT_TILES:
                    mm.then_inc(w_done, 1)
                    pe.wait_ge(w_done, i // 2 + 1)
                    pe.sem_inc(w_used, 1)

        @block.gpsimd
        def _(pool):
            n = [0]

            def link(ins):
                n[0] += 1
                ins.then_inc(pool_chain, 1)
                pool.wait_ge(pool_chain, n[0])

            pool.wait_ge(pad_zero, 1)
            pool.wait_ge(lin_evac, after(J_FOX + 1, 1))
            src = z_fox[:, :, 512:1536]
            pool.dma_start(kv_prev[1:P, :, :], src[0:P - 1, :, :]).then_inc(kv_shifted, 16)
            pool.dma_start(kv_prev[0:1, 1, :], src[P - 1:P, 0, :]).then_inc(kv_shifted, 16)
            pool.wait_ge(lin_evac, after(J_RW + 3, 1))
            pool.wait_ge(par_loaded, 16 * 16)
            for i, t in enumerate((1, 0)):
                pool.dma_start(z_prev[1:P, :], z_rw[0:P - 1, t, :]).then_inc(zr_shifted, 16)
                if t:
                    pool.dma_start(z_prev[0:1, :], z_rw[P - 1:P, 0, :]).then_inc(zr_shifted, 16)
                else:
                    link(pool.memset(z_prev[0:1, :], 0.0))
                pool.wait_ge(zr_shifted, 32 if t else 48)
                link(pool.tensor_tensor(z_prev[:, :], z_prev[:, :], z_rw[:, t, :], ALU.subtract))
                link(pool.tensor_tensor(z_prev[:, :], z_prev[:, :], mu[:, :], ALU.mult))
                ins = pool.tensor_tensor(z_rw[:, t, :], z_rw[:, t, :], z_prev[:, :], ALU.add)
                link(ins)
                pool.sem_inc(lerp_done, 1)
            pool.wait_ge(conv_prod, 1)
            pool.dma_start(conv[1:P, 1, :, :], conv[0:P - 1, 0, :, :]).then_inc(conv_shift, 16)
            pool.dma_start(conv[0:1, 1, 1, :], conv[P - 1:P, 0, 0, :]).then_inc(conv_shift, 16)
            pool.dma_start(conv[2:P, 2, :, :], conv[0:P - 2, 0, :, :]).then_inc(conv_shift, 16)
            pool.dma_start(conv[0:2, 2, 1, :], conv[P - 2:P, 0, 0, :]).then_inc(conv_shift, 16)

        @block.vector
        def _(dve):
            chain = [0]

            def link(ins):
                chain[0] += 1
                ins.then_inc(vec_chain, 1)
                dve.wait_ge(vec_chain, chain[0])

            rstd_n = [0]

            def rsqrt_mean(src, dst, n, eps):
                link(dve.tensor_scalar(dst, src, 1.0 / n, eps, ALU.mult, ALU.add))
                dve.reciprocal(dst, dst).then_inc(inv_var, 1)
                rstd_n[0] += 1
                dve.wait_ge(rstd_done, rstd_n[0])

            tp_n = [0]

            def tp_copy(dst, rows, n, split=4):
                g = tp_n[0]
                tp_n[0] += 1
                dve.wait_ge(tp_mm, g + 1)
                src = bank[4 + g % 2][0:rows, 0:n]
                dve.tensor_copy(dst, src.rearrange("p (i c) -> p i c", i=split)).then_inc(tp_evac, 1)

            def untranspose(kt=KT):
                for t in range(T):
                    for g in range(kt // 4):
                        tp_copy(xT[:, 4 * g:4 * g + 4, t * P:(t + 1) * P], P, BANK)

            def heads(ap, n=HEADS):
                return ap.rearrange("p (h d) -> p h d", d=HD)

            def per_head(ap, n=HEADS):
                return ap.unsqueeze(2).broadcast_to([P, n, HD])

            dve.memset(ones_pp[:, :], 1.0)
            dve.memset(ones[:, :], 1.0).then_inc(ones_ready, 1)
            dve.memset(kv_prev[0:1, 0, :], 0.0).then_inc(pad_zero, 1)
            dve.wait_ge(silu_done, 1)
            dve.tensor_copy(silu_c[:, :, :], small[:, KT:2 * KT].unsqueeze(2).broadcast_to([P, KT, P]))\
                .then_inc(cb_ready, 1)
            dve.wait_ge(x_loaded, 16)
            for t in range(T):
                link(dve.tensor_tensor_reduce(tmp[:, :], x[:, t, :], x[:, t, :], 1.0, 0.0, ALU.mult, ALU.add,
                                              small[:, 16 + t:17 + t]))
            rsqrt_mean(small[:, 16:18], small[:, 16:18], D, RMS_EPS)
            dve.wait_ge(gain_loaded[0], 16)
            dve.wait_ge(lin_evac, after(J_ADA1 + 3))
            link(dve.scalar_tensor_tensor(mod[:, SC, :], mod[:, SC, :], 1.0, gain[:, 0, :], ALU.add, ALU.mult))
            for t in range(T):
                link(dve.scalar_tensor_tensor(xn[:, t, :], x[:, t, :], small[:, 18 + t:19 + t], mod[:, SC, :],
                                              ALU.mult, ALU.mult))
                link(dve.tensor_tensor(xn[:, t, :], xn[:, t, :], mod[:, SH, :], ALU.add))
                dve.sem_inc(xn_ready, 1)
            dve.sem_inc(mod_used, 1)
            untranspose()
            dve.wait_ge(par_loaded, 16 * 16)
            dve.wait_ge(lin_evac, after(J_FOX + 2, 1))
            for t in range(T):
                ins = dve.tensor_tensor(fs[:, 1, 8 * t:8 * t + 8], z_fox[:, t, 2048:2056], forget_b[:, :], ALU.add)
            ins.then_inc(fox_in, 1)
            dve.wait_ge(fox_gates, 1)
            dve.wait_ge(kv_shifted, 32)
            for t in range(T):
                kv = z_fox[:, t, 512:1536]
                prev = kv_prev[:, t, :]
                link(dve.tensor_tensor(prev, prev, kv, ALU.subtract))
                link(dve.tensor_tensor(heads(prev), heads(prev), per_head(fs[:, 0, 16 * t:16 * t + 16], 16), ALU.mult))
                link(dve.tensor_tensor(kv, kv, prev, ALU.add))
            dve.wait_ge(fox_ln, 1)
            link(dve.tensor_scalar(fs[:, 1, 0:16], fs[:, 1, 0:16], 0.0, None, ALU.min))
            dve.tensor_tensor(fs[:, 5, 0:16], fs[:, 1, 0:16], fs[:, 4, 0:16], ALU.subtract).then_inc(logf_ready, 1)
            dve.wait_ge(lin_evac, after(J_FOX + 3, 1))
            dve.wait_ge(sc_mm, SC_CUMF + 1)
            link(dve.tensor_copy(fs[:, 1, 0:16], bank[6][:, 0:16]))
            dve.sem_inc(sc_evac, 1)
            for t in range(T):
                qk = z_fox[:, t, 0:1024]
                link(dve.tensor_tensor(kv_prev[:, t, :], qk, qk, ALU.mult))
                link(dve.tensor_reduce(fs[:, 5 + 2 * t, 0:16], heads(kv_prev[:, t, :]), AX.X, ALU.add))
                link(dve.tensor_scalar(fs[:, 5 + 2 * t, 0:16], fs[:, 5 + 2 * t, 0:16], 1.0 / HD, RMS_EPS, ALU.mult, ALU.add))
                rstd_n[0] += 1
                dve.reciprocal(fs[:, 5 + 2 * t, :][:, 0:16], fs[:, 5 + 2 * t, 0:16]).then_inc(inv_var, 1)
            dve.wait_ge(rstd_done, rstd_n[0])
            for t in range(T):
                qk = z_fox[:, t, 0:1024]
                link(dve.tensor_tensor(heads(qk), heads(qk), per_head(fs[:, 6 + 2 * t, 0:16], 16), ALU.mult))
                link(dve.scalar_tensor_tensor(q_aug[:, t, :, 0:HD], heads(z_fox[:, t, 0:W1]), HD ** -0.5,
                                              heads(fxp[:, 0, :]), ALU.mult, ALU.mult))
                link(dve.tensor_tensor(k_aug[:, t, :, 0:HD], heads(z_fox[:, t, W1:2 * W1]), heads(fxp[:, 1, :]), ALU.mult))
                cum = fs[:, 1, 8 * t:8 * t + 8].unsqueeze(2)
                link(dve.tensor_copy(q_aug[:, t, :, HD:HD + 1], cum))
                link(dve.memset(q_aug[:, t, :, HD + 1:HD + 2], 1.0))
                link(dve.memset(k_aug[:, t, :, HD:HD + 1], 1.0))
                link(dve.tensor_scalar(k_aug[:, t, :, HD + 1:HD + 2], cum, -1.0, None, ALU.mult))
            dve.sem_inc(aug_ready, 1)
            for dst in (q_augT, k_augT):
                for hp in range(HEADS // 2):
                    g = tp_n[0]
                    tp_n[0] += 1
                    dve.wait_ge(tp_mm, g + 1)
                    dve.tensor_copy(dst[:, 2 * hp:2 * hp + 2, :],
                                    bank[4 + g % 2][0:AUG, :].rearrange("p (h c) -> p h c", h=2)).then_inc(tp_evac, 1)

            def prob_copy(h):
                g = tp_n[0]
                tp_n[0] += 1
                dve.wait_ge(tp_mm, g + 1)
                if h >= 2:
                    dve.wait_ge(pv_mm, h - 1)
                dve.tensor_copy(prT[:, h % 2, :], bank[4 + g % 2][:, 0:3 * P]).then_inc(tp_evac, 1)

            for h in range(HEADS):
                n = SC_FOX + h
                dve.wait_ge(sc_mm, n + 1)
                if h >= 2:
                    dve.wait_ge(prob_ready, h - 1)
                dve.tensor_tensor(sc_sb[:, h % 2, :], bank[6 + n % 2][:, 0:3 * P], cst["causal"][:, :], ALU.add)\
                    .then_inc(sc_evac, 1)
                dve.wait_ge(sc_evac, n + 1)
                dve.tensor_reduce(fs[:, 9, 2 * h:2 * h + 1], sc_sb[:, h % 2, 0:P], AX.X, ALU.max, negate=True)
                dve.tensor_reduce(fs[:, 9, 2 * h + 1:2 * h + 2], sc_sb[:, h % 2, P:3 * P], AX.X, ALU.max, negate=True)\
                    .then_inc(negmax_ready, 1)
                if h:
                    prob_copy(h - 1)
            prob_copy(HEADS - 1)
            dve.wait_ge(prob_ready, HEADS)
            link(dve.reciprocal(fs[:, 11, 0:16], fs[:, 10, 0:16]))
            dve.wait_ge(pv_mm, HEADS)
            dve.wait_ge(fox_sig, 1)
            inv_sum = fs[:, 11, 0:16].rearrange("p (h t) -> p t h", t=T)
            for t in range(T):
                o = xn[:, t, 0:W1]
                link(dve.tensor_tensor(heads(o), heads(bank[2 + t][:, :]), per_head(inv_sum[:, t, :]), ALU.mult))
                link(dve.tensor_tensor(kv_prev[:, t, 0:W1], o, o, ALU.mult))
                link(dve.tensor_reduce(fs[:, 5, 8 * t:8 * t + 8], heads(kv_prev[:, t, 0:W1]), AX.X, ALU.add))
            dve.sem_inc(pv_evac, 1)
            rsqrt_mean(fs[:, 5, 0:16], fs[:, 5, 0:16], HD, RMS_EPS)
            for t in range(T):
                o = xn[:, t, 0:W1]
                link(dve.tensor_tensor(heads(o), heads(o), per_head(fs[:, 6, 8 * t:8 * t + 8]), ALU.mult))
                link(dve.tensor_tensor(o, o, fxp[:, 2, :], ALU.mult))
                link(dve.tensor_tensor(o, o, z_fox[:, t, 1536:2048], ALU.mult))
            for t in range(T):
                g = tp_n[0]
                tp_n[0] += 1
                dve.wait_ge(tp_mm, g + 1)
                dve.tensor_copy(loraT[:, 0:2, t * P:(t + 1) * P],
                                bank[4 + g % 2][:, 0:2 * P].rearrange("p (i c) -> p i c", i=2))
                dve.tensor_copy(loraT[0:GATE_R - P, 2, t * P:(t + 1) * P], bank[4 + g % 2][0:GATE_R - P, 2 * P:3 * P])\
                    .then_inc(tp_evac, 1)
            for t in range(T):
                n = SC_LORA + 3 * t
                b = lambda i: bank[6 + (n + i) % 2][:, :]
                dve.wait_ge(sc_mm, n + 1)
                link(dve.tensor_tensor(logw[:, t, :], b(0), rwp[:, W0, :], ALU.add))
                dve.sem_inc(sc_evac, 1)
                dve.sem_inc(lora_in, 1)
                dve.wait_ge(sc_mm, n + 2)
                link(dve.tensor_tensor(iclr[:, t, :], b(1), rwp[:, A0, :], ALU.add))
                dve.sem_inc(sc_evac, 1)
                dve.sem_inc(lora_in, 1)
                dve.wait_ge(sc_mm, n + 3)
                dve.tensor_copy(gate[:, t, :], b(2)).then_inc(sc_evac, 1)
            dve.wait_ge(lerp_done, 2)
            R = lambda t: z_rw[:, t, 0:W1]
            K = lambda t: z_rw[:, t, W1:2 * W1]
            for t in range(T):
                link(dve.tensor_tensor(til[:, AT_, t, :], K(t), rwp[:, KK_, :], ALU.mult))
                link(dve.tensor_tensor(til[:, RT_, t, :], til[:, AT_, t, :], til[:, AT_, t, :], ALU.mult))
                link(dve.tensor_reduce(ws[:, 0, 8 * t:8 * t + 8], heads(til[:, RT_, t, :]), AX.X, ALU.add))
            link(dve.tensor_scalar(ws[:, 0, :], ws[:, 0, :], 1e-24, None, ALU.max))
            dve.reciprocal(ws[:, 0, :], ws[:, 0, :]).then_inc(inv_var, 1)
            rstd_n[0] += 1
            dve.wait_ge(rstd_done, rstd_n[0])
            for t in range(T):
                dve.wait_ge(rw_sig, 2 * t + 1)
                link(dve.tensor_scalar(logw[:, t, :], logw[:, t, :], -math.exp(-0.5), None, ALU.mult))
                dve.sem_inc(logw_ready, 1)
            for t in range(T):
                dve.wait_ge(rw_sig, 2 * t + 2)
                kk = til[:, AT_, t, :]
                link(dve.scalar_tensor_tensor(heads(kk), heads(kk), -1.0, per_head(ws[:, 1, 8 * t:8 * t + 8]),
                                              ALU.mult, ALU.mult))
                link(dve.scalar_tensor_tensor(til[:, BT_, t, :], kk, -1.0, iclr[:, t, :], ALU.mult, ALU.mult))
                link(dve.scalar_tensor_tensor(iclr[:, t, :], iclr[:, t, :], -1.0, rwp[:, KA_, :], ALU.add, ALU.mult))
                link(dve.scalar_tensor_tensor(K(t), iclr[:, t, :], 1.0, K(t), ALU.add, ALU.mult))
                link(dve.tensor_tensor(til[:, RT_, t, :], R(t), K(t), ALU.mult))
                link(dve.tensor_tensor(til[:, RT_, t, :], til[:, RT_, t, :], rwp[:, RK_, :], ALU.mult))
                link(dve.tensor_reduce(ws[:, 3, 8 * t:8 * t + 8], heads(til[:, RT_, t, :]), AX.X, ALU.add))
            for t in range(T):
                n = SC_CUM + t
                dve.wait_ge(rw_exp, 2 * t + 1)
                link(dve.tensor_tensor(y_rw[:, t, :], bank[6 + n % 2][:, :], logw[:, t, :], ALU.subtract))
                dve.sem_inc(logw_ready, 1)
                dve.sem_inc(sc_evac, 1)
                link(dve.tensor_tensor(til[:, RT_, t, :], R(t), rhs_u[:, 0, :], ALU.mult))
                link(dve.tensor_tensor(til[:, BT_, t, :], til[:, BT_, t, :], rhs_u[:, 1, :], ALU.mult))
                link(dve.tensor_tensor(til[:, KTT_, t, :], K(t), rhs_u[:, 1, :], ALU.mult))
                dve.wait_ge(rw_exp, 2 * t + 2)
                link(dve.tensor_tensor(til[:, AT_, t, :], til[:, AT_, t, :], y_rw[:, t, :], ALU.mult))
                dve.sem_inc(til_ready, 1)
            dve.wait_ge(rw_exp, 5)
            dve.sem_inc(sc_evac, 1)
            level_mask = lambda l: cst["level"][:, l * P:(l + 1) * P].unsqueeze(1).broadcast_to([P, 4, P])
            ident4 = cst["ident"][:, :].unsqueeze(1).broadcast_to([P, 4, P])
            four = lambda b: b[:, :].rearrange("p (i c) -> p i c", i=4)
            for t in range(T):
                for pair in range(4):
                    tp_copy(tilT[:, pair, :, :], P, BANK)
                base = SC_GRAM + 11 * t
                for h in range(HEADS):
                    n = base + h
                    dve.wait_ge(sc_mm, n + 1)
                    dve.tensor_tensor(gram[:, slot(h), :, :], four(bank[6 + n % 2]),
                                      cst["wkv_mask"][:, :].rearrange("p (i c) -> p i c", i=4), ALU.mult)\
                        .then_inc(sc_evac, 1)
                for level in range(LEVELS):
                    for g in range(2):
                        hs = slice(4 * g, 4 * g + 4)
                        if level == 0:
                            n = base + HEADS + g
                            dve.wait_ge(sc_mm, n + 1)
                            link(dve.tensor_tensor(amat[:, hs, :], four(bank[6 + n % 2]), level_mask(0), ALU.mult))
                            dve.sem_inc(sc_evac, 1)
                            link(dve.tensor_tensor(inv[:, hs, :], amat[:, hs, :], ident4, ALU.add))
                            link(dve.tensor_copy(invT[:, hs, :], ident4))
                            dve.sem_inc(wkv_w, 1)
                        else:
                            dve.wait_ge(wkv_mm, wkv_count(t, level, g, 0))
                            dve.tensor_tensor(amat[:, hs, :], four(bank[6 + g]), level_mask(level), ALU.mult)\
                                .then_inc(wkv_w, 1)
                    for g in range(2):
                        hs = slice(4 * g, 4 * g + 4)
                        dve.wait_ge(wkv_mm, wkv_count(t, level, g, 1))
                        ins = dve.tensor_tensor(invT[:, hs, :], invT[:, hs, :], four(bank[4 + g]), ALU.add)
                        if 0 < level < LEVELS - 1:
                            ins = dve.tensor_tensor(inv[:, hs, :], inv[:, hs, :], four(bank[g]), ALU.add)
                        link(ins)
                        dve.sem_inc(wkv_upd, 1)
                if t == 0:
                    n = base + HEADS + 2
                    dve.wait_ge(sc_mm, n + 1)
                    for pair in range(4):
                        link(dve.scalar_tensor_tensor(stateT[:, pair, :], bank[6 + n % 2][:, pair * P:(pair + 1) * P],
                                                      ws[:, 2, pair:pair + 1], cst["pairs"][:, :], ALU.mult, ALU.mult))
                    dve.sem_inc(sc_evac, 1)
                    dve.sem_inc(state_ready, 1)
            def mixed_half(half):
                for t in range(T):
                    tp_copy(xT[:, 4 * half:4 * half + 4, t * P:(t + 1) * P], P, BANK)

            for t in range(T):
                if t:
                    mixed_half(0)
                dve.wait_ge(u_evac, 3 * t + 3)
                y = y_rw[:, t, :]
                link(dve.tensor_reduce(ws[:, 4, 8 * t:8 * t + 8], heads(y), AX.X, ALU.add))
                link(dve.tensor_scalar(ws[:, 4, 8 * t:8 * t + 8], ws[:, 4, 8 * t:8 * t + 8], 1.0 / HD, None, ALU.mult))
                link(dve.tensor_tensor(heads(y), heads(y), per_head(ws[:, 4, 8 * t:8 * t + 8]), ALU.subtract))
                link(dve.tensor_tensor(iclr[:, t, :], y, y, ALU.mult))
                link(dve.tensor_reduce(ws[:, 0, 8 * t:8 * t + 8], heads(iclr[:, t, :]), AX.X, ALU.add))
            rsqrt_mean(ws[:, 0, :], ws[:, 0, :], HD, LNX_EPS)
            for t in range(T):
                y = y_rw[:, t, :]
                link(dve.tensor_tensor(heads(y), heads(y), per_head(ws[:, 1, 8 * t:8 * t + 8]), ALU.mult))
                link(dve.tensor_tensor(y, y, rwp[:, LG, :], ALU.mult))
                link(dve.tensor_tensor(y, y, rwp[:, LB, :], ALU.add))
                link(dve.tensor_tensor(heads(iclr[:, t, :]), heads(z_rw[:, t, 1024:1536]),
                                       per_head(ws[:, 3, 8 * t:8 * t + 8]), ALU.mult))
                link(dve.tensor_tensor(y, y, iclr[:, t, :], ALU.add))
                link(dve.tensor_tensor(xn[:, t, W1:2 * W1], y, gate[:, t, :], ALU.mult))
            dve.sem_inc(y_ready, 1)
            link(dve.memset(rel[:, :], MASKED))
            dve.sem_inc(rel_made, 1)
            mixed_half(1)
            dve.wait_ge(gain_loaded[1], 16)
            dve.wait_ge(lin_evac, after(J_SCALE2 + 1))
            link(dve.scalar_tensor_tensor(mod[:, SC, :], mod[:, SC, :], 1.0, gain[:, 1, :], ALU.add, ALU.mult))
            for j in range(2):
                for t in range(T):
                    o = outputs[(J_OUT + j, t)]
                    c = slice(j * BANK, (j + 1) * BANK)
                    dve.wait_ge(lin_mm, o + 1)
                    dve.tensor_tensor(xn[:, t, c], bank[lin_bank(o)][:, :], tmp[:, c], ALU.mult).then_inc(lin_evac, 1)
                    dve.wait_ge(lin_evac, o + 1)
                    link(dve.tensor_tensor(x[:, t, c], x[:, t, c], xn[:, t, c], ALU.add))
            def sum_squares(dst, src):
                link(dve.tensor_tensor_reduce(tmp[:, :], src, src, 1.0, 0.0, ALU.mult, ALU.add, dst))

            asked = [0]

            def sums_of_squares(rows, by_act):
                if by_act == 1:
                    dve.sem_inc(sq_ask, 1)
                for t in range(T - by_act):
                    sum_squares(small[:, 16 + t:17 + t], rows(t))
                asked[0] += by_act
                if by_act:
                    dve.wait_ge(sq_done, asked[0])

            sums_of_squares(lambda t: x[:, t, :], 1)
            rsqrt_mean(small[:, 16:18], small[:, 16:18], D, RMS_EPS)
            for t in range(T):
                link(dve.scalar_tensor_tensor(xn[:, t, :], x[:, t, :], small[:, 18 + t:19 + t], mod[:, SC, :],
                                              ALU.mult, ALU.mult))
                link(dve.tensor_tensor(xn[:, t, :], xn[:, t, :], mod[:, SH, :], ALU.add))
                dve.sem_inc(xn_ready, 1)
            untranspose()
            dve.wait_ge(router_loaded, 48)
            dve.wait_ge(router_sig, 1)
            dve.sem_inc(sc_evac, 1)
            best8, group, picked, eq, cum, masked = (rt[:, i, :, :] for i in range(6))

            def top(values, n, k, mask):
                for t in range(T):
                    dve.max(best8[:, t, 0:8], values[:, t, 0:n])
                link(dve.memset(cum[:, :, :], 1.0))
                for t in range(T):
                    v, least = values[:, t, 0:n], best8[:, t, k - 1:k]
                    link(dve.tensor_scalar(mask[:, t, 0:n], v, least, None, ALU.is_gt))
                    link(dve.tensor_reduce(best8[:, t, 8:9], mask[:, t, 0:n], AX.X, ALU.add))
                    link(dve.tensor_scalar(best8[:, t, 8:9], best8[:, t, 8:9], -1.0, float(k), ALU.mult, ALU.add))
                    link(dve.tensor_scalar(eq[:, t, 0:n], v, least, None, ALU.is_equal))
                    link(dve.tensor_tensor_scan(cum[:, t, 0:n], cum[:, t, 0:n], eq[:, t, 0:n], 0.0, ALU.mult, ALU.add))
                    link(dve.scalar_tensor_tensor(eq[:, t, 0:n], cum[:, t, 0:n], best8[:, t, 8:9], eq[:, t, 0:n],
                                                  ALU.is_le, ALU.mult))
                    link(dve.tensor_tensor(mask[:, t, 0:n], mask[:, t, 0:n], eq[:, t, 0:n], ALU.add))

            link(dve.tensor_tensor(sel[:, :, :], score[:, :, :], router_b[:, :].unsqueeze(1).broadcast_to([P, T, EXPERTS]),
                                   ALU.add))
            for t in range(T):
                for g in range(GROUPS):
                    c = slice(g * GROUP_SIZE, (g + 1) * GROUP_SIZE)
                    link(dve.max(picked[:, t, c], sel[:, t, c]))
            best = picked.rearrange("p t (g i) -> p t g i", i=GROUP_SIZE)
            link(dve.tensor_tensor(group[:, :, 0:GROUPS].unsqueeze(3), best[:, :, :, 0:1], best[:, :, :, 1:2], ALU.add))
            top(group, GROUPS, TOP_GROUPS, picked)
            for t in range(T):
                gmask = picked[:, t, 0:GROUPS]
                link(dve.tensor_scalar(group[:, t, 0:GROUPS], gmask, -MASKED, MASKED, ALU.mult, ALU.add))
                by_group = lambda a: a.rearrange("p (g i) -> p g i", i=GROUP_SIZE)
                wide = lambda a: a.unsqueeze(2).broadcast_to([P, GROUPS, GROUP_SIZE])
                link(dve.tensor_tensor(by_group(masked[:, t, :]), by_group(sel[:, t, :]), wide(gmask), ALU.mult))
                link(dve.tensor_tensor(by_group(masked[:, t, :]), by_group(masked[:, t, :]),
                                       wide(group[:, t, 0:GROUPS]), ALU.add))
            top(masked, EXPERTS, TOP_K, picked)
            for t in range(T):
                link(dve.tensor_tensor(wts[:, t, :], score[:, t, :], picked[:, t, :], ALU.mult))
                link(dve.tensor_reduce(best8[:, t, 9:10], wts[:, t, :], AX.X, ALU.add))
                link(dve.reciprocal(best8[:, t, 9:10], best8[:, t, 9:10]))
                link(dve.tensor_scalar(wts[:, t, :], wts[:, t, :], best8[:, t, 9:10], ROUTED_SCALE, ALU.mult, ALU.mult))

            dve.sem_inc(routed, 1)
            for t in range(T):
                dve.wait_ge(gate_act, t + 1)
                dve.tensor_tensor(act_e[:, t, :], silu_g[:, t, :], bank[4 + t][:, D_E:2 * D_E], ALU.mult)\
                    .then_inc(act_made, 1)
            n = SC_ROUTE
            dve.wait_ge(sc_mm, n + 1)
            ranks = bank[6 + n % 2]
            link(dve.tensor_copy(maskT[:, :], ranks[0:EXPERTS, 0:T * P]))
            link(dve.tensor_scalar(rc[0:EXPERTS, 4:4 + len(TH)], thresholds, ranks[0:EXPERTS, 4 * P - 1:4 * P], None,
                                   ALU.is_lt))
            link(dve.tensor_reduce(rc[0:EXPERTS, 0:1], rc[0:EXPERTS, 4:4 + len(TH)], AX.X, ALU.add))
            dve.sem_inc(routed, 1)
            link(dve.scalar_tensor_tensor(rankT[:, :], ranks[0:EXPERTS, T * P:2 * T * P], UNMATCHED, maskT[:, :],
                                          ALU.add, ALU.mult))
            link(dve.tensor_scalar(rankT[:, :], rankT[:, :], -UNMATCHED, None, ALU.add))
            dve.sem_inc(sc_evac, 1)
            dve.wait_ge(sc_mm, n + 2)
            link(dve.tensor_copy(wtsT[:, :], bank[6 + (n + 1) % 2][0:EXPERTS, 0:T * P]))
            dve.sem_inc(sc_evac, 1)
            dve.wait_ge(sc_mm, n + 3)
            link(dve.tensor_copy(rc[0:EXPERTS, 2:3], bank[6 + (n + 2) % 2][0:EXPERTS, 0:1]))
            link(dve.tensor_copy(rc[:, 3:4], bank[6 + (n + 2) % 2][:, 1:2]))
            dve.sem_inc(sc_evac, 1)
            link(dve.tensor_tensor(rc[0:EXPERTS, 1:2], rc[0:EXPERTS, 2:3], rc[0:EXPERTS, 0:1], ALU.subtract))
            mine, minus = of_chunk[:, 0, :], of_chunk[:, 1, :]
            link(dve.tensor_scalar(mine, chunk_no[0:EXPERTS, :], rc[0:EXPERTS, 1:2], None, ALU.is_ge))
            link(dve.scalar_tensor_tensor(mine, chunk_no[0:EXPERTS, :], rc[0:EXPERTS, 2:3], mine, ALU.is_lt, ALU.mult))
            link(dve.scalar_tensor_tensor(minus, chunk_no[0:EXPERTS, :], rc[0:EXPERTS, 1:2], mine, ALU.subtract,
                                          ALU.mult))
            link(dve.tensor_scalar(minus, minus, -float(CS), None, ALU.mult))
            dve.sem_inc(routed, 1)
            first_of_quad = chunk_no[:, 0:NC].rearrange("p (q c) -> p q c", c=4)[:, :, 0]
            link(dve.tensor_scalar(mod[:, SC, 0:NC // 4], first_of_quad, rc[:, 3:4], None, ALU.is_lt))
            link(dve.tensor_reduce(rc[:, 8:9], mod[:, SC, 0:NC // 4], AX.X, ALU.add))
            link(dve.tensor_copy(quads_i[:, :], rc[0:1, 8:9]))
            dve.wait_ge(sc_mm, n + 4)
            tables = bank[6 + (n + 3) % 2]
            link(dve.tensor_copy(expert_of[:, :], tables[0:1, 4 * NC:5 * NC]))
            link(dve.tensor_copy(place[:, :, :], tables[:, 0:2 * NC].rearrange("p (t c) -> p t c", t=T)))
            link(dve.tensor_copy(weight[:, :, :], tables[:, 2 * NC:4 * NC].rearrange("p (t c) -> p t c", t=T)))
            dve.sem_inc(sc_evac, 1)
            dve.sem_inc(quads_ready, 1)

            def make_pick(p, parity):
                for t in range(T):
                    for c in range(2):
                        at_chunk = bass.ds(p * 2 + c, 1)
                        dve.tensor_scalar(pick[:, parity, t, c * CS:(c + 1) * CS], slot_no, place[:, t, at_chunk],
                                          None, ALU.is_equal).then_inc(pick_ready, 1)
                        dve.tensor_scalar(put[:, parity, t, c * CS:(c + 1) * CS], slot_no, place[:, t, at_chunk],
                                          weight[:, t, at_chunk], ALU.is_equal, ALU.mult).then_inc(pick_ready, 1)

            link(dve.memset(y_sb, 0.0))
            link(dve.memset(putT[:, 1, :, :], 0.0))
            dve.sem_inc(y_copied, 4)
            make_pick(0, 0)
            make_pick(1, 1)
            quads = dve.value_load(quads_i[0:1, 0:1], min_val=1, max_val=MAX_QUADS)
            with dve.Fori(0, quads) as i:
                for parity in range(2):
                    p = i * 2 + parity
                    dve.wait_ge(gate_act, p + 3)
                    dve.wait_ge(actT_mm, p + 2)
                    dve.tensor_tensor(act_e[:, 0, :], silu_g[:, 0, :], bank[4][:, D_E:2 * D_E], ALU.mult)\
                        .then_inc(act_made, 1)
                    dve.wait_ge(put_mm, p + 1)
                    make_pick(p + 2, parity)
            dve.wait_ge(experts_added, 1)
            for t in range(T):
                for h in range(2):
                    c = slice(h * BANK, (h + 1) * BANK)
                    link(dve.tensor_tensor(tmp[:, c], bank[2 * t + h][:, :], mod[:, GT, c], ALU.mult))
                link(dve.tensor_tensor(x[:, t, :], x[:, t, :], tmp[:, :], ALU.add))
            dve.sem_inc(x2_ready, 1)

            FINAL, MIX_PRE, MIX_POST, MEM, CROSS_PRE, CROSS_POST, FFN_PRE, FFN_POST = range(8)

            def norm_into(dst, src, g, by_act=1, ready=None):
                rows = lambda a, t: a[t] if isinstance(a, tuple) else a[:, t, :]
                sums_of_squares(lambda t: rows(src, t), by_act)
                rsqrt_mean(small[:, 16:18], small[:, 16:18], D, RMS_EPS)
                for t in range(T):
                    link(dve.scalar_tensor_tensor(rows(dst, t), rows(src, t), small[:, 18 + t:19 + t],
                                                  gain_of(g), ALU.mult, ALU.mult))
                    if ready is not None:
                        dve.sem_inc(ready, 1)

            def add_normed(src, g):
                norm_into(src, src, g, by_act=2)
                for t in range(T):
                    link(dve.tensor_tensor(x[:, t, :], x[:, t, :], src[:, t, :], ALU.add))

            dve.wait_ge(rel_mm, 1)
            link(dve.tensor_copy(rel_row[:, :], bank[2][0:GH, 0:3 * P]))
            dve.sem_inc(hankel_made, 1)
            dve.wait_ge(p2_loaded, 16 * N_P2)
            norm_into(x, x, FINAL)
            norm_into(xn, x, MIX_PRE, ready=xn_ready)
            untranspose()

            def in_low(u):
                for q in range(PIECES):
                    dve.wait_ge(in_high_made, u * PIECES + q + 1)
                    at_piece = lambda a: of_half(a, u, q * PIECE, PIECE)
                    dve.tensor_tensor(at_piece(w_low), at_piece(ring), at_piece(w_high_in).bitcast(F32), ALU.subtract)\
                        .then_inc(in_low_made, 1)

            dve.wait_ge(x_high_made, 1)
            dve.wait_ge(lin_mm, after(J_IN2, 1))
            dve.tensor_tensor(xT_low[:, :, :], xT[:, :, :], xT_high.bitcast(F32), ALU.subtract).then_inc(x_low_made, 1)
            for u in range(4):
                in_low(u)
            dve.wait_ge(mem_loaded, 32)
            norm_into(mem, mem, MEM, by_act=0, ready=xn_ready)
            col = lambda i: ms[:, i, :].rearrange("p (t h) -> p t h", t=T)
            link(dve.memset(conv[:, :, 0, :], 0.0))
            for u in range(4, 2 * N_IN2):
                in_low(u)
                if u == 2 * (M_F // BANK + 2) + 1:
                    dve.wait_ge(ml_ln, 1)
                    link(dve.tensor_scalar(col(3), z2[:, :, M_F:M_F + GH], 0.0, None, ALU.min))
                    link(dve.tensor_tensor(ms[:, 3, :], ms[:, 3, :], ms[:, 2, :], ALU.subtract))
                    dve.sem_inc(ml_logf, 1)
            dve.wait_ge(sc_mm, SC_G2 + 1)
            link(dve.tensor_copy(ms[:, 4, :], bank[6 + SC_G2 % 2][:, 0:T * GH]))
            dve.sem_inc(sc_evac, 1)
            link(dve.tensor_tensor(col(5), z2[:, :, M_I:M_I + GH], col(4), ALU.subtract))
            dve.sem_inc(e_ready, 1)
            untranspose()

            def next_tp():
                g = tp_n[0]
                tp_n[0] += 1
                dve.wait_ge(tp_mm, g + 1)
                return bank[4 + g % 2]

            def pair_copy(dst):
                dve.tensor_copy(dst[:, :, :], next_tp()[:, :].rearrange("p (i c) -> p i c", i=2)).then_inc(tp_evac, 1)

            link(dve.tensor_copy(e_row[:, 0, :], next_tp()[0:GH, 0:T * P]))
            dve.sem_inc(tp_evac, 1)
            link(dve.tensor_tensor_scan(e_row[:, 1, :], e_row[:, 0, :], e_row[:, 0, :], 0.0, ALU.max, ALU.max))
            dve.sem_inc(m_row, 1)
            pair_copy(qT2)
            pair_copy(kT2)
            dve.wait_ge(lin_evac, after(("in2", (C_H + GW - 1) // BANK), 1))
            link(dve.tensor_tensor(conv[:, 0, :, :], z2[:, :, C_C:C_C + GW], z2[:, :, C_H:C_H + GW], ALU.mult))
            dve.sem_inc(conv_prod, 1)
            link(dve.tensor_copy(ms[:, 6, :], next_tp()[:, 0:T * GH]))
            dve.sem_inc(tp_evac, 1)
            link(dve.tensor_tensor(ms[:, 7, :], ms[:, 6, :], ms[:, 4, :], ALU.add))
            dve.sem_inc(m_ready, 1)
            for t in range(T):
                link(dve.tensor_copy(v_aug[:, t, :, 0:HD], z2[:, t, M_V:M_V + GW].rearrange("p (h d) -> p h d", d=HD)))
            link(dve.memset(v_aug[:, :, :, HD:HD + 1], 1.0))
            for h in range(GH):
                n = SC_ML + 2 * h
                dve.wait_ge(sc_mm, n + 1)
                if h >= 2:
                    dve.wait_ge(w_exp, h - 1)
                a = bank[6 + n % 2]
                dve.tensor_tensor(sc2[:, h % 2, 0:2 * P], a[:, 0:2 * P], cst["causal_t"][:, 0:2 * P], ALU.add)
                link(dve.tensor_tensor(sc2[:, h % 2, 2 * P:3 * P], a[:, P:2 * P], cst["causal_t"][:, 2 * P:3 * P], ALU.add))
                dve.sem_inc(sc_evac, 1)
                dve.sem_inc(d_ready, 1)
                dve.wait_ge(sc_mm, n + 2)
                dve.wait_ge(w_exp, h + 1)
                if h >= 2:
                    dve.wait_ge(o_mm, h - 1)
                link(dve.scalar_tensor_tensor(wT2[:, h % 2, :], bank[6 + (n + 1) % 2][:, 0:3 * P], HD ** -0.5,
                                              pr2[:, h % 2, :], ALU.mult, ALU.mult))
                dve.sem_inc(sc_evac, 1)
                dve.sem_inc(w_ready, 1)
            heads4 = lambda a: a.rearrange("p (h d) -> p h d", d=HD)
            wide4 = lambda a: a.unsqueeze(2).broadcast_to([P, GH, HD])

            def head_norm(row, lo, gain_row, gate_lo):
                for t in range(T):
                    o = xn[:, t, lo:lo + GW]
                    link(dve.tensor_tensor(tmp[:, t * GW:(t + 1) * GW], o, o, ALU.mult))
                link(dve.tensor_reduce(ms[:, row, :], tmp[:, 0:T * GW].rearrange("p (h d) -> p h d", d=HD), AX.X, ALU.add))
                rsqrt_mean(ms[:, row, :], ms[:, row, :], HD, RMS_EPS)
                for t in range(T):
                    o = xn[:, t, lo:lo + GW]
                    link(dve.tensor_tensor(heads4(o), heads4(o), wide4(ms[:, row + 1, t * GH:(t + 1) * GH]), ALU.mult))
                    link(dve.tensor_tensor(o, o, gain_row, ALU.mult))
                    link(dve.tensor_tensor(o, o, z2[:, t, gate_lo:gate_lo + GW], ALU.mult))

            dve.wait_ge(o_mm, GH)
            aug = lambda t: bank[2 + t][:, 0:GH * (HD + 1)].rearrange("p (h d) -> p h d", d=HD + 1)
            for t in range(T):
                link(dve.tensor_copy(ms[:, 9, t * GH:(t + 1) * GH].unsqueeze(2), aug(t)[:, :, HD:HD + 1]))
            dve.sem_inc(den_ready, 1)
            dve.wait_ge(m_exp, 2)
            link(dve.tensor_tensor(ms[:, 10, :], ms[:, 10, :], ms[:, 8, :], ALU.max))
            link(dve.reciprocal(ms[:, 10, :], ms[:, 10, :]))
            for t in range(T):
                link(dve.tensor_tensor(heads4(xn[:, t, 0:GW]), aug(t)[:, :, 0:HD], wide4(ms[:, 10, t * GH:(t + 1) * GH]),
                                       ALU.mult))
            dve.sem_inc(o_used, 1)
            dve.wait_ge(z2_act, 1)
            link(dve.tensor_scalar(z2[:, :, A_Q:A_Q + GW], z2[:, :, A_Q:A_Q + GW], HD ** -0.5, None, ALU.mult))
            dve.sem_inc(qk_ready, 1)
            def hgrn_gates():
                lb = rows2[:, 2, :]
                link(dve.tensor_tensor(lb, lb, lb, ALU.subtract))
                dve.sem_inc(f_ready, 1)
                dve.wait_ge(hg_act, 2)
                link(dve.reciprocal(tmp[:, 0:GW], lb))
                link(dve.tensor_tensor(tmp[:, 0:GW], tmp[:, 0:GW], lb, ALU.mult))
                link(dve.tensor_tensor(lb, tmp[:, 0:GW], tmp[:, 0:GW], ALU.subtract))
                link(dve.tensor_scalar(tmp[:, 0:GW], lb, -1.0, 1.0, ALU.mult, ALU.add))
                both = lambda a: a.unsqueeze(1).broadcast_to([P, T, GW])
                f = hg[:, LF, :, :]
                link(dve.tensor_tensor(f, f, both(tmp[:, 0:GW]), ALU.mult))
                link(dve.tensor_tensor(f, f, both(lb), ALU.add))
                link(dve.tensor_scalar(hg[:, HK, :, :], f, -1.0, 1.0, ALU.mult, ALU.add))
                link(dve.tensor_scalar(f, f, TINY, None, ALU.max))
                dve.sem_inc(f_ready, 1)
                link(dve.tensor_tensor(hg[:, QK, :, :], hg[:, HQ, :, :], hg[:, HK, :, :], ALU.subtract))

            def short_conv(t):
                dve.wait_ge(conv_shift, 64)
                taps = [conv[:, i, t, :] for i in range(3)]
                for i in range(3):
                    link(dve.tensor_tensor(taps[i], taps[i], rows2[:, 5 - i, :], ALU.mult))
                link(dve.tensor_tensor(taps[1], taps[1], taps[2], ALU.add))
                link(dve.tensor_tensor(taps[0], taps[0], taps[1], ALU.add))
                link(dve.tensor_tensor(xn[:, t, GW:2 * GW], taps[0], z2[:, t, C_B:C_B + GW], ALU.mult))

            pair_copy(qT2)
            pair_copy(kT2)

            def moba_copy(h):
                b = next_tp()
                if h >= 2:
                    dve.wait_ge(o_mm, GH + h - 1)
                dve.tensor_copy(wT2[:, h % 2, :], b[:, 0:3 * P]).then_inc(tp_evac, 1)

            for h in range(GH):
                n = SC_MOBA + h
                dve.wait_ge(sc_mm, n + 1)
                if h >= 2:
                    dve.wait_ge(w_exp, GH + h - 1)
                link(dve.tensor_copy(sc2[:, h % 2, :], bank[6 + n % 2][:, 0:3 * P]))
                dve.sem_inc(sc_evac, 1)
                dve.tensor_reduce(ms[:, 13, 2 * h:2 * h + 1], sc2[:, h % 2, 0:P], AX.X, ALU.max, negate=True)
                dve.tensor_reduce(ms[:, 13, 2 * h + 1:2 * h + 2], sc2[:, h % 2, P:3 * P], AX.X, ALU.max, negate=True)\
                    .then_inc(d_ready, 1)
                if h:
                    moba_copy(h - 1)
                if h == 0:
                    hgrn_gates()
                elif h == 1:
                    head_norm(11, 0, rows2[:, 0, :], M_O)
                else:
                    short_conv(h - 2)
            moba_copy(GH - 1)
            dve.wait_ge(w_exp, 2 * GH)
            link(dve.reciprocal(ms[:, 15, :], ms[:, 14, :]))
            dve.wait_ge(o_mm, 2 * GH)
            inv2 = ms[:, 15, :].rearrange("p (h t) -> p t h", t=T)
            for t in range(T):
                link(dve.tensor_tensor(heads4(xn[:, t, 2 * GW:3 * GW]), heads4(bank[2 + t][:, 0:GW]),
                                       wide4(inv2[:, t, :]), ALU.mult))
            dve.sem_inc(o_used, 1)
            dve.wait_ge(hg_act, 3)
            fs2 = hg[:, HS, :, :]
            for level in range(LEVELS + 1):
                n = SC_HG + 3 * level
                if level:
                    dve.wait_ge(tp_mm, TP_HG + level)
                if level < LEVELS:
                    link(dve.scalar_tensor_tensor(fs2, hg[:, QK, :, :], cst["upper"][:, level:level + 1],
                                                  hg[:, HK, :, :], ALU.mult, ALU.add))
                    src = fs2
                dve.wait_ge(hg_exp, level + 1)
                e2 = ex2[:, level % 2, :].rearrange("p (t d) -> p t d", t=T)
                if level < LEVELS:
                    link(dve.tensor_tensor(fs2, fs2, e2, ALU.mult))
                else:
                    link(dve.tensor_tensor(fs2[:, 0, :], hg[:, HK, 0, :], e2[:, 0, :], ALU.mult))
                    link(dve.tensor_tensor(fs2[:, 1, :], hg[:, HQ, 1, :], e2[:, 1, :], ALU.mult))
                dve.sem_inc(sc_evac, 1)
                dve.sem_inc(ft_src, 1)
                if level:
                    dve.wait_ge(sc_mm, n)
                pair_copy(fT)
                for parity in range(2):
                    dve.wait_ge(sc_mm, n + 2 + parity)
                    b = bank[6 + (n + 1 + parity) % 2]
                    a = at[:, parity, :, :]
                    if level < LEVELS:
                        mask = cst["level_t"][:, level * P:(level + 1) * P].unsqueeze(1).broadcast_to([P, 4, P])
                        dst = a if level == 0 else tmp[:, 0:BANK].rearrange("p (i c) -> p i c", i=4)
                        link(dve.tensor_tensor(dst, four(b), mask, ALU.mult))
                        if level:
                            link(dve.tensor_tensor(a, a, dst, ALU.add))
                    else:
                        link(dve.tensor_copy(atx[:, parity, :, :], b[:, 0:2 * P].rearrange("p (i c) -> p i c", i=2)))
                    dve.sem_inc(sc_evac, 1)
            link(dve.tensor_tensor(hg[:, QK, :, :], hg[:, HQ, :, :], hg[:, HK, :, :], ALU.mult))
            link(dve.tensor_reduce(ms[:, 18, :], hg[:, QK, :, :].rearrange("p t (h d) -> p (t h) d", d=HD), AX.X, ALU.add))
            dve.wait_ge(o_mm, 2 * GH + 1)
            for t in range(T):
                o = xn[:, t, 3 * GW:4 * GW]
                link(dve.tensor_tensor(heads4(o), heads4(z2[:, t, H_I:H_I + GW]), wide4(ms[:, 18, t * GH:(t + 1) * GH]),
                                       ALU.mult))
                link(dve.tensor_tensor(o, o, bank[2 + t][:, 0:GW], ALU.add))
            head_norm(16, 3 * GW, rows2[:, 1, :], H_G)
            dve.sem_inc(y_ready, 1)
            untranspose()
            dve.wait_ge(lin_evac, after(J_MIX + 1, 1))
            add_normed(hbuf, MIX_POST)
            dve.sem_inc(h_used, 1)
            norm_into(xn, x, CROSS_PRE, ready=xn_ready)
            untranspose()

            def cross_copy(h):
                b = next_tp()
                if h >= 2:
                    dve.wait_ge(o_mm, 2 * GH + h)
                dve.tensor_copy(prxT[:, h % 2, :], b[:, :]).then_inc(tp_evac, 1)

            for h in range(CH):
                n = SC_X + h
                dve.wait_ge(sc_mm, n + 1)
                if h >= 2:
                    dve.wait_ge(w_exp, 2 * GH + h - 1)
                link(dve.tensor_copy(scx[:, h % 2, :, :], bank[6 + n % 2][:, :].rearrange("p (t m) -> p t m", t=T)))
                dve.sem_inc(sc_evac, 1)
                c = slice(T * h, T * h + T)
                link(dve.tensor_reduce(cs[:, 2, c], scx[:, h % 2, :, :], AX.X, ALU.max, negate=True))
                dve.tensor_scalar(cs[:, 0, c], cs[:, 2, c], CHD ** -0.5, None, ALU.mult).then_inc(d_ready, 1)
                if h:
                    cross_copy(h - 1)
            cross_copy(CH - 1)
            dve.wait_ge(w_exp, 2 * GH + CH)
            link(dve.reciprocal(cs[:, 3, :], cs[:, 1, :]))
            dve.wait_ge(o_mm, 2 * GH + 1 + CH)
            invx = cs[:, 3, :].rearrange("p (h t) -> p t h", t=T)
            for t in range(T):
                link(dve.tensor_tensor(xn[:, t, 0:CW].rearrange("p (h d) -> p h d", d=CHD),
                                       bank[2 + t][:, :].rearrange("p (h d) -> p h d", d=CHD),
                                       invx[:, t, :].unsqueeze(2).broadcast_to([P, CH, CHD]), ALU.mult))
            dve.sem_inc(y_ready, 1)
            untranspose(CW // P)
            dve.wait_ge(lin_evac, after(J_CO, 3))
            add_normed(hbuf, CROSS_POST)
            dve.sem_inc(h_used, 1)
            norm_into(xn, x, FFN_PRE, ready=xn_ready)
            for i in range(2):
                link(dve.memset(gateT[:, i, :, 0:2], 0.0))
            dve.sem_inc(h_used, 1)
            untranspose()

            def ffn_act(i):
                dve.wait_ge(silu_ready, i + 1)
                dve.wait_ge(up_mm, i + 1)
                dve.tensor_tensor(actT[:, 2 * i:2 * i + 2, :], siluT[:, i % 2, :, :],
                                  bank[6 + i % 2][:, :].rearrange("p (i c) -> p i c", i=2), ALU.mult)\
                    .then_inc(act_ready, 1)

            def split_low(u):
                for q in range(PIECES):
                    dve.wait_ge(high_made, u * PIECES + q + 1)
                    at_piece = lambda a: of_unit(a, u, q * PIECE, PIECE)
                    dve.tensor_tensor(at_piece(w_low), at_piece(ring), at_piece(w_high).bitcast(F32), ALU.subtract)\
                        .then_inc(low_made, 1)

            def act_split_low(i):
                dve.wait_ge(act_high_made, i + 1)
                c = slice(2 * i, 2 * i + 2)
                dve.tensor_tensor(act_low[:, c, :], actT[:, c, :], act_high[:, c, :].bitcast(F32), ALU.subtract)\
                    .then_inc(act_low_made, 1)

            split_low(0)
            dve.wait_ge(x_high_made, 2)
            dve.tensor_tensor(xT_low[:, :, :], xT[:, :, :], xT_high.bitcast(F32), ALU.subtract).then_inc(x_low_made, 1)
            split_low(1)
            for i in range(FF_JOBS):
                dve.wait_ge(lin_evac, after(J_FFN + i))
                if i >= 2:
                    dve.wait_ge(silu_ready, i - 1)
                for half in range(2):
                    c, tile = convT[:, i % 2, half, :], 2 * i + half
                    g = lambda shift: gateT[:, i % 2, half, 2 - shift:2 - shift + T * P]
                    link(dve.tensor_scalar(c, g(0), conv_w[:, 2, tile:tile + 1], conv_b[:, tile:tile + 1],
                                           ALU.mult, ALU.add))
                    link(dve.scalar_tensor_tensor(c, g(1), conv_w[:, 1, tile:tile + 1], c, ALU.mult, ALU.add))
                    link(dve.scalar_tensor_tensor(c, g(2), conv_w[:, 0, tile:tile + 1], c, ALU.mult, ALU.add))
                dve.sem_inc(conv_done, 1)
                split_low(2 * i + 2)
                if i:
                    ffn_act(i - 1)
                if i >= 2:
                    act_split_low(i - 2)
                split_low(2 * i + 3)
            ffn_act(FF_JOBS - 1)
            act_split_low(FF_JOBS - 2)
            act_split_low(FF_JOBS - 1)
            for u in range(2 * FF_JOBS + 2, len(units)):
                split_low(u)
            dve.wait_ge(x2_ready, 3)
            add_normed(hbuf_f, FFN_POST)
            dve.sem_inc(out_ready, 1)

    return nc


def kernel(**inputs):
    import concourse.bacc as bacc
    from concourse.bass_utils import run_bass_kernel_spmd as run

    nc = bacc.Bacc("TRN2", target_bir_lowering=False, num_devices=1)
    arrays, A = {}, {}
    for name in INPUTS:
        a = np.asarray(inputs[name])
        if name not in UNLAYERED:
            a = a[0]
        if name in FLAT:
            a = a.reshape(-1)
        if name == "ffn_conv_w_2":
            a = a.reshape(3, FT_TILES, P).transpose(2, 0, 1)
        if name == "ffn_conv_b_2":
            a = a.reshape(FT_TILES, P).T
        if name == "c":
            a = a.reshape(KT, P).T
        a = np.ascontiguousarray(a)
        arrays["in_" + name] = a
        A[name] = nc.dram_tensor("in_" + name, a.shape, mybir.dt.from_np(a.dtype), kind="ExternalInput").ap()
    consts = {}
    for name, a in shape_constants().items():
        arrays["const_" + name] = a
        consts[name] = nc.dram_tensor("const_" + name, a.shape, F32, kind="ExternalInput").ap()
    out = nc.dram_tensor("out_0_dram", (T * P, D), F32, kind="ExternalOutput").ap()
    build(nc, A, consts, out)
    r = run(nc, [arrays], core_ids=[0])
    return r.results[0]["out_0_dram"].reshape(1, T * P, D)
```
